# Optimizing a Trainium2 kernel written in Bass

```python
import jax, jax.numpy as jnp
from jax import lax
import numpy as np

D_MODEL = 2048
BATCH = 1
SEQ = 512
DEPTH = 1
DEC_BATCH = 1
DEC_SEQ = 32
PAST_LEN = 512

CHUNK = 64
D_MIX = D_MODEL
POOL_WIDTH = D_MIX // 2
POOL_WINDOWS = (2, 4, 8, 16)
POOL_GROUP = POOL_WIDTH // len(POOL_WINDOWS)
POOL_HIST = max(POOL_WINDOWS) - 1
DN_WIDTH = D_MIX - POOL_WIDTH
DN_HEAD_DIM = 128
DN_HEADS = DN_WIDTH // DN_HEAD_DIM
CONV_WIDTH = 4
CONV_HIST = CONV_WIDTH - 1
IN_PROJ = POOL_WIDTH + 3 * DN_WIDTH + 2 * DN_HEADS + DN_WIDTH
N_MEM = 256
MEM_HEADS = 4
MEM_HEAD_DIM = D_MODEL // MEM_HEADS
PEER_HEADS = 8
N_KEYS = 128
N_EXPERTS = N_KEYS * N_KEYS
PEER_QUERY = 256
PEER_HALF = PEER_QUERY // 2
PEER_TOPK = 16
PEER_BLOCK = 128
EPS = 1e-6

kernel_name = "streaming_pool_deltanet_peer_step"

def _rmsnorm(x, g):
    xf = x.astype(jnp.float32)
    y = xf * lax.rsqrt(jnp.mean(xf * xf, axis=-1, keepdims=True) + EPS)
    return (y * g.astype(jnp.float32)).astype(x.dtype)

def _l2norm(x):
    xf = x.astype(jnp.float32)
    return xf * lax.rsqrt(jnp.sum(xf * xf, axis=-1, keepdims=True) + EPS)

def _pool_mixer(u, hist, w_pool, pool_scale, start):
    L = u.shape[1]
    u_ext = jnp.concatenate([hist.astype(u.dtype), u], axis=1)
    cs = jnp.pad(jnp.cumsum(u_ext.astype(jnp.float32), axis=1), ((0, 0), (1, 0), (0, 0)))
    end = cs[:, POOL_HIST + 1:POOL_HIST + 1 + L]
    pos = start + jnp.arange(L, dtype=jnp.int32)
    outs = []
    for gi, w in enumerate(POOL_WINDOWS):
        sl = slice(gi * POOL_GROUP, (gi + 1) * POOL_GROUP)
        wsum = end[..., sl] - cs[:, POOL_HIST + 1 - w:POOL_HIST + 1 - w + L, sl]
        count = jnp.minimum(pos + 1, w).astype(jnp.float32)
        mix = wsum / count[None, :, None] - u[..., sl].astype(jnp.float32)
        outs.append(jnp.einsum('blc,cd->bld', mix.astype(u.dtype), w_pool[gi]))
    out = jnp.concatenate(outs, axis=-1) * pool_scale
    return out, u_ext[:, -POOL_HIST:]

def _short_conv(hist, xin, w):
    L = xin.shape[1]
    ext = jnp.concatenate([hist.astype(xin.dtype), xin], axis=1)
    out = ext[:, 0:L] * w[0]
    for i in range(1, CONV_WIDTH):
        out = out + ext[:, i:i + L] * w[i]
    return jax.nn.silu(out), ext[:, -CONV_HIST:]

def _gated_delta_chunked(q, k, v, g, beta, S0):
    B, L, H, d = q.shape
    n = L // CHUNK

    def to_chunks(t):
        t = t.reshape((B, n, CHUNK, H) + t.shape[3:])
        return jnp.moveaxis(t, 3, 1)

    q, k, v, g, beta = (to_chunks(t) for t in (q, k, v, g, beta))
    gam = jnp.cumsum(g, axis=-1)
    tril = jnp.tril(jnp.ones((CHUNK, CHUNK), bool))
    strict = jnp.tril(jnp.ones((CHUNK, CHUNK), bool), -1)
    decay = jnp.exp(jnp.where(tril, gam[..., :, None] - gam[..., None, :], -jnp.inf))
    kb = k * beta[..., None]
    A = jnp.where(strict, jnp.einsum('bhntd,bhnsd->bhnts', kb, k) * decay, 0.0)
    lhs = A + jnp.eye(CHUNK, dtype=A.dtype)
    rhs = jnp.concatenate([v * beta[..., None], kb * jnp.exp(gam)[..., None]], axis=-1)
    sol = lax.linalg.triangular_solve(lhs, rhs, left_side=True, lower=True)
    u_val, w_k = sol[..., :d], sol[..., d:]
    att = jnp.einsum('bhntd,bhnsd->bhnts', q, k) * decay
    q_dec = q * jnp.exp(gam)[..., None]
    k_dec = k * jnp.exp(gam[..., -1:] - gam)[..., None]
    g_last = jnp.exp(gam[..., -1])
    xs = tuple(jnp.moveaxis(t, 2, 0) for t in (u_val, w_k, att, q_dec, k_dec, g_last))

    def step(S, inp):
        uc, wc, ac, qc, kc, gc = inp
        v_new = uc - jnp.einsum('bhtk,bhkv->bhtv', wc, S)
        o = jnp.einsum('bhtk,bhkv->bhtv', qc, S) + jnp.einsum('bhts,bhsv->bhtv', ac, v_new)
        S = S * gc[..., None, None] + jnp.einsum('bhtk,bhtv->bhkv', kc, v_new)
        return S, o

    S, o = lax.scan(step, S0, xs)
    o = jnp.moveaxis(o, 0, 2).reshape(B, H, L, d)
    return jnp.moveaxis(o, 1, 2), S

def _deltanet_mixer(qkv, a, b, z, conv_hist, S0, conv_w, a_log, dt_bias, norm_dn):
    B, L, _ = qkv.shape
    c, new_conv = _short_conv(conv_hist, qkv, conv_w)
    q, k, v = jnp.split(c, 3, axis=-1)
    shp = (B, L, DN_HEADS, DN_HEAD_DIM)
    q = _l2norm(q.reshape(shp)) * (DN_HEAD_DIM ** -0.5)
    k = _l2norm(k.reshape(shp))
    v = v.reshape(shp).astype(jnp.float32)
    beta = jax.nn.sigmoid(b.astype(jnp.float32))
    g = -jnp.exp(a_log.astype(jnp.float32)) * jax.nn.softplus(a.astype(jnp.float32) + dt_bias.astype(jnp.float32))
    pad = (-L) % CHUNK
    if pad:
        p4 = ((0, 0), (0, pad), (0, 0), (0, 0))
        p3 = ((0, 0), (0, pad), (0, 0))
        q, k, v = jnp.pad(q, p4), jnp.pad(k, p4), jnp.pad(v, p4)
        g, beta = jnp.pad(g, p3), jnp.pad(beta, p3)
    o, S = _gated_delta_chunked(q, k, v, g, beta, S0.astype(jnp.float32))
    o = o[:, :L]
    o = _rmsnorm(o, norm_dn) * jax.nn.silu(z.reshape(shp).astype(jnp.float32))
    return o.reshape(B, L, DN_WIDTH).astype(qkv.dtype), new_conv, S.astype(S0.dtype)

def _mem_kv(mem, norm_mem, w_mk, w_mv):
    B, M, _ = mem.shape
    m = _rmsnorm(mem, norm_mem)
    k = jnp.einsum('bmd,de->bme', m, w_mk).reshape(B, M, MEM_HEADS, MEM_HEAD_DIM)
    v = jnp.einsum('bmd,de->bme', m, w_mv).reshape(B, M, MEM_HEADS, MEM_HEAD_DIM)
    return k, v

def _mem_attend(h, mk, mv, w_mq, w_mo):
    B, L, _ = h.shape
    q = jnp.einsum('bld,de->ble', h, w_mq).reshape(B, L, MEM_HEADS, MEM_HEAD_DIM)
    s = jnp.einsum('blhd,bmhd->bhlm', q, mk).astype(jnp.float32) * (MEM_HEAD_DIM ** -0.5)
    p = jax.nn.softmax(s, axis=-1).astype(mv.dtype)
    o = jnp.einsum('bhlm,bmhd->blhd', p, mv).reshape(B, L, D_MODEL)
    return jnp.einsum('bld,de->ble', o, w_mo)

def _peer(h, w_pq, sub_keys, u_experts, v_experts):
    B, L, D = h.shape
    t = h.reshape(-1, D)
    T = t.shape[0]
    pad = (-T) % PEER_BLOCK
    t = jnp.pad(t, ((0, pad), (0, 0))).reshape(-1, PEER_BLOCK, D)

    def block(xb):
        qh = jnp.einsum('td,de->te', xb, w_pq).reshape(PEER_BLOCK, PEER_HEADS, 2, PEER_HALF)
        s = jnp.einsum('thcd,hckd->thck', qh, sub_keys).astype(jnp.float32)
        sv, si = lax.top_k(s, PEER_TOPK)
        cand = (sv[:, :, 0, :, None] + sv[:, :, 1, None, :]).reshape(PEER_BLOCK, PEER_HEADS, -1)
        cid = (si[:, :, 0, :, None] * N_KEYS + si[:, :, 1, None, :]).reshape(PEER_BLOCK, PEER_HEADS, -1)
        top_s, top_pos = lax.top_k(cand, PEER_TOPK)
        eid = jnp.take_along_axis(cid, top_pos, axis=-1)
        gate = jax.nn.softmax(top_s, axis=-1)
        ue = u_experts[eid]
        act = jax.nn.gelu(jnp.einsum('thkd,td->thk', ue, xb).astype(jnp.float32), approximate=False)
        coef = (gate * act).astype(xb.dtype)
        ve = v_experts[eid]
        return jnp.einsum('thk,thkd->td', coef, ve)

    out = lax.map(block, t).reshape(-1, D)[:T]
    return out.reshape(B, L, D)

def _layer(x, pool_hist, conv_hist, S0, mem_k, mem_v, start, lw):
    (norm_mix, w_in, w_pool, pool_scale, conv_w, a_log, dt_bias, norm_dn, w_out,
     norm_xattn, w_mq, w_mo, norm_ffn, w_pq, sub_keys, u_experts, v_experts) = lw
    h = _rmsnorm(x, norm_mix)
    proj = jnp.einsum('bld,de->ble', h, w_in)
    off = POOL_WIDTH + 3 * DN_WIDTH
    u_pool = proj[..., :POOL_WIDTH]
    qkv = proj[..., POOL_WIDTH:off]
    a = proj[..., off:off + DN_HEADS]
    b = proj[..., off + DN_HEADS:off + 2 * DN_HEADS]
    z = proj[..., off + 2 * DN_HEADS:]
    pool_out, new_pool = _pool_mixer(u_pool, pool_hist, w_pool, pool_scale, start)
    dn_out, new_conv, new_S = _deltanet_mixer(qkv, a, b, z, conv_hist, S0, conv_w, a_log, dt_bias, norm_dn)
    x = x + jnp.einsum('ble,ed->bld', jnp.concatenate([pool_out, dn_out], axis=-1), w_out)
    x = x + _mem_attend(_rmsnorm(x, norm_xattn), mem_k, mem_v, w_mq, w_mo)
    x = x + _peer(_rmsnorm(x, norm_ffn), w_pq, sub_keys, u_experts, v_experts)
    return x, new_pool, new_conv, new_S

def setup_inputs(seed: int = 0) -> dict:
    key = jax.random.key(seed)
    ks = jax.random.split(key, 32)
    f32 = jnp.float32

    def nrm(k, shape, scale):
        return jax.random.normal(k, shape, f32) * scale

    def gain(k, shape):
        return 1.0 + 0.02 * jax.random.normal(k, shape, f32)

    dt = jnp.exp(jax.random.uniform(ks[20], (DEPTH, DN_HEADS), f32, np.log(1e-3), np.log(1e-1)))
    return {
        "x_prompt": nrm(ks[0], (BATCH, SEQ, D_MODEL), 1.0),
        "mem_prompt": nrm(ks[1], (BATCH, N_MEM, D_MODEL), 1.0),
        "x_sample": nrm(ks[2], (DEC_BATCH, DEC_SEQ, D_MODEL), 1.0),
        "cache_pool": nrm(ks[3], (DEPTH, DEC_BATCH, POOL_HIST, POOL_WIDTH), 1.0),
        "cache_conv": nrm(ks[4], (DEPTH, DEC_BATCH, CONV_HIST, 3 * DN_WIDTH), 1.0),
        "state_dn": nrm(ks[5], (DEPTH, DEC_BATCH, DN_HEADS, DN_HEAD_DIM, DN_HEAD_DIM), 0.1),
        "cache_mem_k": nrm(ks[6], (DEPTH, DEC_BATCH, N_MEM, MEM_HEADS, MEM_HEAD_DIM), 1.0),
        "cache_mem_v": nrm(ks[7], (DEPTH, DEC_BATCH, N_MEM, MEM_HEADS, MEM_HEAD_DIM), 1.0),
        "norm_mix": gain(ks[8], (DEPTH, D_MODEL)),
        "w_in": nrm(ks[9], (DEPTH, D_MODEL, IN_PROJ), D_MODEL ** -0.5),
        "w_pool": nrm(ks[10], (DEPTH, len(POOL_WINDOWS), POOL_GROUP, POOL_GROUP), POOL_GROUP ** -0.5),
        "pool_scale": gain(ks[11], (DEPTH, POOL_WIDTH)),
        "conv_w": nrm(ks[12], (DEPTH, CONV_WIDTH, 3 * DN_WIDTH), CONV_WIDTH ** -0.5),
        "a_log": jnp.log(jax.random.uniform(ks[13], (DEPTH, DN_HEADS), f32, 1.0, 16.0)),
        "dt_bias": dt + jnp.log(-jnp.expm1(-dt)),
        "norm_dn": gain(ks[14], (DEPTH, DN_HEAD_DIM)),
        "w_out": nrm(ks[15], (DEPTH, D_MIX, D_MODEL), D_MIX ** -0.5),
        "norm_xattn": gain(ks[16], (DEPTH, D_MODEL)),
        "norm_mem": gain(ks[17], (DEPTH, D_MODEL)),
        "w_mq": nrm(ks[18], (DEPTH, D_MODEL, D_MODEL), D_MODEL ** -0.5),
        "w_mk": nrm(ks[19], (DEPTH, D_MODEL, D_MODEL), D_MODEL ** -0.5),
        "w_mv": nrm(ks[21], (DEPTH, D_MODEL, D_MODEL), D_MODEL ** -0.5),
        "w_mo": nrm(ks[22], (DEPTH, D_MODEL, D_MODEL), D_MODEL ** -0.5),
        "norm_ffn": gain(ks[23], (DEPTH, D_MODEL)),
        "w_pq": nrm(ks[24], (DEPTH, D_MODEL, PEER_HEADS * PEER_QUERY), D_MODEL ** -0.5),
        "sub_keys": nrm(ks[25], (DEPTH, PEER_HEADS, 2, N_KEYS, PEER_HALF), PEER_HALF ** -0.5),
        "u_experts": nrm(ks[26], (DEPTH, N_EXPERTS, D_MODEL), D_MODEL ** -0.5),
        "v_experts": nrm(ks[27], (DEPTH, N_EXPERTS, D_MODEL), PEER_HEADS ** -0.5),
        "norm_final": gain(ks[28], (D_MODEL,)),
    }

def reference(x_prompt, mem_prompt, x_sample, cache_pool, cache_conv, state_dn, cache_mem_k, cache_mem_v,
              norm_mix, w_in, w_pool, pool_scale, conv_w, a_log, dt_bias, norm_dn, w_out,
              norm_xattn, norm_mem, w_mq, w_mk, w_mv, w_mo,
              norm_ffn, w_pq, sub_keys, u_experts, v_experts, norm_final):
    xp, xs = x_prompt, x_sample
    Bp = x_prompt.shape[0]
    pool_p, conv_p, dn_p, mk_p, mv_p = [], [], [], [], []
    pool_s, conv_s, dn_s = [], [], []
    for l in range(DEPTH):
        lw = (norm_mix[l], w_in[l], w_pool[l], pool_scale[l], conv_w[l], a_log[l], dt_bias[l], norm_dn[l],
              w_out[l], norm_xattn[l], w_mq[l], w_mo[l], norm_ffn[l], w_pq[l], sub_keys[l],
              u_experts[l], v_experts[l])
        mk, mv = _mem_kv(mem_prompt, norm_mem[l], w_mk[l], w_mv[l])
        zp = jnp.zeros((Bp, POOL_HIST, POOL_WIDTH), xp.dtype)
        zc = jnp.zeros((Bp, CONV_HIST, 3 * DN_WIDTH), xp.dtype)
        zs = jnp.zeros((Bp, DN_HEADS, DN_HEAD_DIM, DN_HEAD_DIM), xp.dtype)
        xp, np_, nc_, ns_ = _layer(xp, zp, zc, zs, mk, mv, 0, lw)
        pool_p.append(np_); conv_p.append(nc_); dn_p.append(ns_); mk_p.append(mk); mv_p.append(mv)
        xs, np2, nc2, ns2 = _layer(xs, cache_pool[l], cache_conv[l], state_dn[l],
                                   cache_mem_k[l], cache_mem_v[l], PAST_LEN, lw)
        pool_s.append(np2); conv_s.append(nc2); dn_s.append(ns2)
    y_prompt = _rmsnorm(xp, norm_final)
    y_sample = _rmsnorm(xs, norm_final)
    return (y_prompt, y_sample,
            jnp.stack(pool_p), jnp.stack(conv_p), jnp.stack(dn_p), jnp.stack(mk_p), jnp.stack(mv_p),
            jnp.stack(pool_s), jnp.stack(conv_s), jnp.stack(dn_s))


_drawn_inputs = setup_inputs


def setup_inputs(seed=0):
    import zlib

    import numpy as np

    out = dict(_drawn_inputs(seed))
    spreads = {}
    factors = {'pool_scale': 3.142,
     'norm_dn': 3.977,
     'norm_xattn': 8.0,
     'norm_mem': 2.838,
     'norm_final': 7.468,
     'norm_ffn': 6.23}
    for name, (base, spread) in spreads.items():
        noise = np.random.default_rng([zlib.crc32(name.encode()), seed]).standard_normal(out[name].shape)
        drawn = base * np.exp(spread * noise) if base else spread * noise
        out[name] = __import__('jax').numpy.asarray(drawn.astype(out[name].dtype))
    for name, factor in factors.items():
        out[name] = (out[name] * factor).astype(out[name].dtype)
    return out
```

```python
from contextlib import ExitStack

import numpy as np

import concourse.bass as bass
from concourse import mybir

F32 = mybir.dt.float32
F32R = mybir.dt.float32r
U32 = mybir.dt.uint32
ALU = mybir.AluOpType
ACT = mybir.ActivationFunctionType
AX_X = mybir.AxisListType.X

P = 128
D = 2048
KT = D // P
TP, TS = 512, 32
T = TP + TS
HALF = T // 2
NCH = 5
TPAD = NCH * P
M = 256
EPS = 1e-6
HEADS = 8
LEVELS = 7
MH, MHT = 4, 4
MEM_SCALE = float(MHT * P) ** -0.5
SLOTS = 128
TOPK = 16
GRP = 4
NGRP = P // GRP
LOWEST = -3.0e38

MK0 = 0
MV0 = MK0 + KT
Z0 = MV0 + KT
POOL0 = Z0 + 8
QKV0 = POOL0 + 8
AB0 = QKV0 + 24
OUT0 = AB0 + 1
MQ0 = OUT0 + KT
MO0 = MQ0 + KT
PQ0 = MO0 + KT
EXP0 = PQ0 + KT
UNITS = EXP0 + 2 * P

V_MIX, V_XATTN, V_MEM, V_FFN, V_FINAL = (16 * i for i in range(5))
V_POOL = 80
V_CONV = V_POOL + 8
V_DN = V_CONV + 96
V_EPS = V_DN + 1
V_ALOG = V_EPS + 1
V_DT = V_ALOG + 8
NV = V_DT + 8

C_ID = 0
C_ONE = C_ID + P
C_CUM = C_ONE + P
C_LEV = C_CUM + P
C_IOTA = C_LEV + LEVELS * P
C_CNT = C_IOTA + P
C_VALID = C_CNT + 64
NC = C_VALID + NCH * HEADS


def constants():
    c = np.zeros((P, NC), np.float32)
    r = np.arange(P)
    c[:, C_ID:C_ID + P] = np.eye(P)
    c[:, C_ONE:C_ONE + P] = 1.0
    c[:, C_CUM:C_CUM + P] = r[:, None] <= r[None, :]
    for l in range(LEVELS):
        s = 1 << l
        same = (r[:, None] // (2 * s)) == (r[None, :] // (2 * s))
        c[:, C_LEV + l * P:C_LEV + (l + 1) * P] = same & ((r[:, None] // s) % 2 == 1) & ((r[None, :] // s) % 2 == 0)
    c[:, C_IOTA:C_IOTA + P] = r[None, :]
    for g in range(4):
        c[:, C_CNT + 16 * g:C_CNT + 16 * g + 16] = 1.0 / np.minimum(np.arange(16) + 1, 2 << g)
    v = np.ones((P, NCH, HEADS), np.float32)
    v[TS:, NCH - 1] = 0.0
    c[:, C_VALID:NC] = v.reshape(P, -1)
    return c


class Chain:

    def __init__(self, eng, sem):
        self.eng, self.sem, self.base, self.n = eng, sem, 0, 0

    def link(self, ins):
        ins.then_inc(self.sem, 1)
        self.n += 1
        self.eng.wait_ge(self.sem, self.base + self.n)

    def enter(self, i, per):
        self.start, self.per = self.base + self.n, per
        self.base, self.n = self.start + i * per, 0

    def leave(self, count):
        assert self.n == self.per, (self.n, self.per)
        self.base, self.n = self.start + count * self.per, 0


def build(nc, a):
    es = ExitStack()

    def sem(name):
        return es.enter_context(nc.semaphore(name))

    start = -(-nc.sbuf_base // 64) * 64

    def region(offset, size):
        at = [offset]

        def place(name, free, dtype=F32):
            t = nc.alloc_sbuf_tensor_at(name, [P] + list(free), dtype, offset=at[0])
            at[0] += 4 * int(np.prod(free))
            at[0] = -(-at[0] // 32) * 32
            assert at[0] <= offset + size, (name, at[0] - offset - size)
            return t
        return place

    XR = start
    HR = XR + 4 * KT * T
    RR = HR + 8 * KT * T
    CR = RR + 6 * 4 * KT * P
    WR = -(-(CR + 4 * (NC + NV + 2 * NCH * HEADS) + 128) // 64) * 64
    W_SIZE = nc.sbuf_usable_end - WR
    H_SIZE = 8 * KT * T

    place = region(RR, CR - RR)
    raw = place("raw", [2, KT, P])
    whi = place("whi", [2, KT, P], F32R)
    wlo = place("wlo", [2, KT, P], F32R)
    place = region(CR, WR - CR)
    consts = place("consts", [NC])
    vecs = place("vecs", [NV])
    gcol = place("gcol", [NCH * HEADS])
    beta = place("beta", [NCH * HEADS])
    place = region(XR, HR - XR)
    x = place("x", [KT, T])
    place = region(XR, HR - XR)
    cat = place("cat", [KT, T])
    place = region(XR, HR - XR)
    mem = place("mem", [KT, M])
    place = region(HR, H_SIZE)
    xhi = place("xhi", [KT, T], F32R)
    xlo = place("xlo", [KT, T], F32R)
    place = region(HR, H_SIZE)
    memhi = place("memhi", [KT, M], F32R)
    memlo = place("memlo", [KT, M], F32R)

    pu = es.enter_context(nc.psum_tensor("pu", [P, 2, 2, 512], F32))
    pm = es.enter_context(nc.psum_tensor("pm", [P, 2, 2, 512], F32))
    SLOT = [t[:, s].rearrange("p b n -> p (b n)") for t in (pu, pm) for s in (0, 1)]

    ident = consts[:, C_ID:C_ID + P]
    ones = consts[:, C_ONE:C_ONE + P]
    cum = consts[:, C_CUM:C_CUM + P]

    qkv_s = nc.dram_tensor("qkv_s", (24, P, TPAD), F32, kind="Internal").ap()
    q_s = nc.dram_tensor("q_s", (KT, P, TPAD), F32, kind="Internal").ap()
    gate_s = nc.dram_tensor("gate_s", (NGRP, P, T * GRP), F32, kind="Internal").ap()

    raw_loaded = [sem("raw_loaded0"), sem("raw_loaded1")]
    hi_ready = sem("hi_ready")
    lo_ready = sem("lo_ready")
    tiles_done = sem("tiles_done")
    psum_free = sem("psum_free")

    def taken(eng, tile):
        eng.wait_ge(psum_free, tile + 3)

    def unit(base, i, s):
        return base + s + 2 * i, (base + s) % 2, i + (base + s) // 2 + 1

    def load_unit(sp, u, slot):
        sp.wait_ge(lo_ready, u - 1)
        sp.dma_start(raw[:, slot].rearrange("p k n -> p (k n)"), a["units"][bass.ds(u, 1)].rearrange("a p n -> (a p) n")).then_inc(raw_loaded[slot], 16)

    def split_hi(act, slot, fills, done):
        act.wait_ge(raw_loaded[slot], 16 * fills)
        act.wait_ge(tiles_done, done)
        nc.scalar.copy(whi[:, slot], raw[:, slot]).then_inc(hi_ready, 1)

    def split_lo(dve, u, slot):
        dve.wait_ge(hi_ready, u + 1)
        nc.vector.tensor_tensor(wlo[:, slot], raw[:, slot], whi[:, slot].bitcast(F32), ALU.subtract).then_inc(lo_ready, 1)

    def products(outs, terms):
        last = len(terms) - 1
        for n, (wh, wl, xs) in enumerate(terms):
            for m, w in enumerate((wh, wh, wl)):
                for b, out in enumerate(outs):
                    ins = nc.tensor.matmul(out, w, xs[b][m == 1], start=(n == 0 and m == 0), stop=(n == last and m == 2))
        return ins

    def halves(hi, lo, k):
        return [(hi[:, k, b * HALF:(b + 1) * HALF], lo[:, k, b * HALF:(b + 1) * HALF]) for b in (0, 1)]

    def unit_product(pe, u, slot):
        pe.wait_ge(lo_ready, u + 1)
        pe.wait_ge(psum_free, u + 1)
        products([pu[:, slot, b, 0:HALF] for b in (0, 1)],
                 [(whi[:, slot, k], wlo[:, slot, k], halves(xhi, xlo, k)) for k in range(KT)]).then_inc(tiles_done, 1)

    both = lambda slot: pu[:, slot, :, 0:HALF]
    in_two = lambda ap: ap.rearrange("p (b n) -> p b n", b=2)

    set_loaded = sem("set_loaded")
    mem_loaded = sem("mem_loaded")
    with nc.Block() as block:
        @block.sync
        def _(sp):
            sp.dma_start(consts[:], a["consts"]).then_inc(set_loaded, 16)
            sp.dma_start(vecs[:], a["vecs"]).then_inc(set_loaded, 16)
            sp.dma_start(mem[:], a["memT"]).then_inc(mem_loaded, 16)
            for u in (0, 1):
                sp.dma_start(raw[:, u].rearrange("p k n -> p (k n)"), a["units"][u]).then_inc(raw_loaded[u], 16)

        @block.scalar
        def _(act):
            act.wait_ge(set_loaded, 32)
            act.wait_ge(mem_loaded, 16)
            split_hi(act, 0, 1, 0)

        @block.vector
        def _(dve):
            dve.wait_ge(set_loaded, 32)
            dve.wait_ge(mem_loaded, 16)
            nc.vector.memset(gcol[:], 0.0).then_inc(psum_free, 2)
            split_lo(dve, 0, 0)

    squared = sem("squared")
    summed = sem("summed")
    ln_done = sem("ln_done")
    rinv_ready = sem("rinv_ready")
    scaled_ready = sem("scaled_ready")
    scaled_hi = sem("scaled_hi")
    scaled_lo = sem("scaled_lo")
    y_stored = [sem("y_stored0"), sem("y_stored1")]
    norm_count = [0]

    def rmsnorm(name, src, gain, n, hi=None, lo=None, final=None):
        place = region(WR, W_SIZE)
        squares = place(name + "_squares", [2, n])
        rinv = place(name + "_rinv", [n])
        scaled = place(name + "_scaled", [2, n])
        parts = [(0, n)] if n <= 512 else [(0, HALF), (HALF, n)]
        before = norm_count[0] * KT
        runs = norm_count[0]
        norm_count[0] += 1
        with nc.Block() as block:
            @block.scalar
            def _(act):
                with act.Fori(0, KT // 2) as i:
                    for s in (0, 1):
                        k = 2 * i + s
                        act.wait_ge(summed, 2 * i + before)
                        nc.scalar.activation(squares[:, s], src[:, bass.ds(k, 1)].rearrange("p k n -> p (k n)"), ACT.Square).then_inc(squared, 1)
                act.wait_ge(summed, before + KT)
                for b, (lo_, hi_) in enumerate(parts):
                    ins = nc.scalar.activation(rinv[:, lo_:hi_], pm[:, 0, b, 0:hi_ - lo_], ACT.Ln, scale=1.0 / D, bias=vecs[:, V_EPS:V_EPS + 1])
                ins.then_inc(ln_done, 1)
                act.wait_ge(ln_done, runs + 1)
                nc.scalar.activation(rinv[:], rinv[:], ACT.Exp, scale=-0.5).then_inc(rinv_ready, 1)
                if final is None:
                    with act.Fori(0, KT // 2) as i:
                        for s in (0, 1):
                            k = 2 * i + s
                            act.wait_ge(scaled_ready, k + (before + 1))
                            nc.scalar.copy(hi[:, bass.ds(k, 1)].rearrange("p k n -> p (k n)"), scaled[:, s]).then_inc(scaled_hi, 1)

            @block.tensor
            def _(pe):
                for k in range(KT):
                    pe.wait_ge(squared, before + k + 1)
                    for b, (lo_, hi_) in enumerate(parts):
                        ins = nc.tensor.matmul(pm[:, 0, b, 0:hi_ - lo_], ones, squares[:, k % 2, lo_:hi_], start=(k == 0), stop=(k == KT - 1))
                    ins.then_inc(summed, 1)

            @block.vector
            def _(dve):
                dve.wait_ge(rinv_ready, runs + 1)
                with dve.Fori(0, KT // 2) as i:
                    for s in (0, 1):
                        k = 2 * i + s
                        if final is None:
                            dve.wait_ge(scaled_lo, 2 * i + before)
                        else:
                            dve.wait_ge(y_stored[s], 16 * i)
                        nc.vector.scalar_tensor_tensor(scaled[:, s], src[:, bass.ds(k, 1)].rearrange("p k n -> p (k n)"),
                                                       vecs[:, bass.ds(k + gain, 1)], rinv[:], ALU.mult, ALU.mult).then_inc(scaled_ready, 1)

            @block.gpsimd
            def _(pool):
                if final is None:
                    with pool.Fori(0, KT // 2) as i:
                        for s in (0, 1):
                            k = 2 * i + s
                            pool.wait_ge(scaled_hi, k + (before + 1))
                            at = bass.ds(k, 1)
                            nc.gpsimd.tensor_tensor(lo[:, at].rearrange("p k n -> p (k n)"), scaled[:, s],
                                                    hi[:, at].rearrange("p k n -> p (k n)").bitcast(F32), ALU.subtract).then_inc(scaled_lo, 1)

            @block.sync
            def _(sp):
                if final is not None:
                    with sp.Fori(0, KT // 2) as i:
                        for s in (0, 1):
                            k = 2 * i + s
                            sp.wait_ge(scaled_ready, k + (before + 1))
                            sp.dma_start(final[bass.ds(k, 1)].rearrange("k p n -> (k p) n"), scaled[:, s]).then_inc(y_stored[s], 16)
                    for s in (0, 1):
                        sp.wait_ge(y_stored[s], 16 * KT // 2)

    def layer(base, n, pe_tile, act_tile=None, dve_tile=None, sp_tile=None, pool_tile=None):
        def loop(eng, before, tile):
            with eng.Fori(0, n // 2) as i:
                for s in (0, 1):
                    u, slot, fills = unit(base, i, s)
                    before(eng, i, s)
                    if tile:
                        tile(eng, u, slot, i, s)

        with nc.Block() as block:
            @block.sync
            def _(sp):
                def before(eng, i, s):
                    u, slot, _ = unit(base, i, s + 2)
                    load_unit(eng, u, slot)
                loop(sp, before, sp_tile)

            @block.scalar
            def _(act):
                def before(eng, i, s):
                    u, slot, fills = unit(base, i, s + 1)
                    split_hi(eng, slot, fills, u - 1)
                loop(act, before, act_tile)

            @block.vector
            def _(dve):
                def before(eng, i, s):
                    u, slot, _ = unit(base, i, s + 1)
                    split_lo(eng, u, slot)
                loop(dve, before, dve_tile)

            @block.tensor
            def _(pe):
                loop(pe, lambda *_: None, pe_tile)

            @block.gpsimd
            def _(pool):
                if pool_tile:
                    loop(pool, lambda *_: None, pool_tile)

    rmsnorm("nmem", mem, V_MEM, M, memhi, memlo)
    place = region(WR, W_SIZE)
    kv_out = place("kv_out", [2, M])
    k_stored = [sem("k_stored0"), sem("k_stored1")]
    v_stored = [sem("v_stored0"), sem("v_stored1")]

    def pe_k(pe, u, slot, i, s):
        pe.wait_ge(lo_ready, u + 1)
        pe.wait_ge(psum_free, u + 1)
        products([pu[:, slot, 0, 0:M]],
                 [(whi[:, slot, k], wlo[:, slot, k], [(memhi[:, k], memlo[:, k])]) for k in range(KT)]).then_inc(tiles_done, 1)

    def act_k(act, u, slot, i, s):
        act.wait_ge(tiles_done, u + 1)
        act.wait_ge(k_stored[s], 16 * i)
        nc.scalar.copy(kv_out[:, s], pu[:, slot, 0, 0:M]).then_inc(psum_free, 1)

    def sp_k(sp, u, slot, i, s):
        taken(sp, u)
        sp.dma_start(a["mkT"][bass.ds(2 * i + s, 1)].rearrange("k p n -> (k p) n"), kv_out[:, s]).then_inc(k_stored[s], 16)

    def pe_v(pe, u, slot, i, s):
        pe.wait_ge(lo_ready, u + 1)
        pe.wait_ge(psum_free, u + 1)
        for b in (0, 1):
            ins = products([pu[:, slot, b, 0:P]],
                           [(memhi[:, k, b * P:(b + 1) * P], memlo[:, k, b * P:(b + 1) * P], [(whi[:, slot, k], wlo[:, slot, k])]) for k in range(KT)])
        ins.then_inc(tiles_done, 1)

    def act_v(act, u, slot, i, s):
        act.wait_ge(tiles_done, u + 1)
        act.wait_ge(v_stored[s], 16 * i)
        nc.scalar.copy(kv_out[:, s].rearrange("p (b n) -> p b n", b=2), pu[:, slot, :, 0:P]).then_inc(psum_free, 1)

    def sp_v(sp, u, slot, i, s):
        taken(sp, u)
        sp.dma_start(a["mv"][:, :, bass.ds((2 * i + s) * P, P)], kv_out[:, s].rearrange("p (b n) -> p b n", b=2)).then_inc(v_stored[s], 16)

    layer(MK0, KT, pe_k, act_k, None, sp_k)
    with nc.Block() as block:
        @block.sync
        def _(sp):
            for s in (0, 1):
                sp.wait_ge(k_stored[s], 16 * KT // 2)
    layer(MV0, KT, pe_v, act_v, None, sp_v)

    x_loaded = sem("x_loaded")
    with nc.Block() as block:
        @block.sync
        def _(sp):
            for s in (0, 1):
                sp.wait_ge(v_stored[s], 16 * KT // 2)
            sp.dma_start(x[:], a["xT"]).then_inc(x_loaded, 16)
            sp.wait_ge(x_loaded, 16)
    rmsnorm("nmix", x, V_MIX, T, xhi, xlo)

    place = region(WR, W_SIZE)
    CL = 3 + TP + 3 + TS
    ext = place("ext", [2, CL])
    acc = [place(f"acc{i}", [CL - 3]) for i in range(4)]
    convd = place("convd", [2, TPAD])
    chist = place("chist", [24, 3])
    conv_new = place("conv_new", [24, 2, 3])
    PH = 15
    PL = PH + TP + PH + TS
    phist = place("phist", [8, PH])
    pool_new = place("pool_new", [8, 2, PH])
    pext = place("pext", [2, PL])
    wins = [place(f"win{i}", [PL]) for i in range(2)]
    mix = place("mix", [2, T])
    wpool = place("wpool", [KT, P])
    abT = place("abT", [TPAD])

    def act_z(act, u, slot, i, s):
        act.wait_ge(tiles_done, u + 1)
        nc.scalar.activation(cat[:, bass.ds(2 * i + s + 8, 1)].rearrange("p k (b n) -> p (k b) n", b=2), both(slot), ACT.Silu).then_inc(psum_free, 1)

    pe_linear = lambda pe, u, slot, i, s: unit_product(pe, u, slot)
    layer(Z0, 8, pe_linear, act_z)

    pool_loaded = sem("pool_loaded")
    pext_used = sem("pext_used")
    mix_ready = sem("mix_ready")
    mixed = sem("mixed")
    mixed_out = sem("mixed_out")
    pool_chain = sem("pool_chain")
    pool_stored = sem("pool_stored")
    with nc.Block() as block:
        @block.sync
        def _(sp):
            sp.dma_start(phist[:], a["phist"]).then_inc(pool_loaded, 16)
            sp.dma_start(chist[:], a["chist"]).then_inc(pool_loaded, 16)
            sp.dma_start(wpool[:], a["wpool"]).then_inc(pool_loaded, 16)
            sp.wait_ge(pool_loaded, 48)

        @block.gpsimd
        def _(pool):
            nc.gpsimd.memset(pext[:], 0.0)
            nc.gpsimd.memset(ext[:], 0.0)
            nc.gpsimd.memset(convd[:], 0.0)
            nc.gpsimd.memset(abT[:], 0.0)

    with nc.Block() as block:
        S0 = PH + TP + PH

        @block.sync
        def _(sp):
            with sp.Fori(0, 4) as i:
                for s in (0, 1):
                    u, slot, _ = unit(POOL0, i, s + 2)
                    load_unit(sp, u, slot)
            sp.wait_ge(pext_used, 8)
            sp.dma_start(a["pool_new"], pool_new[:]).then_inc(pool_stored, 16)
            sp.wait_ge(pool_stored, 16)

        @block.tensor
        def _(pe):
            for g in range(4):
                for s in (0, 1):
                    u, slot, _ = unit(POOL0, g, s)
                    unit_product(pe, u, slot)
                pe.wait_ge(mix_ready, 2 * g + 2)
                for d in (0, 1):
                    if g:
                        pe.wait_ge(mixed_out, 2 * (g - 1) + d + 1)
                    for b in (0, 1):
                        for c in (0, 1):
                            ins = nc.tensor.matmul(pm[:, d, b, 0:HALF], wpool[:, 4 * g + 2 * c + d], mix[:, c, b * HALF:(b + 1) * HALF],
                                                   start=(c == 0), stop=(c == 1))
                    ins.then_inc(mixed, 1)

        @block.scalar
        def _(act):
            for g in range(4):
                for s in (0, 1):
                    j = 2 * g + s
                    u, slot, fills = unit(POOL0, g, s + 1)
                    split_hi(act, slot, fills, u - 1)
                    u, slot, _ = unit(POOL0, g, s)
                    act.wait_ge(tiles_done, u + 1)
                    if g:
                        act.wait_ge(pext_used, j - 1)
                    nc.scalar.copy(pext[:, s, PH:PH + HALF], pu[:, slot, 0, 0:HALF])
                    nc.scalar.copy(pext[:, s, PH + HALF:PH + TP], pu[:, slot, 1, 0:TP - HALF])
                    nc.scalar.copy(pext[:, s, S0 - PH:S0], phist[:, j])
                    nc.scalar.copy(pext[:, s, S0:PL], pu[:, slot, 1, TP - HALF:HALF]).then_inc(psum_free, 1)
                for d in (0, 1):
                    act.wait_ge(mixed, 2 * g + d + 1)
                    nc.scalar.activation(in_two(cat[:, 2 * g + d]), pm[:, d, :, 0:HALF], ACT.Copy, scale=vecs[:, V_POOL + 2 * g + d:V_POOL + 2 * g + d + 1]).then_inc(mixed_out, 1)

        @block.vector
        def _(dve):
            chain = Chain(dve, pool_chain)
            for g in range(4):
                for s in (0, 1):
                    j = 2 * g + s
                    u, slot, _ = unit(POOL0, g, s + 1)
                    split_lo(dve, u, slot)
                    taken(dve, POOL0 + j)
                    e = pext[:, s]
                    cur = e
                    for l in range(g + 1):
                        sh = 1 << l
                        nxt = wins[l % 2]
                        chain.link(nc.vector.tensor_tensor(nxt[:, 2 * sh - 1:PL], cur[:, 2 * sh - 1:PL], cur[:, sh - 1:PL - sh], ALU.add))
                        cur = nxt
                    if j >= 2:
                        dve.wait_ge(mixed, 2 * g)
                    w = 2 << g
                    chain.link(nc.vector.tensor_tensor(wins[(g + 1) % 2][:, 0:16], cur[:, PH:PH + 16], consts[:, C_CNT + 16 * g:C_CNT + 16 * g + 16], ALU.mult))
                    nc.vector.tensor_tensor(mix[:, s, 0:16], wins[(g + 1) % 2][:, 0:16], e[:, PH:PH + 16], ALU.subtract)
                    nc.vector.scalar_tensor_tensor(mix[:, s, 16:TP], cur[:, PH + 16:PH + TP], 1.0 / w, e[:, PH + 16:PH + TP], ALU.mult, ALU.subtract)
                    nc.vector.scalar_tensor_tensor(mix[:, s, TP:T], cur[:, S0:PL], 1.0 / w, e[:, S0:PL], ALU.mult, ALU.subtract).then_inc(mix_ready, 1)
                    nc.vector.tensor_copy(pool_new[:, j, 0], e[:, TP:TP + PH])
                    nc.vector.tensor_copy(pool_new[:, j, 1], e[:, PL - PH:PL]).then_inc(pext_used, 1)
                    dve.wait_ge(pext_used, j + 1)

    conv_done = sem("conv_done")
    silu_done = sem("silu_done")
    qkv_stored = [sem("qkv_stored0"), sem("qkv_stored1")]
    conv_chain = sem("conv_chain")
    hist_kept = sem("hist_kept")
    conv_stored = sem("conv_stored")

    def act_qkv(act, u, slot, i, s):
        j = 2 * i + s
        act.wait_ge(tiles_done, u + 1)
        act.wait_ge(conv_done, 2 * i)
        act.wait_ge(hist_kept, 2 * i)
        nc.scalar.copy(ext[:, s, 3:3 + HALF], pu[:, slot, 0, 0:HALF])
        nc.scalar.copy(ext[:, s, 3 + HALF:3 + TP], pu[:, slot, 1, 0:TP - HALF])
        nc.scalar.copy(ext[:, s, 3 + TP:6 + TP], chist[:, bass.ds(j, 1)].rearrange("p j n -> p (j n)"))
        nc.scalar.copy(ext[:, s, 6 + TP:CL], pu[:, slot, 1, TP - HALF:HALF]).then_inc(psum_free, 1)
        act.wait_ge(conv_done, j + 1)
        act.wait_ge(qkv_stored[s], 16 * i)
        nc.scalar.activation(convd[:, s, 0:TP], acc[3][:, 0:TP], ACT.Silu)
        nc.scalar.activation(convd[:, s, TP:T], acc[3][:, TP + 3:TP + 3 + TS], ACT.Silu).then_inc(silu_done, 1)

    def pool_qkv(pool, u, slot, i, s):
        j = 2 * i + s
        taken(pool, u)
        at = bass.ds(j, 1)
        nc.gpsimd.tensor_copy(conv_new[:, at, 0].rearrange("p j n -> p (j n)"), ext[:, s, TP:TP + 3])
        nc.gpsimd.tensor_copy(conv_new[:, at, 1].rearrange("p j n -> p (j n)"), ext[:, s, CL - 3:CL]).then_inc(hist_kept, 1)

    def sp_qkv(sp, u, slot, i, s):
        sp.wait_ge(silu_done, 2 * i + s + 1)
        sp.dma_start(qkv_s[bass.ds(2 * i + s, 1)].rearrange("k p n -> (k p) n"), convd[:, s]).then_inc(qkv_stored[s], 16)

    chains = {}

    def dve_qkv(dve, u, slot, i, s):
        j = 2 * i + s
        if s == 0:
            chains["conv"] = Chain(dve, conv_chain)
            chains["conv"].enter(i, 6)
        link = chains["conv"].link
        taken(dve, u)
        n = CL - 3
        tap = lambda q: vecs[:, bass.ds(j * 4 + (V_CONV + q), 1)]
        dve.wait_ge(silu_done, j)
        link(nc.vector.tensor_scalar(acc[0][:], ext[:, s, 0:n], tap(0), None, ALU.mult))
        link(nc.vector.scalar_tensor_tensor(acc[1][:], ext[:, s, 1:1 + n], tap(1), acc[0][:], ALU.mult, ALU.add))
        link(nc.vector.scalar_tensor_tensor(acc[2][:], ext[:, s, 2:2 + n], tap(2), acc[1][:], ALU.mult, ALU.add))
        nc.vector.scalar_tensor_tensor(acc[3][:], ext[:, s, 3:3 + n], tap(3), acc[2][:], ALU.mult, ALU.add).then_inc(conv_done, 1)

    layer(QKV0, 24, pe_linear, act_qkv, dve_qkv, sp_qkv, pool_qkv)

    ab_turned = sem("ab_turned")
    g_act = sem("g_act")
    g_chain = sem("g_chain")
    place = region(WR + 4 * (2 * CL + 4 * (CL - 3) + 2 * TPAD + 24 * 9 + 8 * 45 + 2 * PL + 2 * PL + 2 * T + KT * P + TPAD) + 1024, 8192)
    NG = NCH * HEADS
    ab = place("ab", [NCH, 16])
    gt = [place(f"gt{i}", [NG]) for i in range(6)]
    with nc.Block() as block:
        @block.sync
        def _(sp):
            for s in (0, 1):
                sp.wait_ge(qkv_stored[s], 16 * 12)
            sp.dma_start(a["conv_new"], conv_new[:]).then_inc(conv_stored, 16)
            load_unit(sp, AB0 + 2, AB0 % 2)
            sp.wait_ge(conv_stored, 16)

        @block.tensor
        def _(pe):
            unit_product(pe, AB0, AB0 % 2)
            taken(pe, AB0)
            for c in range(NCH):
                ins = nc.tensor.transpose(pm[:, 0, 0, 16 * c:16 * c + 16], abT[0:16, c * P:(c + 1) * P], ident[0:16, 0:16])
            ins.then_inc(ab_turned, 1)

        @block.scalar
        def _(act):
            split_hi(act, (AB0 + 1) % 2, (AB0 + 1) // 2 + 1, AB0)
            act.wait_ge(tiles_done, AB0 + 1)
            for b in (0, 1):
                ins = nc.scalar.copy(abT[0:16, b * HALF:(b + 1) * HALF], pu[0:16, AB0 % 2, b, 0:HALF])
            ins.then_inc(psum_free, 1)
            act.wait_ge(g_chain, 4)
            nc.scalar.activation(gt[2][:], gt[1][:], ACT.Exp).then_inc(g_act, 1)
            act.wait_ge(g_act, 1)
            nc.scalar.activation(gt[3][:], gt[2][:], ACT.Ln, bias=1.0).then_inc(g_act, 1)
            nc.scalar.activation(gt[5][:, 0:HEADS], vecs[:, V_ALOG:V_ALOG + HEADS], ACT.Exp)
            nc.scalar.activation(beta[:].rearrange("p (c h) -> p c h", c=NCH), ab[:, :, 8:16], ACT.Sigmoid).then_inc(g_act, 1)

        @block.vector
        def _(dve):
            chain = Chain(dve, g_chain)
            split_lo(dve, AB0 + 1, (AB0 + 1) % 2)
            v3 = lambda t: t[:].rearrange("p (c h) -> p c h", c=NCH)
            dve.wait_ge(ab_turned, 1)
            chain.link(nc.vector.tensor_copy(ab[:], pm[:, 0, 0, 0:16 * NCH].rearrange("p (c n) -> p c n", c=NCH)))
            chain.link(nc.vector.tensor_tensor(v3(gt[0]), ab[:, :, 0:8], vecs[:, V_DT:V_DT + 8].unsqueeze(1).broadcast_to([P, NCH, 8]), ALU.add))
            chain.link(nc.vector.tensor_scalar(gt[4][:], gt[0][:], -1.0, None, ALU.mult))
            chain.link(nc.vector.tensor_tensor(gt[1][:], gt[0][:], gt[4][:], ALU.min))
            dve.wait_ge(g_act, 3)
            chain.link(nc.vector.scalar_tensor_tensor(gt[4][:], gt[0][:], 0.0, gt[3][:], ALU.max, ALU.add))
            chain.link(nc.vector.scalar_tensor_tensor(v3(gt[0]), v3(gt[4]), -1.0, gt[5][:, 0:8].unsqueeze(1).broadcast_to([P, NCH, 8]), ALU.mult, ALU.mult))
            valid = consts[:, C_VALID:C_VALID + NG]
            nc.vector.tensor_tensor(gcol[:], gt[0][:], valid, ALU.mult)
            chain.link(nc.vector.tensor_tensor(gt[1][:], beta[:], valid, ALU.mult))
            chain.link(nc.vector.tensor_copy(beta[:], gt[1][:]))

    deltanet(nc, es, sem, region, a, dict(
        HR=HR, H_SIZE=H_SIZE, WR=WR, W_SIZE=W_SIZE, consts=consts, vecs=vecs, gcol=gcol, beta=beta, cat=cat,
        SLOT=SLOT, qkv_s=qkv_s, ident=ident, ones=ones, cum=cum))

    cat_hi = sem("cat_hi")
    x_back = sem("x_back")
    cat_lo = sem("cat_lo")
    with nc.Block() as block:
        @block.scalar
        def _(act):
            with act.Fori(0, KT) as k:
                nc.scalar.copy(xhi[:, bass.ds(k, 1)], cat[:, bass.ds(k, 1)]).then_inc(cat_hi, 1)

        @block.vector
        def _(dve):
            with dve.Fori(0, KT) as k:
                at = bass.ds(k, 1)
                dve.wait_ge(cat_hi, k + 1)
                nc.vector.tensor_tensor(xlo[:, at], cat[:, at], xhi[:, at].bitcast(F32), ALU.subtract).then_inc(cat_lo, 1)

        @block.sync
        def _(sp):
            sp.wait_ge(cat_lo, KT)
            sp.dma_start(x[:], a["xT"]).then_inc(x_back, 16)
            sp.wait_ge(x_back, 16)

    def dve_residual(dve, u, slot, i, s):
        dve.wait_ge(tiles_done, u + 1)
        at = x[:, bass.ds(2 * i + s, 1)].rearrange("p k (b n) -> p (k b) n", b=2)
        nc.vector.tensor_tensor(at, both(slot), at, ALU.add).then_inc(psum_free, 1)

    layer(OUT0, KT, pe_linear, None, dve_residual)

    def to_scratch(name, base):
        place = region(WR, W_SIZE)
        q_out = place(name + "_out", [2, TPAD])
        q_stored = [sem(name + "_stored0"), sem(name + "_stored1")]
        with nc.Block() as block:
            @block.gpsimd
            def _(pool):
                nc.gpsimd.memset(q_out[:], 0.0)

        def act_q(act, u, slot, i, s):
            act.wait_ge(tiles_done, u + 1)
            act.wait_ge(q_stored[s], 16 * i)
            nc.scalar.copy(in_two(q_out[:, s, 0:T]), both(slot)).then_inc(psum_free, 1)

        def sp_q(sp, u, slot, i, s):
            taken(sp, u)
            sp.dma_start(q_s[bass.ds(2 * i + s, 1)].rearrange("k p n -> (k p) n"), q_out[:, s]).then_inc(q_stored[s], 16)

        layer(base, KT, pe_linear, act_q, None, sp_q)
        with nc.Block() as block:
            @block.sync
            def _(sp):
                for s in (0, 1):
                    sp.wait_ge(q_stored[s], 16 * KT // 2)

    rmsnorm("nxa", x, V_XATTN, T, xhi, xlo)
    to_scratch("mq", MQ0)
    attention(nc, es, sem, region, a, dict(WR=WR, W_SIZE=W_SIZE, pu=pu, pm=pm, q_s=q_s, xhi=xhi, xlo=xlo, ident=ident))
    layer(MO0, KT, pe_linear, None, dve_residual)

    rmsnorm("nffn", x, V_FFN, T, xhi, xlo)
    to_scratch("pq", PQ0)
    routing(nc, es, sem, region, a, dict(WR=WR, W_SIZE=W_SIZE, pu=pu, pm=pm, q_s=q_s, gate_s=gate_s, ident=ident, consts=consts))

    place = region(WR, W_SIZE)
    gates = place("gates", [T, GRP])
    hidden = place("hidden", [2, T])
    coef = place("coef", [2, T])
    chi = place("chi", [GRP, T], F32R)
    clo = place("clo", [GRP, T], F32R)
    gates_loaded = sem("gates_loaded")
    coef_done = sem("coef_done")
    chi_done = sem("chi_done")
    clo_done = sem("clo_done")
    TILES = GRP + KT
    VU = KT // 4

    def done_by(g, q):
        return g * TILES + (EXP0 + (q + 1 if q < GRP else GRP + 4 * (q + 1 - GRP)))

    def group_sp(sp, g, last):
        for q in range(GRP + VU):
            if not (last and q >= GRP + VU - 2):
                load_unit(sp, g * 8 + (EXP0 + q + 2), (EXP0 + q) % 2)
            if q == 0:
                sp.wait_ge(coef_done, g * GRP)
                sp.dma_start(gates[:].rearrange("p t i -> p (t i)"), a["gate_s"][bass.ds(g, 1)].rearrange("g p n -> (g p) n")).then_inc(gates_loaded, 16)

    def group_pe(pe, g):
        for q in range(GRP + VU):
            slot = (EXP0 + q) % 2
            pe.wait_ge(lo_ready, g * 8 + (EXP0 + q + 1))
            if q < GRP:
                pe.wait_ge(psum_free, g * TILES + (EXP0 + q + 1))
                products([pu[:, q % 2, b, 0:HALF] for b in (0, 1)],
                         [(whi[:, slot, k], wlo[:, slot, k], halves(xhi, xlo, k)) for k in range(KT)]).then_inc(tiles_done, 1)
                continue
            if q == GRP:
                pe.wait_ge(clo_done, g * GRP + GRP)
            for d in range(4):
                pe.wait_ge(psum_free, g * TILES + (EXP0 + GRP + 4 * (q - GRP) + d + 1))
                products([pu[:, d % 2, b, 0:HALF] for b in (0, 1)],
                         [(whi[:, slot, GRP * d + k], wlo[:, slot, GRP * d + k], halves(chi, clo, k)) for k in range(GRP)]).then_inc(tiles_done, 1)

    def group_act(act, g, last):
        for q in range(GRP + VU):
            if not (last and q == GRP + VU - 1):
                split_hi(act, (EXP0 + q + 1) % 2, g * 4 + ((EXP0 + q + 1) // 2 + 1), done_by(g, q - 1) if q else g * TILES + EXP0)
            if q < GRP:
                n = g * GRP + q
                act.wait_ge(tiles_done, g * TILES + (EXP0 + q + 1))
                if q >= 2:
                    act.wait_ge(coef_done, n - 1)
                nc.scalar.activation(in_two(hidden[:, q % 2]), pu[:, q % 2, :, 0:HALF], ACT.Gelu).then_inc(psum_free, 1)
                act.wait_ge(coef_done, n + 1)
                if q == 0:
                    act.wait_ge(tiles_done, g * TILES + EXP0)
                nc.scalar.copy(chi[:, q], coef[:, q % 2]).then_inc(chi_done, 1)

    def group_dve(dve, g, last):
        for q in range(GRP + VU):
            if not (last and q == GRP + VU - 1):
                split_lo(dve, g * 8 + (EXP0 + q + 1), (EXP0 + q + 1) % 2)
            if q < GRP:
                n = g * GRP + q
                taken(dve, g * TILES + (EXP0 + q))
                if q == 0:
                    dve.wait_ge(gates_loaded, 16 * g + 16)
                nc.vector.tensor_tensor(coef[:, q % 2], hidden[:, q % 2], gates[:, :, q], ALU.mult).then_inc(coef_done, 1)
                dve.wait_ge(chi_done, n + 1)
                nc.vector.tensor_tensor(clo[:, q], coef[:, q % 2], chi[:, q].bitcast(F32), ALU.subtract).then_inc(clo_done, 1)
                continue
            for d in range(4):
                o = 4 * (q - GRP) + d
                dve.wait_ge(tiles_done, g * TILES + (EXP0 + GRP + o + 1))
                nc.vector.tensor_tensor(in_two(x[:, o]), pu[:, d % 2, :, 0:HALF], in_two(x[:, o]), ALU.add).then_inc(psum_free, 1)

    a["gate_s"] = gate_s
    with nc.Block() as block:
        @block.sync
        def _(sp):
            with sp.Fori(0, NGRP - 1) as g:
                group_sp(sp, g, False)
            group_sp(sp, NGRP - 1, True)

        @block.tensor
        def _(pe):
            with pe.Fori(0, NGRP) as g:
                group_pe(pe, g)

        @block.scalar
        def _(act):
            with act.Fori(0, NGRP - 1) as g:
                group_act(act, g, False)
            group_act(act, NGRP - 1, True)

        @block.vector
        def _(dve):
            with dve.Fori(0, NGRP - 1) as g:
                group_dve(dve, g, False)
            group_dve(dve, NGRP - 1, True)

    rmsnorm("nfin", x, V_FINAL, T, final=a["yT"])
    es.close()


def deltanet(nc, es, sem, region, a, m):
    consts, vecs, SLOT, cat, ident, ones, cum = (m[k] for k in ("consts", "vecs", "SLOT", "cat", "ident", "ones", "cum"))
    beta, gcol, qkv_s = m["beta"], m["gcol"], m["qkv_s"]
    HP = [HEADS, P]
    pw = region(m["WR"], m["W_SIZE"])
    ph = region(m["HR"], m["H_SIZE"])
    qc, kc, vc = (pw(n, HP) for n in ("qc", "kc", "vc"))
    qn, kn, qdec, grows, egam = (pw(n, HP) for n in ("qn", "kn", "qdec", "grows", "egam"))
    vnat, kdec, resid = (pw(n, HP) for n in ("vnat", "kdec", "resid"))
    gcum, egcum = pw("gcum", [NCH * HEADS]), pw("egcum", [NCH * HEADS])
    glast, kscale = pw("glast", [HEADS]), pw("kscale", [HEADS])
    dA, dB, A, att, attm = (ph(n, HP) for n in ("dA", "dB", "A", "att", "attm"))
    Tn, Tt, half, vnew, S, Sd, o, og = (ph(n, HP) for n in ("Tn", "Tt", "halfp", "vnew", "S", "Sd", "o", "og"))
    L = [ph(f"L{i}", HP) for i in (0, 1)]
    sq = ph("sq", HP)
    rr = ph("rr", HP)
    flat = lambda t: t[:].rearrange("p h n -> p (h n)")
    psum = lambda s: SLOT[s].rearrange("p (h n) -> p h n", n=P)
    bc_in = lambda ap: ap.unsqueeze(2).broadcast_to([P, HEADS, P])
    bc_h = lambda ap: ap.unsqueeze(1).broadcast_to([P, HEADS, P])

    names = ("loaded summed spread gamma gam_ready diffs exps sq_q sq_k ssq ssk rk normed_k scores decayed turned "
             "kdec_done vnat_done level_l level_p level_pc level_x level_t ks resid_done vn vn_copied qdec_done outs sqo sso "
             "ro cat_done s_loaded chain_a chain_d").split()
    q = {n: sem("dn_" + n) for n in names}
    s_stored = sem("dn_s_stored")

    with nc.Block() as block:
        @block.tensor
        def _(pe):
            nc.tensor.matmul(SLOT[0][:, 0:NCH * HEADS], cum, gcol[:], start=True, stop=True).then_inc(q["summed"], 1)

        @block.vector
        def _(dve):
            dve.wait_ge(q["summed"], 1)
            nc.vector.tensor_copy(gcum[:], SLOT[0][:, 0:NCH * HEADS]).then_inc(q["gam_ready"], 1)
            nc.vector.memset(flat(S), 0.0)

        @block.scalar
        def _(act):
            act.wait_ge(q["gam_ready"], 1)
            nc.scalar.activation(egcum[:], gcum[:], ACT.Exp)

    A_, B_, C_, D_ = range(4)
    PER = {"level": LEVELS}

    def sp_chunk(sp, c):
        sp.wait_ge(q["cat_done"], c)
        for n, t in enumerate((qc, kc, vc)):
            sp.dma_start(t[:], qkv_s[8 * n:8 * n + 8, :, bass.ds(c * P, P)].rearrange("h p n -> p h n")).then_inc(q["loaded"], 16)

    def pe_chunk(pe, c):
        pe.wait_ge(q["spread"], c + 1)
        for h in range(HEADS):
            ins = nc.tensor.matmul(psum(A_)[:, h], grows[:, h], cum, start=True, stop=True)
        ins.then_inc(q["gamma"], 1)
        for slot, src, ready, out in ((B_, 0, "sq_q", "ssq"), (C_, 1, "sq_k", "ssk")):
            pe.wait_ge(q[ready], c + 1)
            t = (sq, rr)[src]
            for b in (0, 1):
                ins = nc.tensor.matmul(SLOT[slot][:, 512 * b:512 * b + 512], ones, flat(t)[:, 512 * b:512 * b + 512], start=True, stop=True)
            ins.then_inc(q[out], 1)
        pe.wait_ge(q["normed_k"], c + 1)
        for h in range(HEADS):
            nc.tensor.matmul(psum(D_)[:, h], kn[:, h], kn[:, h], start=True, stop=True)
        pe.wait_ge(q["exps"], c + 1)
        for h in range(HEADS):
            ins = nc.tensor.matmul(psum(A_)[:, h], kn[:, h], qn[:, h], start=True, stop=True)
        ins.then_inc(q["scores"], 1)
        for h in range(HEADS):
            nc.tensor.transpose(psum(B_)[:, h], kn[:, h], ident)
        for h in range(HEADS):
            ins = nc.tensor.transpose(psum(C_)[:, h], vc[:, h], ident)
        ins.then_inc(q["turned"], 1)
        pe.wait_ge(q["kdec_done"], c + 1)
        pe.wait_ge(q["vnat_done"], c + 1)
        for l in range(LEVELS):
            n = c * LEVELS + l
            pe.wait_ge(q["level_l"], n + 1)
            if l == 0:
                pe.wait_ge(q["decayed"], c + 1)
            pe.wait_ge(q["level_t"], n + c + 1)
            for h in range(HEADS):
                ins = nc.tensor.matmul(psum(D_)[:, h], L[l % 2][:, h], Tt[:, h], start=True, stop=True)
            ins.then_inc(q["level_p"], 1)
            pe.wait_ge(q["level_pc"], n + 1)
            for h in range(HEADS):
                nc.tensor.matmul(psum(A_)[:, h], Tn[:, h], half[:, h], start=True, stop=True)
            for h in range(HEADS):
                ins = nc.tensor.matmul(psum(B_)[:, h], half[:, h], Tn[:, h], start=True, stop=True)
            ins.then_inc(q["level_x"], 1)
        for h in range(HEADS):
            ins = nc.tensor.matmul(psum(C_)[:, h], kn[:, h], S[:, h], start=True, stop=True)
        ins.then_inc(q["ks"], 1)
        pe.wait_ge(q["resid_done"], c + 1)
        for h in range(HEADS):
            ins = nc.tensor.matmul(psum(D_)[:, h], Tt[:, h], resid[:, h], start=True, stop=True)
        ins.then_inc(q["vn"], 1)
        pe.wait_ge(q["vn_copied"], c + 1)
        pe.wait_ge(q["qdec_done"], c + 1)
        for h in range(HEADS):
            nc.tensor.matmul(psum(A_)[:, h], S[:, h], qdec[:, h], start=True, stop=False)
            nc.tensor.matmul(psum(A_)[:, h], vnew[:, h], attm[:, h], start=False, stop=True)
        for h in range(HEADS):
            ins = nc.tensor.matmul(psum(B_)[:, h], kdec[:, h], vnew[:, h], start=True, stop=True)
        ins.then_inc(q["outs"], 1)
        pe.wait_ge(q["sqo"], c + 1)
        for b in (0, 1):
            ins = nc.tensor.matmul(SLOT[C_][:, 512 * b:512 * b + 512], ones, flat(sq)[:, 512 * b:512 * b + 512], start=True, stop=True)
        ins.then_inc(q["sso"], 1)

    eps = vecs[:, V_EPS:V_EPS + 1]

    def act_chunk(act, c, chain):
        act.wait_ge(q["loaded"], 48 * c + 48)
        nc.scalar.activation(flat(sq), flat(qc), ACT.Square).then_inc(q["sq_q"], 1)
        nc.scalar.activation(flat(rr), flat(kc), ACT.Square).then_inc(q["sq_k"], 1)
        act.wait_ge(q["diffs"], c + 1)
        nc.scalar.activation(flat(egam), SLOT[A_], ACT.Exp)
        nc.scalar.activation(flat(dA), flat(dA), ACT.Exp, scale=-1.0)
        nc.scalar.activation(flat(dB), flat(dB), ACT.Exp)
        nc.scalar.activation(kscale[:], glast[:], ACT.Exp).then_inc(q["exps"], 1)
        act.wait_ge(q["ssq"], c + 1)
        act.wait_ge(q["ssk"], c + 1)
        nc.scalar.activation(flat(sq), SLOT[B_], ACT.Ln, bias=eps)
        chain.link(nc.scalar.activation(flat(rr), SLOT[C_], ACT.Ln, bias=eps))
        nc.scalar.activation(flat(sq), flat(sq), ACT.Exp, scale=-0.5)
        nc.scalar.activation(flat(rr), flat(rr), ACT.Exp, scale=-0.5).then_inc(q["rk"], 1)
        act.wait_ge(q["turned"], c + 1)
        nc.scalar.copy(flat(vnat), SLOT[C_]).then_inc(q["vnat_done"], 1)
        for l in range(LEVELS):
            act.wait_ge(q["level_p"], c * LEVELS + l + 1)
            nc.scalar.copy(flat(half), SLOT[D_]).then_inc(q["level_pc"], 1)
        act.wait_ge(q["vn"], c + 1)
        nc.scalar.copy(flat(vnew), SLOT[D_]).then_inc(q["vn_copied"], 1)
        act.wait_ge(q["outs"], c + 1)
        nc.scalar.activation(flat(sq), SLOT[A_], ACT.Square).then_inc(q["sqo"], 1)
        nc.scalar.copy(flat(o), SLOT[A_])
        act.wait_ge(q["sso"], c + 1)
        chain.link(nc.scalar.activation(flat(rr), SLOT[C_], ACT.Ln, scale=1.0 / P, bias=eps))
        nc.scalar.activation(flat(rr), flat(rr), ACT.Exp, scale=-0.5).then_inc(q["ro"], 1)
        act.wait_ge(q["cat_done"], c + 1)

    def dve_chunk(dve, c, chain, width):
        tt = nc.vector.tensor_tensor
        cols = lambda t: t[:, bass.ds(c * HEADS, HEADS)]
        dve.wait_ge(q["gamma"], c + 1)
        tt(dA[:], psum(A_), bc_in(cols(gcum)), ALU.subtract)
        tt(glast[:], psum(A_)[:, :, P - 1], cols(gcum), ALU.subtract)
        chain.link(tt(dB[:], psum(A_), bc_in(cols(gcum)), ALU.subtract))
        nc.vector.tensor_scalar(flat(dA), flat(dA), 0.0, None, ALU.max)
        nc.vector.tensor_scalar(flat(dB), flat(dB), 0.0, None, ALU.min).then_inc(q["diffs"], 1)
        dve.wait_ge(q["loaded"], 48 * c + 48)
        dve.wait_ge(q["rk"], c + 1)
        nc.vector.scalar_tensor_tensor(flat(qn), flat(qc), float(P) ** -0.5, flat(sq), ALU.mult, ALU.mult)
        tt(flat(kn), flat(kc), flat(rr), ALU.mult).then_inc(q["normed_k"], 1)
        dve.wait_ge(q["scores"], c + 1)
        chain.link(tt(A[:], psum(D_), bc_in(cols(beta)), ALU.mult))
        dve.wait_ge(q["exps"], c + 1)
        tt(flat(A), flat(A), flat(dA), ALU.mult).then_inc(q["decayed"], 1)
        chain.link(tt(flat(att), SLOT[A_], flat(dB), ALU.mult))
        tt(attm[:], att[:], bc_h(cum), ALU.mult)
        dve.wait_ge(q["turned"], c + 1)
        tt(kdec[:], psum(B_), bc_in(kscale[:]), ALU.mult).then_inc(q["kdec_done"], 1)
        nc.vector.tensor_copy(Tn[:], bc_h(ident))
        nc.vector.tensor_copy(Tt[:], bc_h(ident)).then_inc(q["level_t"], 1)
        for l in range(LEVELS):
            dve.wait_ge(q["level_x"], c * LEVELS + l + 1)
            tt(flat(Tt), flat(Tt), SLOT[A_], ALU.subtract)
            tt(flat(Tn), flat(Tn), SLOT[B_], ALU.subtract).then_inc(q["level_t"], 1)
        dve.wait_ge(q["ks"], c + 1)
        chain.link(tt(resid[:], psum(C_), bc_in(cols(egcum)), ALU.mult))
        chain.link(tt(flat(resid), flat(vnat), flat(resid), ALU.subtract))
        tt(resid[:], resid[:], bc_in(cols(beta)), ALU.mult).then_inc(q["resid_done"], 1)
        dve.wait_ge(q["outs"], c + 1)
        chain.link(tt(Sd[:], S[:], bc_in(egam[:, :, P - 1]), ALU.mult))
        tt(flat(S), flat(Sd), SLOT[B_], ALU.add)
        dve.wait_ge(q["ro"], c + 1)
        chain.link(nc.vector.scalar_tensor_tensor(flat(og), flat(o), vecs[:, V_DN:V_DN + 1], flat(rr), ALU.mult, ALU.mult))
        at = cat[:, 8:16, bass.ds(c * P, width)]
        tt(at, og[:, :, 0:width], at, ALU.mult).then_inc(q["cat_done"], 1)

    def pool_chunk(pool, c):
        pool.wait_ge(q["cat_done"], c)
        nc.gpsimd.tensor_tensor(grows[:], bc_h(ones), bc_in(gcol[:, bass.ds(c * HEADS, HEADS)]), ALU.mult).then_inc(q["spread"], 1)
        pool.wait_ge(q["decayed"], c + 1)
        for l in range(LEVELS):
            if l >= 2:
                pool.wait_ge(q["level_p"], c * LEVELS + l - 1)
            nc.gpsimd.tensor_tensor(L[l % 2][:], A[:], bc_h(consts[:, C_LEV + l * P:C_LEV + (l + 1) * P]), ALU.mult).then_inc(q["level_l"], 1)
        nc.gpsimd.tensor_tensor(flat(qdec), flat(qn), flat(egam), ALU.mult).then_inc(q["qdec_done"], 1)

    def chunks(first, count, width):
        def run(eng, body):
            if count > 1:
                with eng.Fori(first, first + count) as c:
                    body(c)
            else:
                body(first)

        with nc.Block() as block:
            @block.sync
            def _(sp):
                run(sp, lambda c: sp_chunk(sp, c))

            @block.tensor
            def _(pe):
                run(pe, lambda c: pe_chunk(pe, c))

            @block.scalar
            def _(act):
                def body(c):
                    chain = Chain(act, q["chain_a"])
                    chain.enter(c, 2)
                    act_chunk(act, c, chain)
                run(act, body)

            @block.vector
            def _(dve):
                def body(c):
                    chain = Chain(dve, q["chain_d"])
                    chain.enter(c, 7)
                    dve_chunk(dve, c, chain, width)
                    assert chain.n == 7, chain.n
                run(dve, body)

            @block.gpsimd
            def _(pool):
                run(pool, lambda c: pool_chunk(pool, c))

    chunks(0, NCH - 1, P)
    with nc.Block() as block:
        @block.sync
        def _(sp):
            sp.dma_start(a["dn_prompt"].rearrange("h p n -> p h n"), S[:]).then_inc(s_stored, 16)
            sp.wait_ge(s_stored, 16)
            sp.dma_start(S[:], a["state"].rearrange("h p n -> p h n")).then_inc(q["s_loaded"], 16)
            sp.wait_ge(q["s_loaded"], 16)
    chunks(NCH - 1, 1, TS)
    with nc.Block() as block:
        @block.sync
        def _(sp):
            sp.dma_start(a["dn_sample"].rearrange("h p n -> p h n"), S[:]).then_inc(s_stored, 16)
            sp.wait_ge(s_stored, 32)


def attention(nc, es, sem, region, a, m):
    pu, pm, q_s, xhi, xlo, ident = (m[k] for k in ("pu", "pm", "q_s", "xhi", "xlo", "ident"))
    place = region(m["WR"], m["W_SIZE"])
    qh = place("qh", [2, MHT, T])
    kh = place("kh", [2, MHT, M])
    vh = place("vh", [2, 2, MHT * P])
    pr = place("pr", [4, M])
    pn = place("pn", [4, M])
    pT = place("pT", [2, TP])
    mx, nmx, sm, rs = (place("at_" + n, [4]) for n in ("mx", "nmx", "sm", "rs"))
    names = "k_loaded0 k_loaded1 scores maxed exps normed turned copied pv out_hi out_lo".split()
    q = {n: sem("at_" + n) for n in names}
    chain_sem = sem("at_chain")
    loaded = [q["k_loaded0"], q["k_loaded1"]]
    jobs = [(h, 0, P, TP // P, a["mkT"], a["mv"]) for h in range(MH)]
    jobs += [(h, TP, TS, 1, a["mkT_sample"], a["mv_sample"]) for h in range(MH)]
    with nc.Block() as block:
        @block.sync
        def _(sp):
            for n, (h, t0, w, tiles, kk, vv) in enumerate(jobs):
                if n >= 2:
                    sp.wait_ge(q["pv"], MHT * (n - 1))
                s = n % 2
                sp.dma_start(qh[:, s], q_s[MHT * h:MHT * h + MHT, :, 0:T].rearrange("k p n -> p k n")).then_inc(loaded[s], 16)
                sp.dma_start(kh[:, s], kk[MHT * h:MHT * h + MHT].rearrange("k p n -> p k n")).then_inc(loaded[s], 16)
                sp.dma_start(vh[:, s], vv[:, :, h * MHT * P:(h + 1) * MHT * P]).then_inc(loaded[s], 16)

        @block.tensor
        def _(pe):
            for n, (h, t0, w, tiles, kk, vv) in enumerate(jobs):
                s = n % 2
                pe.wait_ge(loaded[s], 48 * (n // 2 + 1))
                if n:
                    pe.wait_ge(q["exps"], n)
                for i in range(tiles):
                    for j in range(MHT):
                        ins = nc.tensor.matmul(pm[0:w, i // 2, i % 2, 0:M], qh[:, s, j, t0 + i * P:t0 + i * P + w], kh[:, s, j],
                                               start=(j == 0), stop=(j == MHT - 1))
                ins.then_inc(q["scores"], 1)
                pe.wait_ge(q["normed"], n + 1)
                for i in range(tiles):
                    for b in (0, 1):
                        ins = nc.tensor.transpose(pu[:, 0, b, i * P:i * P + w], pn[0:w, i, b * P:(b + 1) * P], ident[0:w, 0:w])
                ins.then_inc(q["turned"], 1)
                pe.wait_ge(q["copied"], n + 1)
                for j in range(MHT):
                    o = n * MHT + j
                    if o >= 2:
                        pe.wait_ge(q["out_lo"], o - 1)
                    for b in (0, 1):
                        ins = nc.tensor.matmul(pu[:, 1, o % 2, 0:tiles * w], vh[:, s, b, j * P:(j + 1) * P], pT[:, b, 0:tiles * w],
                                               start=(b == 0), stop=(b == 1))
                    ins.then_inc(q["pv"], 1)

        @block.vector
        def _(dve):
            chain = Chain(dve, chain_sem)
            for n, (h, t0, w, tiles, kk, vv) in enumerate(jobs):
                dve.wait_ge(q["scores"], n + 1)
                sc = pm[0:w].rearrange("p a b n -> p (a b) n")[:, 0:tiles, 0:M]
                chain.link(nc.vector.tensor_reduce(mx[0:w, 0:tiles], sc, AX_X, ALU.max))
                nc.vector.tensor_scalar(nmx[0:w, 0:tiles], mx[0:w, 0:tiles], -MEM_SCALE, None, ALU.mult).then_inc(q["maxed"], 1)
                dve.wait_ge(q["exps"], n + 1)
                chain.link(nc.vector.reciprocal(rs[0:w, 0:tiles], sm[0:w, 0:tiles]))
                nc.vector.tensor_tensor(pn[0:w, 0:tiles], pr[0:w, 0:tiles], rs[0:w, 0:tiles].unsqueeze(2).broadcast_to([w, tiles, M]), ALU.mult).then_inc(q["normed"], 1)
                for j in range(MHT):
                    o = n * MHT + j
                    dve.wait_ge(q["out_hi"], o + 1)
                    at = slice(t0, t0 + tiles * w)
                    nc.vector.tensor_tensor(xlo[:, MHT * h + j, at], pu[:, 1, o % 2, 0:tiles * w], xhi[:, MHT * h + j, at].bitcast(F32), ALU.subtract).then_inc(q["out_lo"], 1)

        @block.scalar
        def _(act):
            for n, (h, t0, w, tiles, kk, vv) in enumerate(jobs):
                act.wait_ge(q["maxed"], n + 1)
                for i in range(tiles):
                    ins = nc.scalar.activation(pr[0:w, i], pm[0:w, i // 2, i % 2, 0:M], ACT.Exp, scale=MEM_SCALE,
                                               bias=nmx[0:w, i:i + 1], accum_out=sm[0:w, i:i + 1])
                ins.then_inc(q["exps"], 1)
                act.wait_ge(q["turned"], n + 1)
                nc.scalar.copy(pT[:, :, 0:tiles * w], pu[:, 0, :, 0:tiles * w]).then_inc(q["copied"], 1)
                for j in range(MHT):
                    o = n * MHT + j
                    act.wait_ge(q["pv"], o + 1)
                    nc.scalar.copy(xhi[:, MHT * h + j, t0:t0 + tiles * w], pu[:, 1, o % 2, 0:tiles * w]).then_inc(q["out_hi"], 1)


def routing(nc, es, sem, region, a, m):
    pu, pm, q_s, gate_s, ident, consts = (m[k] for k in ("pu", "pm", "q_s", "gate_s", "ident", "consts"))
    place = region(m["WR"], m["W_SIZE"])
    gateT, rowT, colT = (place(n, [TPAD]) for n in ("gateT", "rowT", "colT"))
    used = 3 * 4 * TPAD
    place = region(m["WR"] + used, m["W_SIZE"] - used)
    qt = place("qt", [KT, P])
    keys = place("keys", [KT, P])
    sc = place("sc", [KT, P])
    cand = place("cand", [8, TOPK * TOPK])
    v1 = place("v1", [KT, TOPK])
    i1 = place("i1", [KT, TOPK], U32)
    f1 = place("f1", [KT, TOPK])
    v2 = place("v2", [8, TOPK])
    i2 = place("i2", [8, TOPK], U32)
    ia, ib = place("ia", [8, TOPK], U32), place("ib", [8, TOPK], U32)
    fa, fb = place("fa", [8, TOPK]), place("fb", [8, TOPK])
    row, col = place("row", [8, TOPK]), place("col", [8, TOPK])
    ex, gate = place("ex", [8, TOPK]), place("gate", [8, TOPK])
    sm, rs, pause = place("rt_sm", [8]), place("rt_rs", [8]), place("pause", [1])
    pick = cand
    names = "keys_loaded q_loaded scores sc_ready dif exped slots_ready turned taken chain".split()
    q = {n: sem("rt_" + n) for n in names}
    LINKS = 21

    with nc.Block() as block:
        @block.sync
        def _(sp):
            sp.dma_start(keys[:], a["keys"]).then_inc(q["keys_loaded"], 16)
            with sp.Fori(0, NCH) as t:
                sp.wait_ge(q["scores"], t)
                sp.dma_start(qt[:], q_s[:, :, bass.ds(t * P, P)].rearrange("k p n -> p k n")).then_inc(q["q_loaded"], 16)

        @block.tensor
        def _(pe):
            pe.wait_ge(q["keys_loaded"], 16)
            with pe.Fori(0, NCH) as t:
                pe.wait_ge(q["q_loaded"], 16 * t + 16)
                pe.wait_ge(q["sc_ready"], t)
                for k in range(KT):
                    ins = nc.tensor.matmul(pm[:, k // 8, (k // 4) % 2, (k % 4) * P:(k % 4 + 1) * P], qt[:, k], keys[:, k], start=True, stop=True)
                ins.then_inc(q["scores"], 1)
                pe.wait_ge(q["slots_ready"], t + 1)
                for n, src in enumerate((gate, row, col)):
                    ins = nc.tensor.transpose(pu[:, 0, 0, n * P:(n + 1) * P], src[:].rearrange("p h k -> p (h k)"), ident)
                ins.then_inc(q["turned"], 1)

        @block.scalar
        def _(act):
            with act.Fori(0, NCH) as t:
                act.wait_ge(q["scores"], t + 1)
                act.wait_ge(q["slots_ready"], t)
                nc.scalar.copy(sc[:].rearrange("p k n -> p (k n)"), pm[:].rearrange("p a b n -> p (a b n)")).then_inc(q["sc_ready"], 1)
                act.wait_ge(q["dif"], t + 1)
                nc.scalar.activation(ex[:], v2[:], ACT.Exp).then_inc(q["exped"], 1)
                act.wait_ge(q["turned"], t + 1)
                for n, dst in enumerate((gateT, rowT, colT)):
                    ins = nc.scalar.copy(dst[:, bass.ds(t * P, P)], pu[:, 0, 0, n * P:(n + 1) * P])
                ins.then_inc(q["taken"], 1)

        @block.vector
        def _(dve):
            chain = Chain(dve, q["chain"])
            link = chain.link
            v = nc.vector

            def settle(ins):
                link(ins)
                v.memset(pause[:], 0.0)
            with dve.Fori(0, NCH) as t:
                chain.enter(t, LINKS)
                dve.wait_ge(q["sc_ready"], t + 1)
                v.memset(pause[:], 0.0)
                for vals, n, best, at in ((sc, KT, v1, i1), (cand, 8, v2, i2)):
                    if n == 8:
                        settle(v.tensor_tensor(cand[:].rearrange("p h (i j) -> p h i j", i=TOPK),
                                             v1[:, 0:KT:2].unsqueeze(3).broadcast_to([P, 8, TOPK, TOPK]),
                                             v1[:, 1:KT:2].unsqueeze(2).broadcast_to([P, 8, TOPK, TOPK]), ALU.add))
                    for r in (0, 1):
                        o = slice(8 * r, 8 * r + 8)
                        for k in range(n):
                            ins = v.max(best[:, k, o], vals[:, k])
                        settle(ins)
                        for k in range(n):
                            ins = v.max_index(at[:, k, o], best[:, k, o], vals[:, k])
                        if r == 0:
                            settle(ins)
                            for k in range(n):
                                ins = v.match_replace(vals[:, k], best[:, k, o], vals[:, k], LOWEST)
                        settle(ins)
                v.tensor_scalar(ia[:], i2[:], 4, None, ALU.logical_shift_right)
                v.tensor_scalar(ib[:], i2[:], 15, None, ALU.bitwise_and)
                link(v.tensor_copy(f1[:], i1[:]))
                v.tensor_copy(fa[:], ia[:])
                link(v.tensor_copy(fb[:], ib[:]))
                steps = consts[:, C_IOTA:C_IOTA + TOPK].unsqueeze(1).broadcast_to([P, 128, TOPK])
                for place_, half, key in ((fa, 0, row), (fb, 1, col)):
                    pk = pick[:].rearrange("p h (k n) -> p (h k) n", k=TOPK)
                    link(v.tensor_tensor(pk, place_[:].rearrange("p h k -> p (h k)").unsqueeze(2).broadcast_to([P, 128, TOPK]), steps, ALU.is_equal))
                    p4 = pick[:].rearrange("p h (k n) -> p h k n", k=TOPK)
                    link(v.tensor_tensor(p4, p4, f1[:, half:KT:2].unsqueeze(2).broadcast_to([P, 8, TOPK, TOPK]), ALU.mult))
                    ins = v.tensor_reduce(key[:].rearrange("p h k -> p (h k)"), pk, AX_X, ALU.add)
                    if half == 0:
                        link(ins)
                link(v.tensor_copy(rs[:], v2[:, :, 0]))
                v.tensor_tensor(v2[:], v2[:], rs[:].unsqueeze(2).broadcast_to([P, 8, TOPK]), ALU.subtract).then_inc(q["dif"], 1)
                dve.wait_ge(q["exped"], t + 1)
                link(v.tensor_reduce(sm[:], ex[:], AX_X, ALU.add))
                link(v.reciprocal(rs[:], sm[:]))
                v.tensor_tensor(gate[:], ex[:], rs[:].unsqueeze(2).broadcast_to([P, 8, TOPK]), ALU.mult).then_inc(q["slots_ready"], 1)
                dve.wait_ge(q["taken"], t + 1)
                assert chain.n == LINKS, chain.n

    TC = 32
    place = region(m["WR"] + used, m["W_SIZE"] - used)
    hot_r = place("hot_r", [2, 4, P])
    hot_c = place("hot_c", [2, 4, P])
    table = [place(f"table{i}", [NGRP, TC, GRP]) for i in (0, 1)]
    names = "rows cols dense out stored0 stored1".split()
    q = {n: sem("gt_" + n) for n in names}
    stored = [q["stored0"], q["stored1"]]
    iota = consts[:, C_IOTA:C_IOTA + P]
    with nc.Block() as block:
        def quads(eng, body):
            with eng.Fori(0, 8) as c:
                for s in (0, 1):
                    with eng.Fori(0, 4) as k:
                        for r in (0, 1):
                            body(c * 16 + k * 2 + (8 * s + r), k * 2 + r, r, c, s)
                    yield c, s
            with eng.Fori(0, 4) as k:
                for r in (0, 1):
                    body(k * 2 + (128 + r), k * 2 + r, r, 8, 0)
            yield 8, 0

        @block.vector
        def _(dve):
            def body(n, k, r, c, s):
                dve.wait_ge(q["dense"], n - r)
                for i in range(4):
                    at = bass.ds(n * 4 + i, 1)
                    ins = nc.vector.tensor_scalar(hot_r[:, r, i], iota, rowT[:, at], gateT[:, at], ALU.is_equal, ALU.mult)
                ins.then_inc(q["rows"], 1)
                nc.vector.tensor_tensor(hot_c[:, r], iota.unsqueeze(1).broadcast_to([P, 4, P]),
                                        colT[:, bass.ds(n * 4, 4)].unsqueeze(2).broadcast_to([P, 4, P]), ALU.is_equal).then_inc(q["cols"], 1)
            for _ in quads(dve, body):
                pass

        @block.tensor
        def _(pe):
            def body(n, k, r, c, s):
                pe.wait_ge(q["rows"], n + 1)
                pe.wait_ge(q["cols"], n + 1)
                pe.wait_ge(q["out"], n - r)
                for i in range(4):
                    ins = nc.tensor.matmul(pm[:, r, 0, i * P:(i + 1) * P], hot_c[:, r, i], hot_r[:, r, i], start=True, stop=True)
                ins.then_inc(q["dense"], 1)
            for _ in quads(pe, body):
                pass

        @block.scalar
        def _(act):
            def body(n, k, r, c, s):
                act.wait_ge(q["dense"], n + 1)
                act.wait_ge(stored[s], 16 * c)
                out = table[s][:, :, bass.ds(k * 4, 4), :]
                nc.scalar.copy(out.rearrange("p g t i -> p t g i"), pm[:, r, 0].rearrange("p (t g i) -> p t g i", t=4, g=NGRP)).then_inc(q["out"], 1)
            for _ in quads(act, body):
                pass

        @block.sync
        def _(sp):
            def store(c, s):
                sp.wait_ge(q["out"], c * 16 + (8 * s + 8))
                sp.dma_start(gate_s[:, :, bass.ds(c * (2 * TC * GRP) + s * TC * GRP, TC * GRP)].rearrange("g p n -> p g n"),
                             table[s][:].rearrange("p g t i -> p g (t i)")).then_inc(stored[s], 16)
            with sp.Fori(0, 8) as c:
                for s in (0, 1):
                    store(c, s)
            store(8, 0)
            sp.wait_ge(stored[0], 16 * 9)
            sp.wait_ge(stored[1], 16 * 8)


def _tiles(a):
    n, m = a.shape
    return np.ascontiguousarray(a.reshape(n // P, P, m).transpose(1, 0, 2))


def _units(w):
    n = w.shape[1] // P
    return w.reshape(KT, P, n, P).transpose(2, 1, 0, 3).reshape(n, P, KT * P)


def kernel(**inputs):
    import concourse.bacc as bacc
    from concourse.bass_utils import run_bass_kernel_spmd

    g = {k: np.asarray(v) for k, v in inputs.items()}
    w_in = g["w_in"][0]
    units = np.zeros((UNITS, P, KT * P), np.float32)
    units[MK0:MV0] = _units(g["w_mk"][0])
    units[MV0:Z0] = _units(g["w_mv"][0])
    units[Z0:POOL0] = _units(w_in[:, 4112:])
    units[POOL0:AB0] = _units(w_in[:, :4096])
    ab = np.zeros((D, P), np.float32)
    ab[:, :16] = w_in[:, 4096:4112]
    units[AB0:OUT0] = _units(ab)
    units[OUT0:MQ0] = _units(g["w_out"][0])
    units[MQ0:MO0] = _units(g["w_mq"][0])
    units[MO0:PQ0] = _units(g["w_mo"][0])
    units[PQ0:EXP0] = _units(g["w_pq"][0])
    ex = units[EXP0:].reshape(NGRP, 2, GRP, P, KT * P)
    ex[:, 0] = g["u_experts"][0].reshape(NGRP, GRP, P, KT, P).transpose(0, 1, 4, 3, 2).reshape(NGRP, GRP, P, KT * P)
    ex[:, 1] = g["v_experts"][0].reshape(NGRP, GRP, P, 4, 4, P).transpose(0, 3, 2, 4, 1, 5).reshape(NGRP, 4, P, KT * P)
    vecs = np.zeros((P, NV), np.float32)
    for at, name in ((V_MIX, "norm_mix"), (V_XATTN, "norm_xattn"), (V_MEM, "norm_mem"), (V_FFN, "norm_ffn"), (V_FINAL, "norm_final")):
        vecs[:, at:at + KT] = g[name].reshape(KT, P).T
    vecs[:, V_POOL:V_POOL + 8] = g["pool_scale"].reshape(8, P).T
    vecs[:, V_CONV:V_CONV + 96] = g["conv_w"][0].reshape(4, 24, P).transpose(2, 1, 0).reshape(P, 96)
    vecs[:, V_DN] = g["norm_dn"][0]
    vecs[:, V_EPS] = EPS
    vecs[:, V_ALOG:V_ALOG + 8] = g["a_log"][0]
    vecs[:, V_DT:V_DT + 8] = g["dt_bias"][0]
    ins = {
        "units": units,
        "consts": constants(),
        "vecs": vecs,
        "xT": _tiles(np.concatenate([g["x_prompt"][0], g["x_sample"][0]], 0).T),
        "memT": _tiles(g["mem_prompt"][0].T),
        "phist": _tiles(g["cache_pool"][0, 0].T),
        "chist": _tiles(g["cache_conv"][0, 0].T),
        "wpool": np.ascontiguousarray(g["w_pool"][0].reshape(4, 2, P, 2, P).transpose(2, 0, 1, 3, 4).reshape(P, KT, P)),
        "state": np.ascontiguousarray(g["state_dn"][0, 0]),
        "mkT_sample": np.ascontiguousarray(g["cache_mem_k"][0, 0].reshape(M, D).T.reshape(KT, P, M)),
        "mv_sample": _tiles(g["cache_mem_v"][0, 0].reshape(M, D)),
        "keys": np.ascontiguousarray(g["sub_keys"][0].transpose(3, 0, 1, 2).reshape(P, KT, P)),
    }
    outs = {
        "yT": (KT, P, T), "pool_new": (P, 8, 2, 15), "conv_new": (P, 24, 2, 3), "dn_prompt": (8, P, P),
        "dn_sample": (8, P, P), "mkT": (KT, P, M), "mv": (P, 2, D),
    }
    nc = bacc.Bacc("TRN2", target_bir_lowering=False, num_devices=1)
    a = {k: nc.dram_tensor(k, v.shape, F32, kind="ExternalInput").ap() for k, v in ins.items()}
    a.update({k: nc.dram_tensor(k, s, F32, kind="ExternalOutput").ap() for k, s in outs.items()})
    build(nc, a)
    r = run_bass_kernel_spmd(nc, [ins], core_ids=[0]).results[0]
    y = r["yT"].reshape(D, T).T
    hist = lambda v, n: np.ascontiguousarray(v.transpose(2, 3, 1, 0)).reshape(2, 1, 1, n, -1)
    pool, conv = hist(r["pool_new"], 15), hist(r["conv_new"], 3)
    mk = np.ascontiguousarray(r["mkT"].reshape(D, M).T).reshape(1, 1, M, 4, 512)
    mv = np.ascontiguousarray(r["mv"].transpose(1, 0, 2)).reshape(1, 1, M, 4, 512)
    return (np.ascontiguousarray(y[:TP])[None], np.ascontiguousarray(y[TP:])[None],
            pool[0], conv[0], r["dn_prompt"][None, None], mk, mv,
            pool[1], conv[1], r["dn_sample"][None, None])
```

```python
from contextlib import ExitStack

import numpy as np

import concourse.bass as bass
from concourse import mybir

F32 = mybir.dt.float32
F32R = mybir.dt.float32r
U32 = mybir.dt.uint32
ALU = mybir.AluOpType
ACT = mybir.ActivationFunctionType
AX_X = mybir.AxisListType.X

P = 128
D = 2048
KT = D // P
TP, TS = 512, 32
T = TP + TS
HALF = T // 2
NCH = 5
TPAD = NCH * P
M = 256
EPS = 1e-6
HEADS = 8
LEVELS = 7
MH, MHT = 4, 4
MEM_SCALE = float(MHT * P) ** -0.5
SLOTS = 128
TOPK = 16
GRP = 4
NGRP = P // GRP
LOWEST = -3.0e38
PRIME = 1

MK0 = 0
MV0 = MK0 + KT
Z0 = MV0 + KT
POOL0 = Z0 + 8
QKV0 = POOL0 + 8
AB0 = QKV0 + 24
OUT0 = AB0 + 1
MQ0 = OUT0 + KT
MO0 = MQ0 + KT
PQ0 = MO0 + KT
EXP0 = PQ0 + KT
UNITS = EXP0 + 2 * P

V_MIX, V_XATTN, V_MEM, V_FFN, V_FINAL = (16 * i for i in range(5))
V_POOL = 80
V_CONV = V_POOL + 8
V_DN = V_CONV + 96
V_EPS = V_DN + 1
V_ALOG = V_EPS + 1
V_DT = V_ALOG + 8
NV = V_DT + 8

C_ID = 0
C_ONE = C_ID + P
C_CUM = C_ONE + P
C_LEV = C_CUM + P
C_IOTA = C_LEV + LEVELS * P
C_CNT = C_IOTA + P
C_VALID = C_CNT + 64
NC = C_VALID + NCH * HEADS


def constants():
    c = np.zeros((P, NC), np.float32)
    r = np.arange(P)
    c[:, C_ID:C_ID + P] = np.eye(P)
    c[:, C_ONE:C_ONE + P] = 1.0
    c[:, C_CUM:C_CUM + P] = r[:, None] <= r[None, :]
    for l in range(LEVELS):
        s = 1 << l
        same = (r[:, None] // (2 * s)) == (r[None, :] // (2 * s))
        c[:, C_LEV + l * P:C_LEV + (l + 1) * P] = same & ((r[:, None] // s) % 2 == 1) & ((r[None, :] // s) % 2 == 0)
    c[:, C_IOTA:C_IOTA + P] = r[None, :]
    for g in range(4):
        c[:, C_CNT + 16 * g:C_CNT + 16 * g + 16] = 1.0 / np.minimum(np.arange(16) + 1, 2 << g)
    v = np.ones((P, NCH, HEADS), np.float32)
    v[TS:, NCH - 1] = 0.0
    c[:, C_VALID:NC] = v.reshape(P, -1)
    return c


class Chain:

    def __init__(self, eng, sem):
        self.eng, self.sem, self.base, self.n = eng, sem, 0, 0

    def link(self, ins):
        ins.then_inc(self.sem, 1)
        self.n += 1
        self.eng.wait_ge(self.sem, self.base + self.n)

    def enter(self, i, per):
        self.start, self.per = self.base + self.n, per
        self.base, self.n = self.start + i * per, 0

    def leave(self, count):
        assert self.n == self.per, (self.n, self.per)
        self.base, self.n = self.start + count * self.per, 0


def build(nc, a):
    es = ExitStack()

    def sem(name):
        return es.enter_context(nc.semaphore(name))

    primed = {n: sem(n) for n in (
        "tiles_done v_stored scaled_lo0 scaled_lo1 y_stored0 y_stored1 k_stored0 k_stored1 conv_done hist_kept "
        "qkv_stored0 qkv_stored1 silu_done q_stored0 q_stored1 cat_done scores sc_copied slots_ready dense table_ready "
        "table_stored0 table_stored1 h_stored0 h_stored1 squares_summed coefs_used").split()}

    start = -(-nc.sbuf_base // 64) * 64

    def region(offset, size):
        at = [offset]

        def place(name, free, dtype=F32):
            t = nc.alloc_sbuf_tensor_at(name, [P] + list(free), dtype, offset=at[0])
            at[0] += 4 * int(np.prod(free))
            at[0] = -(-at[0] // 32) * 32
            assert at[0] <= offset + size, (name, at[0] - offset - size)
            return t
        return place

    XR = start
    HR = XR + 4 * KT * T
    RR = HR + 8 * KT * T
    CR = RR + 6 * 4 * KT * P
    WR = -(-(CR + 4 * (NC + NV + 2 * NCH * HEADS) + 128) // 64) * 64
    W_SIZE = nc.sbuf_usable_end - WR
    NR_SIZE = 8 * 4 * T
    NR = (nc.sbuf_usable_end - NR_SIZE) // 64 * 64
    H_SIZE = 8 * KT * T

    place = region(RR, CR - RR)
    raw = place("raw", [2, KT, P])
    whi = place("whi", [2, KT, P], F32R)
    wlo = place("wlo", [2, KT, P], F32R)
    place = region(CR, WR - CR)
    consts = place("consts", [NC])
    vecs = place("vecs", [NV])
    gcol = place("gcol", [NCH * HEADS])
    beta = place("beta", [NCH * HEADS])
    place = region(XR, HR - XR)
    x = place("x", [KT, T])
    place = region(XR, HR - XR)
    cat = place("cat", [KT, T])
    place = region(XR, HR - XR)
    mem = place("mem", [KT, M])
    place = region(HR, H_SIZE)
    xhi = place("xhi", [KT, T], F32R)
    xlo = place("xlo", [KT, T], F32R)
    place = region(HR, H_SIZE)
    memhi = place("memhi", [KT, M], F32R)
    memlo = place("memlo", [KT, M], F32R)

    pu = es.enter_context(nc.psum_tensor("pu", [P, 2, 2, 512], F32))
    pm = es.enter_context(nc.psum_tensor("pm", [P, 2, 2, 512], F32))
    SLOT = [t[:, s].rearrange("p b n -> p (b n)") for t in (pu, pm) for s in (0, 1)]

    ident = consts[:, C_ID:C_ID + P]
    ones = consts[:, C_ONE:C_ONE + P]
    cum = consts[:, C_CUM:C_CUM + P]

    qkv_s = nc.dram_tensor("qkv_s", (24, P, TPAD), F32, kind="Internal").ap()
    q_s = nc.dram_tensor("q_s", (KT, P, TPAD), F32, kind="Internal").ap()
    gate_s = nc.dram_tensor("gate_s", (NGRP, P, T * GRP), F32, kind="Internal").ap()

    raw_loaded = [sem("raw_loaded0"), sem("raw_loaded1")]
    hi_ready = sem("hi_ready")
    lo_ready = sem("lo_ready")
    tiles_done = primed["tiles_done"]
    psum_free = sem("psum_free")

    def finished(eng, n):
        eng.wait_ge(tiles_done, n + PRIME)

    def taken(eng, tile):
        eng.wait_ge(psum_free, tile + 3)

    def unit(base, i, s):
        return base + s + 2 * i, (base + s) % 2, i + (base + s) // 2 + 1

    def load_unit(sp, u, slot):
        sp.wait_ge(lo_ready, u - 1)
        sp.dma_start(raw[:, slot].rearrange("p k n -> p (k n)"), a["units"][bass.ds(u, 1)].rearrange("a p n -> (a p) n")).then_inc(raw_loaded[slot], 16)

    def split_hi(act, slot, fills, done):
        act.wait_ge(raw_loaded[slot], 16 * fills)
        finished(act, done)
        nc.scalar.copy(whi[:, slot], raw[:, slot]).then_inc(hi_ready, 1)

    def split_lo(eng, u, slot, how=None):
        eng.wait_ge(hi_ready, u + 1)
        (how or nc.vector).tensor_tensor(wlo[:, slot], raw[:, slot], whi[:, slot].bitcast(F32), ALU.subtract).then_inc(lo_ready, 1)

    def products(outs, terms, first=True, last=True, before=None, after=None):
        for n, (wh, wl, xs) in enumerate(terms):
            if before:
                before(n)
            for m, w in enumerate((wh, wh, wl)):
                for b, out in enumerate(outs):
                    ins = nc.tensor.matmul(out, w, xs[b][m == 1], start=(first and n == 0 and m == 0),
                                           stop=(last and n == len(terms) - 1 and m == 2))
            if after and n < len(terms) - 1:
                after(n)
        return ins

    def halves(hi, lo, k):
        return [(hi[:, k, b * HALF:(b + 1) * HALF], lo[:, k, b * HALF:(b + 1) * HALF]) for b in (0, 1)]

    def unit_product(pe, u, slot, before=None, after=None):
        pe.wait_ge(lo_ready, u + 1)
        pe.wait_ge(psum_free, u + 1)
        products([pu[:, slot, b, 0:HALF] for b in (0, 1)],
                 [(whi[:, slot, k], wlo[:, slot, k], halves(xhi, xlo, k)) for k in range(KT)],
                 before=before, after=after).then_inc(tiles_done, 1)

    both = lambda slot: pu[:, slot, :, 0:HALF]
    in_two = lambda ap: ap.rearrange("p (b n) -> p b n", b=2)

    set_loaded = sem("set_loaded")
    mem_loaded = sem("mem_loaded")
    with nc.Block() as block:
        @block.sync
        def _(sp):
            sp.dma_start(consts[:], a["consts"]).then_inc(set_loaded, 16)
            sp.dma_start(vecs[:], a["vecs"]).then_inc(set_loaded, 16)
            sp.dma_start(mem[:], a["memT"]).then_inc(mem_loaded, 16)
            for u in (0, 1):
                sp.dma_start(raw[:, u].rearrange("p k n -> p (k n)"), a["units"][u]).then_inc(raw_loaded[u], 16)

        @block.gpsimd
        def _(pool):
            for s in primed.values():
                nc.gpsimd.engine_nop().then_inc(s, PRIME)
            nc.gpsimd.engine_nop().then_inc(psum_free, 2)

        @block.scalar
        def _(act):
            split_hi(act, 0, 1, 0)

        @block.vector
        def _(dve):
            split_lo(dve, 0, 0)
            dve.wait_ge(set_loaded, 32)
            dve.wait_ge(mem_loaded, 16)

    place = region(NR, NR_SIZE)
    sumsq = place("sumsq", [T])
    rinv = place("rinv", [T])
    squares = place("squares", [2, T])
    scaled = place("scaled", [4, T])
    squared = sem("squared")
    squares_summed = primed["squares_summed"]
    summed = sem("summed")
    ln_done = sem("ln_done")
    rinv_ready = sem("rinv_ready")
    scaled_ready = sem("scaled_ready")
    scaled_hi = sem("scaled_hi")
    scaled_lo = [primed["scaled_lo0"], primed["scaled_lo1"]]
    y_stored = [primed["y_stored0"], primed["y_stored1"]]
    counts = {"squares": 0, "norms": 0}
    row = lambda t, k: t[:, bass.ds(k, 1)].rearrange("p k n -> p (k n)")

    def clear_sum():
        with nc.Block() as block:
            @block.gpsimd
            def _(pool):
                nc.gpsimd.memset(sumsq[:], 0.0)

    def act_square(act, src, k, s, n, base):
        act.wait_ge(squares_summed, (k - s) + (base + PRIME))
        nc.scalar.activation(squares[:, s, 0:n], row(src, k), ACT.Square).then_inc(squared, 1)

    def sum_squares(eng, how, k, s, n, base):
        eng.wait_ge(squared, k + (base + 1))
        eng.wait_ge(squares_summed, k + (base + PRIME))
        how.tensor_tensor(sumsq[:, 0:n], sumsq[:, 0:n], squares[:, s, 0:n], ALU.add).then_inc(squares_summed, 1)

    def sum_pass(src, n):
        base = counts["squares"]
        counts["squares"] += KT
        clear_sum()
        with nc.Block() as block:
            @block.scalar
            def _(act):
                with act.Fori(0, KT // 2) as i:
                    for s in (0, 1):
                        act_square(act, src, 2 * i + s, s, n, base)

            @block.vector
            def _(dve):
                with dve.Fori(0, KT // 2) as i:
                    for s in (0, 1):
                        sum_squares(dve, nc.vector, 2 * i + s, s, n, base)

    class Norm:

        def __init__(self, src, gain, n, hi=None, lo=None, final=None):
            self.src, self.gain, self.n, self.hi, self.lo, self.final = src, gain, n, hi, lo, final
            self.parts = [(0, n)] if n <= 512 else [(0, HALF), (HALF, n)]
            self.run = counts["norms"]
            counts["norms"] += 1
            self.base = self.run * KT

        def pe(self, pe):
            for b, (u, v) in enumerate(self.parts):
                ins = nc.tensor.matmul(pm[:, 0, b, 0:v - u], ones, sumsq[:, u:v], start=True, stop=True)
            ins.then_inc(summed, 1)

        def tile_ready(self, pe, k):
            pe.wait_ge(scaled_lo[k % 2], self.base // 2 + k // 2 + 1 + PRIME)

        def act(self, act):
            act.wait_ge(summed, self.run + 1)
            for b, (u, v) in enumerate(self.parts):
                ins = nc.scalar.activation(rinv[:, u:v], pm[:, 0, b, 0:v - u], ACT.Ln, scale=1.0 / D, bias=vecs[:, V_EPS:V_EPS + 1])
            ins.then_inc(ln_done, 1)
            act.wait_ge(ln_done, self.run + 1)
            nc.scalar.activation(rinv[:, 0:self.n], rinv[:, 0:self.n], ACT.Exp, scale=-0.5).then_inc(rinv_ready, 1)
            if self.final is None:
                with act.Fori(0, KT // 4) as i:
                    for s in range(4):
                        act.wait_ge(scaled_ready, 4 * i + (self.base + s + 1))
                        nc.scalar.copy(row(self.hi, 4 * i + s), scaled[:, s, 0:self.n]).then_inc(scaled_hi, 1)

        def lower(self, eng, how, i, s):
            eng.wait_ge(scaled_hi, 4 * i + (self.base + s + 1))
            how.tensor_tensor(row(self.lo, 4 * i + s), scaled[:, s, 0:self.n], row(self.hi, 4 * i + s).bitcast(F32), ALU.subtract).then_inc(scaled_lo[s % 2], 1)

        def dve(self, dve):
            dve.wait_ge(rinv_ready, self.run + 1)
            with dve.Fori(0, KT // 4) as i:
                for s in range(4):
                    if self.final is None:
                        dve.wait_ge(scaled_lo[s % 2], 2 * i + (self.base // 2 + PRIME))
                    else:
                        dve.wait_ge(y_stored[s % 2], 32 * i + PRIME)
                    nc.vector.scalar_tensor_tensor(scaled[:, s, 0:self.n], row(self.src, 4 * i + s), vecs[:, bass.ds(4 * i + (s + self.gain), 1)],
                                                   rinv[:, 0:self.n], ALU.mult, ALU.mult).then_inc(scaled_ready, 1)
                if self.final is None:
                    for s in (0, 2):
                        self.lower(dve, nc.vector, i, s)

        def sp(self, sp):
            with sp.Fori(0, KT // 4) as i:
                for s in range(4):
                    sp.wait_ge(scaled_ready, 4 * i + (self.base + s + 1))
                    sp.dma_start(self.final[bass.ds(4 * i + s, 1)].rearrange("k p n -> (k p) n"), scaled[:, s, 0:self.n]).then_inc(y_stored[s % 2], 16)
            for s in (0, 1):
                sp.wait_ge(y_stored[s], 8 * KT + PRIME)

        def pool(self, pool):
            if self.final is None:
                with pool.Fori(0, KT // 4) as i:
                    for s in (1, 3):
                        self.lower(pool, nc.gpsimd, i, s)

    def layer(base, n, pe_tile, act_tile=None, dve_tile=None, sp_tile=None, pool_tile=None, norm=None, pe_first=None):
        def loop(eng, before, tile, start=0):
            with eng.Fori(start, n // 2) as i:
                for s in (0, 1):
                    u, slot, fills = unit(base, i, s)
                    before(eng, i, s)
                    if tile:
                        tile(eng, u, slot, i, s)

        with nc.Block() as block:
            @block.sync
            def _(sp):
                def before(eng, i, s):
                    u, slot, _ = unit(base, i, s + 2)
                    load_unit(eng, u, slot)
                loop(sp, before, sp_tile)

            @block.scalar
            def _(act):
                def before(eng, i, s):
                    u, slot, fills = unit(base, i, s + 1)
                    split_hi(eng, slot, fills, u - 1)
                if norm:
                    norm.act(act)
                loop(act, before, act_tile)

            @block.vector
            def _(dve):
                def before(eng, i, s):
                    u, slot, _ = unit(base, i, s + 1)
                    split_lo(eng, u, slot)
                if norm:
                    norm.dve(dve)
                loop(dve, before, dve_tile)

            @block.tensor
            def _(pe):
                nothing = lambda *_: None
                if norm:
                    norm.pe(pe)
                    for s in (0, 1):
                        u, slot, _ = unit(base, 0, s)
                        pe_first(pe, u, slot, (lambda k: norm.tile_ready(pe, k)) if s == 0 else None)
                    loop(pe, nothing, pe_tile, 1)
                else:
                    loop(pe, nothing, pe_tile)

            @block.gpsimd
            def _(pool):
                if norm:
                    norm.pool(pool)
                if pool_tile:
                    loop(pool, lambda *_: None, pool_tile)

    place = region(WR, W_SIZE)
    k_out = place("k_out", [2, M])
    v_out = place("v_out", [2, 2, 512])
    k_stored = [primed["k_stored0"], primed["k_stored1"]]
    v_stored = primed["v_stored"]
    x_loaded = sem("x_loaded")

    def pe_k(pe, u, slot, before=None):
        pe.wait_ge(lo_ready, u + 1)
        pe.wait_ge(psum_free, u + 1)
        products([pu[:, slot, 0, 0:M]],
                 [(whi[:, slot, k], wlo[:, slot, k], [(memhi[:, k], memlo[:, k])]) for k in range(KT)], before=before).then_inc(tiles_done, 1)

    def act_k(act, u, slot, i, s):
        finished(act, u + 1)
        act.wait_ge(k_stored[s], 16 * i + PRIME)
        nc.scalar.copy(k_out[:, s], pu[:, slot, 0, 0:M]).then_inc(psum_free, 1)

    def sp_k(sp, u, slot, i, s):
        taken(sp, u)
        sp.dma_start(a["mkT"][bass.ds(2 * i + s, 1)].rearrange("k p n -> (k p) n"), k_out[:, s]).then_inc(k_stored[s], 16)

    sum_pass(mem, M)
    layer(MK0, KT, lambda pe, u, slot, i, s: pe_k(pe, u, slot), act_k, None, sp_k, norm=Norm(mem, V_MEM, M, memhi, memlo), pe_first=pe_k)

    with nc.Block() as block:
        @block.sync
        def _(sp):
            for s in (0, 1):
                sp.wait_ge(k_stored[s], 16 * KT // 2 + PRIME)
            sp.dma_start(x[:], a["xT"]).then_inc(x_loaded, 16)
            with sp.Fori(0, 2) as i:
                for r in (0, 1):
                    for j in range(4):
                        load_unit(sp, i * 8 + (MV0 + 4 * r + j + 2), (MV0 + j) % 2)
                    taken(sp, i * 8 + (MV0 + 4 * r + 3))
                    sp.dma_start(a["mv"][:, :, bass.ds(i * 1024 + 512 * r, 512)], v_out[:, r]).then_inc(v_stored, 16)
            sp.wait_ge(v_stored, 16 * 4 + PRIME)
            sp.wait_ge(x_loaded, 16)

        @block.tensor
        def _(pe):
            with pe.Fori(0, 2) as i:
                for r in (0, 1):
                    pe.wait_ge(psum_free, i * 8 + (MV0 + 4 * r - 2))
                    for j in range(4):
                        slot = (MV0 + j) % 2
                        pe.wait_ge(lo_ready, i * 8 + (MV0 + 4 * r + j + 1))
                        for b in (0, 1):
                            at = slice(b * P, (b + 1) * P)
                            wide = lambda w: w[:, slot].rearrange("p k n -> p (k n)").rearrange("p (k n) -> p k n", k=4)
                            ins = products([pu[:, r, b]],
                                           [(memhi[:, 4 * j + k, at], memlo[:, 4 * j + k, at], [(wide(whi)[:, k], wide(wlo)[:, k])]) for k in range(4)],
                                           first=(j == 0), last=(j == 3))
                        ins.then_inc(tiles_done, 1)

        @block.scalar
        def _(act):
            with act.Fori(0, 2) as i:
                for r in (0, 1):
                    for j in range(4):
                        c = 4 * r + j
                        split_hi(act, (MV0 + j + 1) % 2, i * 4 + ((MV0 + c + 1) // 2 + 1), i * 8 + (MV0 + c))
                    finished(act, i * 8 + (MV0 + 4 * r + 4))
                    if r == 0:
                        act.wait_ge(v_stored, 32 * i + PRIME)
                    nc.scalar.copy(v_out[:, r], pu[:, r]).then_inc(psum_free, 4)

        @block.vector
        def _(dve):
            with dve.Fori(0, 2) as i:
                for c in range(8):
                    split_lo(dve, i * 8 + (MV0 + c + 1), (MV0 + c + 1) % 2)

    sum_pass(x, T)
    norm_mix = Norm(x, V_MIX, T, xhi, xlo)

    place = region(WR, W_SIZE)
    CL = 3 + TP + 3 + TS
    ext = place("ext", [2, CL])
    acc = [place(f"acc{i}", [CL - 3]) for i in range(4)]
    convd = place("convd", [2, TPAD])
    chist = place("chist", [24, 3])
    conv_new = place("conv_new", [24, 2, 3])
    PH = 15
    PL = PH + TP + PH + TS
    phist = place("phist", [8, PH])
    pool_new = place("pool_new", [8, 2, PH])
    pext = place("pext", [2, PL])
    wins = [place(f"win{i}", [PL]) for i in range(2)]
    mixes = [place(f"mix{i}", [2, T]) for i in (0, 1)]
    wpool = place("wpool", [KT, P])
    abT = place("abT", [TPAD])

    def act_z(act, u, slot, i, s):
        finished(act, u + 1)
        nc.scalar.activation(cat[:, bass.ds(2 * i + s + 8, 1)].rearrange("p k (b n) -> p (k b) n", b=2), both(slot), ACT.Silu).then_inc(psum_free, 1)

    pe_linear = lambda pe, u, slot, i, s: unit_product(pe, u, slot)
    layer(Z0, 8, pe_linear, act_z, norm=norm_mix, pe_first=unit_product)

    pool_loaded = sem("pool_loaded")
    pext_used = sem("pext_used")
    mix_ready = sem("mix_ready")
    mixed = sem("mixed")
    mixed_out = sem("mixed_out")
    pool_chain = sem("pool_chain")
    pool_stored = sem("pool_stored")
    with nc.Block() as block:
        @block.sync
        def _(sp):
            sp.dma_start(phist[:], a["phist"]).then_inc(pool_loaded, 16)
            sp.dma_start(chist[:], a["chist"]).then_inc(pool_loaded, 16)
            sp.dma_start(wpool[:], a["wpool"]).then_inc(pool_loaded, 16)
            sp.wait_ge(pool_loaded, 48)

        @block.gpsimd
        def _(pool):
            nc.gpsimd.memset(pext[:], 0.0)
            nc.gpsimd.memset(ext[:], 0.0)
            nc.gpsimd.memset(convd[:], 0.0)
            nc.gpsimd.memset(abT[:], 0.0)

    with nc.Block() as block:
        S0 = PH + TP + PH

        @block.sync
        def _(sp):
            with sp.Fori(0, 4) as i:
                for s in (0, 1):
                    u, slot, _ = unit(POOL0, i, s + 2)
                    load_unit(sp, u, slot)
            sp.wait_ge(pext_used, 8)
            sp.dma_start(a["pool_new"], pool_new[:]).then_inc(pool_stored, 16)
            sp.wait_ge(pool_stored, 16)

        @block.tensor
        def _(pe):
            for g in range(5):
                if g < 4:
                    for s in (0, 1):
                        u, slot, _ = unit(POOL0, g, s)
                        unit_product(pe, u, slot)
                g -= 1
                if g < 0:
                    continue
                pe.wait_ge(mix_ready, 2 * g + 2)
                for d in (0, 1):
                    if g:
                        pe.wait_ge(mixed_out, 2 * (g - 1) + d + 1)
                    for b in (0, 1):
                        for c in (0, 1):
                            ins = nc.tensor.matmul(pm[:, d, b, 0:HALF], wpool[:, 4 * g + 2 * c + d], mixes[g % 2][:, c, b * HALF:(b + 1) * HALF],
                                                   start=(c == 0), stop=(c == 1))
                    ins.then_inc(mixed, 1)

        @block.scalar
        def _(act):
            for g in range(5):
                for s in (0, 1) if g < 4 else ():
                    j = 2 * g + s
                    u, slot, fills = unit(POOL0, g, s + 1)
                    split_hi(act, slot, fills, u - 1)
                    u, slot, _ = unit(POOL0, g, s)
                    finished(act, u + 1)
                    if g:
                        act.wait_ge(pext_used, j - 1)
                    nc.scalar.copy(pext[:, s, PH:PH + HALF], pu[:, slot, 0, 0:HALF])
                    nc.scalar.copy(pext[:, s, PH + HALF:PH + TP], pu[:, slot, 1, 0:TP - HALF])
                    nc.scalar.copy(pext[:, s, S0 - PH:S0], phist[:, j])
                    nc.scalar.copy(pext[:, s, S0:PL], pu[:, slot, 1, TP - HALF:HALF]).then_inc(psum_free, 1)
                g -= 1
                for d in (0, 1) if g >= 0 else ():
                    act.wait_ge(mixed, 2 * g + d + 1)
                    nc.scalar.activation(in_two(cat[:, 2 * g + d]), pm[:, d, :, 0:HALF], ACT.Copy, scale=vecs[:, V_POOL + 2 * g + d:V_POOL + 2 * g + d + 1]).then_inc(mixed_out, 1)

        @block.vector
        def _(dve):
            chain = Chain(dve, pool_chain)
            for g in range(4):
                for s in (0, 1):
                    j = 2 * g + s
                    u, slot, _ = unit(POOL0, g, s + 1)
                    split_lo(dve, u, slot)
                    taken(dve, POOL0 + j)
                    e = pext[:, s]
                    cur = e
                    for l in range(g + 1):
                        sh = 1 << l
                        nxt = wins[l % 2]
                        chain.link(nc.vector.tensor_tensor(nxt[:, 2 * sh - 1:PL], cur[:, 2 * sh - 1:PL], cur[:, sh - 1:PL - sh], ALU.add))
                        cur = nxt
                    if g >= 2:
                        dve.wait_ge(mixed, 2 * g - 2)
                    w = 2 << g
                    chain.link(nc.vector.tensor_tensor(wins[(g + 1) % 2][:, 0:16], cur[:, PH:PH + 16], consts[:, C_CNT + 16 * g:C_CNT + 16 * g + 16], ALU.mult))
                    nc.vector.tensor_tensor(mixes[g % 2][:, s, 0:16], wins[(g + 1) % 2][:, 0:16], e[:, PH:PH + 16], ALU.subtract)
                    nc.vector.scalar_tensor_tensor(mixes[g % 2][:, s, 16:TP], cur[:, PH + 16:PH + TP], 1.0 / w, e[:, PH + 16:PH + TP], ALU.mult, ALU.subtract)
                    nc.vector.scalar_tensor_tensor(mixes[g % 2][:, s, TP:T], cur[:, S0:PL], 1.0 / w, e[:, S0:PL], ALU.mult, ALU.subtract).then_inc(mix_ready, 1)
                    nc.vector.tensor_copy(pool_new[:, j, 0], e[:, TP:TP + PH])
                    nc.vector.tensor_copy(pool_new[:, j, 1], e[:, PL - PH:PL]).then_inc(pext_used, 1)
                    dve.wait_ge(pext_used, j + 1)

    conv_done = primed["conv_done"]
    silu_done = primed["silu_done"]
    qkv_stored = [primed["qkv_stored0"], primed["qkv_stored1"]]
    conv_chain = sem("conv_chain")
    hist_kept = primed["hist_kept"]
    conv_stored = sem("conv_stored")

    def act_qkv(act, u, slot, i, s):
        j = 2 * i + s
        finished(act, u + 1)
        act.wait_ge(conv_done, 2 * i + PRIME)
        act.wait_ge(hist_kept, 2 * i + PRIME)
        nc.scalar.copy(ext[:, s, 3:3 + HALF], pu[:, slot, 0, 0:HALF])
        nc.scalar.copy(ext[:, s, 3 + HALF:3 + TP], pu[:, slot, 1, 0:TP - HALF])
        nc.scalar.copy(ext[:, s, 3 + TP:6 + TP], chist[:, bass.ds(j, 1)].rearrange("p j n -> p (j n)"))
        nc.scalar.copy(ext[:, s, 6 + TP:CL], pu[:, slot, 1, TP - HALF:HALF]).then_inc(psum_free, 1)
        act.wait_ge(conv_done, j + (1 + PRIME))
        act.wait_ge(qkv_stored[s], 16 * i + PRIME)
        nc.scalar.activation(convd[:, s, 0:TP], acc[3][:, 0:TP], ACT.Silu)
        nc.scalar.activation(convd[:, s, TP:T], acc[3][:, TP + 3:TP + 3 + TS], ACT.Silu).then_inc(silu_done, 1)

    def pool_qkv(pool, u, slot, i, s):
        j = 2 * i + s
        taken(pool, u)
        at = bass.ds(j, 1)
        nc.gpsimd.tensor_copy(conv_new[:, at, 0].rearrange("p j n -> p (j n)"), ext[:, s, TP:TP + 3])
        nc.gpsimd.tensor_copy(conv_new[:, at, 1].rearrange("p j n -> p (j n)"), ext[:, s, CL - 3:CL]).then_inc(hist_kept, 1)

    def sp_qkv(sp, u, slot, i, s):
        sp.wait_ge(silu_done, 2 * i + (s + 1 + PRIME))
        sp.dma_start(qkv_s[bass.ds(2 * i + s, 1)].rearrange("k p n -> (k p) n"), convd[:, s]).then_inc(qkv_stored[s], 16)

    chains = {}

    def dve_qkv(dve, u, slot, i, s):
        j = 2 * i + s
        if s == 0:
            chains["conv"] = Chain(dve, conv_chain)
            chains["conv"].enter(i, 6)
        link = chains["conv"].link
        taken(dve, u)
        n = CL - 3
        tap = lambda q: vecs[:, bass.ds(j * 4 + (V_CONV + q), 1)]
        dve.wait_ge(silu_done, j + PRIME)
        link(nc.vector.tensor_scalar(acc[0][:], ext[:, s, 0:n], tap(0), None, ALU.mult))
        link(nc.vector.scalar_tensor_tensor(acc[1][:], ext[:, s, 1:1 + n], tap(1), acc[0][:], ALU.mult, ALU.add))
        link(nc.vector.scalar_tensor_tensor(acc[2][:], ext[:, s, 2:2 + n], tap(2), acc[1][:], ALU.mult, ALU.add))
        nc.vector.scalar_tensor_tensor(acc[3][:], ext[:, s, 3:3 + n], tap(3), acc[2][:], ALU.mult, ALU.add).then_inc(conv_done, 1)

    layer(QKV0, 24, pe_linear, act_qkv, dve_qkv, sp_qkv, pool_qkv)

    ab_turned = sem("ab_turned")
    g_act = sem("g_act")
    g_chain = sem("g_chain")
    place = region(NR, 2048)
    NG = NCH * HEADS
    ab = place("ab", [NCH, 16])
    gt = [place(f"gt{i}", [NG]) for i in range(6)]
    with nc.Block() as block:
        @block.sync
        def _(sp):
            for s in (0, 1):
                sp.wait_ge(qkv_stored[s], 16 * 12 + PRIME)
            sp.dma_start(a["conv_new"], conv_new[:]).then_inc(conv_stored, 16)
            load_unit(sp, AB0 + 2, AB0 % 2)
            sp.wait_ge(conv_stored, 16)

        @block.tensor
        def _(pe):
            unit_product(pe, AB0, AB0 % 2)
            taken(pe, AB0)
            for c in range(NCH):
                ins = nc.tensor.transpose(pm[:, 0, 0, 16 * c:16 * c + 16], abT[0:16, c * P:(c + 1) * P], ident[0:16, 0:16])
            ins.then_inc(ab_turned, 1)

        @block.scalar
        def _(act):
            split_hi(act, (AB0 + 1) % 2, (AB0 + 1) // 2 + 1, AB0)
            finished(act, AB0 + 1)
            for b in (0, 1):
                ins = nc.scalar.copy(abT[0:16, b * HALF:(b + 1) * HALF], pu[0:16, AB0 % 2, b, 0:HALF])
            ins.then_inc(psum_free, 1)
            act.wait_ge(g_chain, 4)
            nc.scalar.activation(gt[2][:], gt[1][:], ACT.Exp).then_inc(g_act, 1)
            act.wait_ge(g_act, 1)
            nc.scalar.activation(gt[3][:], gt[2][:], ACT.Ln, bias=1.0).then_inc(g_act, 1)
            nc.scalar.activation(gt[5][:, 0:HEADS], vecs[:, V_ALOG:V_ALOG + HEADS], ACT.Exp)
            nc.scalar.activation(beta[:].rearrange("p (c h) -> p c h", c=NCH), ab[:, :, 8:16], ACT.Sigmoid).then_inc(g_act, 1)

        @block.vector
        def _(dve):
            chain = Chain(dve, g_chain)
            split_lo(dve, AB0 + 1, (AB0 + 1) % 2)
            v3 = lambda t: t[:].rearrange("p (c h) -> p c h", c=NCH)
            dve.wait_ge(ab_turned, 1)
            chain.link(nc.vector.tensor_copy(ab[:], pm[:, 0, 0, 0:16 * NCH].rearrange("p (c n) -> p c n", c=NCH)))
            chain.link(nc.vector.tensor_tensor(v3(gt[0]), ab[:, :, 0:8], vecs[:, V_DT:V_DT + 8].unsqueeze(1).broadcast_to([P, NCH, 8]), ALU.add))
            chain.link(nc.vector.tensor_scalar(gt[4][:], gt[0][:], -1.0, None, ALU.mult))
            chain.link(nc.vector.tensor_tensor(gt[1][:], gt[0][:], gt[4][:], ALU.min))
            dve.wait_ge(g_act, 3)
            chain.link(nc.vector.scalar_tensor_tensor(gt[4][:], gt[0][:], 0.0, gt[3][:], ALU.max, ALU.add))
            chain.link(nc.vector.scalar_tensor_tensor(v3(gt[0]), v3(gt[4]), -1.0, gt[5][:, 0:8].unsqueeze(1).broadcast_to([P, NCH, 8]), ALU.mult, ALU.mult))
            valid = consts[:, C_VALID:C_VALID + NG]
            nc.vector.tensor_tensor(gcol[:], gt[0][:], valid, ALU.mult)
            chain.link(nc.vector.tensor_tensor(gt[1][:], beta[:], valid, ALU.mult))
            chain.link(nc.vector.tensor_copy(beta[:], gt[1][:]))

    deltanet(nc, es, sem, region, a, dict(
        HR=HR, H_SIZE=H_SIZE, WR=WR, W_SIZE=W_SIZE, consts=consts, vecs=vecs, gcol=gcol, beta=beta, cat=cat,
        SLOT=SLOT, qkv_s=qkv_s, ident=ident, ones=ones, cum=cum, cat_done=primed["cat_done"]))

    cat_hi = sem("cat_hi")
    x_back = sem("x_back")
    cat_lo = sem("cat_lo")
    with nc.Block() as block:
        @block.scalar
        def _(act):
            with act.Fori(0, KT) as k:
                nc.scalar.copy(xhi[:, bass.ds(k, 1)], cat[:, bass.ds(k, 1)]).then_inc(cat_hi, 1)

        @block.vector
        def _(dve):
            with dve.Fori(0, KT) as k:
                at = bass.ds(k, 1)
                dve.wait_ge(cat_hi, k + 1)
                nc.vector.tensor_tensor(xlo[:, at], cat[:, at], xhi[:, at].bitcast(F32), ALU.subtract).then_inc(cat_lo, 1)

        @block.sync
        def _(sp):
            sp.wait_ge(cat_lo, KT)
            sp.dma_start(x[:], a["xT"]).then_inc(x_back, 16)
            sp.wait_ge(x_back, 16)

    def residual_layer(base):
        before = counts["squares"]
        counts["squares"] += KT
        clear_sum()

        def dve_residual(dve, u, slot, i, s):
            finished(dve, u + 1)
            at = x[:, bass.ds(2 * i + s, 1)].rearrange("p k (b n) -> p (k b) n", b=2)
            nc.vector.tensor_tensor(at, both(slot), at, ALU.add).then_inc(psum_free, 1)

        def act_residual(act, u, slot, i, s):
            taken(act, u)
            act_square(act, x, 2 * i + s, s, T, before)

        def pool_residual(pool, u, slot, i, s):
            sum_squares(pool, nc.gpsimd, 2 * i + s, s, T, before)

        layer(base, KT, pe_linear, act_residual, dve_residual, None, pool_residual)

    residual_layer(OUT0)

    q_stored = [primed["q_stored0"], primed["q_stored1"]]
    place = region(WR, W_SIZE)
    q_out = place("q_out", [2, TPAD])

    def to_scratch(base, norm, run):
        with nc.Block() as block:
            @block.gpsimd
            def _(pool):
                nc.gpsimd.memset(q_out[:], 0.0)

        def act_q(act, u, slot, i, s):
            finished(act, u + 1)
            act.wait_ge(q_stored[s], 16 * i + (run * 8 * KT + PRIME))
            nc.scalar.copy(in_two(q_out[:, s, 0:T]), both(slot)).then_inc(psum_free, 1)

        def sp_q(sp, u, slot, i, s):
            taken(sp, u)
            sp.dma_start(q_s[bass.ds(2 * i + s, 1)].rearrange("k p n -> (k p) n"), q_out[:, s]).then_inc(q_stored[s], 16)

        layer(base, KT, pe_linear, act_q, None, sp_q, norm=norm, pe_first=unit_product)
        with nc.Block() as block:
            @block.sync
            def _(sp):
                for s in (0, 1):
                    sp.wait_ge(q_stored[s], (run + 1) * 8 * KT + PRIME)

    to_scratch(MQ0, Norm(x, V_XATTN, T, xhi, xlo), 0)
    attention(nc, es, sem, region, a, dict(WR=WR, W_SIZE=W_SIZE, pu=pu, pm=pm, q_s=q_s, xhi=xhi, xlo=xlo, ident=ident))
    residual_layer(MO0)

    to_scratch(PQ0, Norm(x, V_FFN, T, xhi, xlo), 1)
    routing(nc, es, sem, region, a, dict(WR=WR, W_SIZE=W_SIZE, pu=pu, pm=pm, q_s=q_s, gate_s=gate_s, ident=ident, consts=consts))

    place = region(WR, W_SIZE)
    gates = place("gates", [T, GRP])
    hidden = place("hidden", [2, T])
    coef = place("coef", [2, T])
    chi = place("chi", [GRP, T], F32R)
    clo = place("clo", [GRP, T], F32R)
    gates_loaded = sem("gates_loaded")
    coef_done = sem("coef_done")
    chi_done = sem("chi_done")
    clo_done = sem("clo_done")
    TILES = GRP + KT
    VU = KT // 4

    def done_by(g, q):
        return g * TILES + (EXP0 + (q + 1 if q < GRP else GRP + 4 * (q + 1 - GRP)))

    def group_sp(sp, g, last):
        for q in range(GRP + VU):
            if not (last and q >= GRP + VU - 2):
                load_unit(sp, g * 8 + (EXP0 + q + 2), (EXP0 + q) % 2)
            if q == 0:
                sp.wait_ge(coef_done, g * GRP)
                sp.dma_start(gates[:].rearrange("p t i -> p (t i)"), a["gate_s"][bass.ds(g, 1)].rearrange("g p n -> (g p) n")).then_inc(gates_loaded, 16)

    def group_pe(pe, g):
        for q in range(GRP + VU):
            slot = (EXP0 + q) % 2
            pe.wait_ge(lo_ready, g * 8 + (EXP0 + q + 1))
            if q < GRP:
                pe.wait_ge(psum_free, g * TILES + (EXP0 + q + 1))
                products([pu[:, q % 2, b, 0:HALF] for b in (0, 1)],
                         [(whi[:, slot, k], wlo[:, slot, k], halves(xhi, xlo, k)) for k in range(KT)]).then_inc(tiles_done, 1)
                continue
            if q == GRP:
                pe.wait_ge(clo_done, g * GRP + GRP)
            for d in range(4):
                pe.wait_ge(psum_free, g * TILES + (EXP0 + GRP + 4 * (q - GRP) + d + 1))
                products([pu[:, d % 2, b, 0:HALF] for b in (0, 1)],
                         [(whi[:, slot, GRP * d + k], wlo[:, slot, GRP * d + k], halves(chi, clo, k)) for k in range(GRP)]).then_inc(tiles_done, 1)

    def group_act(act, g, last):
        for q in range(GRP + VU):
            if not (last and q == GRP + VU - 1):
                split_hi(act, (EXP0 + q + 1) % 2, g * 4 + ((EXP0 + q + 1) // 2 + 1), done_by(g, q - 1) if q else g * TILES + EXP0)
            if q < GRP:
                n = g * GRP + q
                finished(act, g * TILES + (EXP0 + q + 1))
                if q >= 2:
                    act.wait_ge(coef_done, n - 1)
                nc.scalar.activation(in_two(hidden[:, q % 2]), pu[:, q % 2, :, 0:HALF], ACT.Gelu).then_inc(psum_free, 1)
                act.wait_ge(coef_done, n + 1)
                if q == 0:
                    finished(act, g * TILES + EXP0)
                nc.scalar.copy(chi[:, q], coef[:, q % 2]).then_inc(chi_done, 1)

    def group_dve(dve, g, last):
        for q in range(GRP + VU):
            if not (last and q == GRP + VU - 1):
                split_lo(dve, g * 8 + (EXP0 + q + 1), (EXP0 + q + 1) % 2)
            if q < GRP:
                n = g * GRP + q
                taken(dve, g * TILES + (EXP0 + q))
                if q == 0:
                    dve.wait_ge(gates_loaded, 16 * g + 16)
                nc.vector.tensor_tensor(coef[:, q % 2], hidden[:, q % 2], gates[:, :, q], ALU.mult).then_inc(coef_done, 1)
                dve.wait_ge(chi_done, n + 1)
                nc.vector.tensor_tensor(clo[:, q], coef[:, q % 2], chi[:, q].bitcast(F32), ALU.subtract).then_inc(clo_done, 1)
                continue
            for d in range(4):
                o = 4 * (q - GRP) + d
                finished(dve, g * TILES + (EXP0 + GRP + o + 1))
                nc.vector.tensor_tensor(in_two(x[:, o]), pu[:, d % 2, :, 0:HALF], in_two(x[:, o]), ALU.add).then_inc(psum_free, 1)

    a["gate_s"] = gate_s
    with nc.Block() as block:
        @block.sync
        def _(sp):
            with sp.Fori(0, NGRP - 1) as g:
                group_sp(sp, g, False)
            group_sp(sp, NGRP - 1, True)

        @block.tensor
        def _(pe):
            with pe.Fori(0, NGRP) as g:
                group_pe(pe, g)

        @block.scalar
        def _(act):
            with act.Fori(0, NGRP - 1) as g:
                group_act(act, g, False)
            group_act(act, NGRP - 1, True)

        @block.vector
        def _(dve):
            with dve.Fori(0, NGRP - 1) as g:
                group_dve(dve, g, False)
            group_dve(dve, NGRP - 1, True)

    sum_pass(x, T)
    norm_final = Norm(x, V_FINAL, T, final=a["yT"])
    with nc.Block() as block:
        @block.tensor
        def _(pe):
            norm_final.pe(pe)

        @block.scalar
        def _(act):
            norm_final.act(act)

        @block.vector
        def _(dve):
            norm_final.dve(dve)

        @block.sync
        def _(sp):
            norm_final.sp(sp)

    es.close()


def deltanet(nc, es, sem, region, a, m):
    consts, vecs, SLOT, cat, ident, ones, cum = (m[k] for k in ("consts", "vecs", "SLOT", "cat", "ident", "ones", "cum"))
    beta, gcol, qkv_s = m["beta"], m["gcol"], m["qkv_s"]
    HP = [HEADS, P]
    pw = region(m["WR"], m["W_SIZE"])
    ph = region(m["HR"], m["H_SIZE"])
    qc, kc, vc = (pw(n, HP) for n in ("qc", "kc", "vc"))
    qn, kn, qdec, grows, egam = (pw(n, HP) for n in ("qn", "kn", "qdec", "grows", "egam"))
    vnat, kdec, resid = (pw(n, HP) for n in ("vnat", "kdec", "resid"))
    gcum, egcum = pw("gcum", [NCH * HEADS]), pw("egcum", [NCH * HEADS])
    glast, kscale = pw("glast", [HEADS]), pw("kscale", [HEADS])
    dA, dB, A, att, attm = (ph(n, HP) for n in ("dA", "dB", "A", "att", "attm"))
    Tn, Tt, half, vnew, S, Sd, o, og = (ph(n, HP) for n in ("Tn", "Tt", "halfp", "vnew", "S", "Sd", "o", "og"))
    L = [ph(f"L{i}", HP) for i in (0, 1)]
    sq = ph("sq", HP)
    rr = ph("rr", HP)
    flat = lambda t: t[:].rearrange("p h n -> p (h n)")
    psum = lambda s: SLOT[s].rearrange("p (h n) -> p h n", n=P)
    bc_in = lambda ap: ap.unsqueeze(2).broadcast_to([P, HEADS, P])
    bc_h = lambda ap: ap.unsqueeze(1).broadcast_to([P, HEADS, P])

    names = ("loaded summed spread gamma gam_ready diffs exps sq_q sq_k ssq ssk rk normed_k scores decayed turned "
             "kdec_done vnat_done level_l level_p level_pc level_x level_t ks resid_done vn vn_copied qdec_done outs sqo sso "
             "ro s_loaded chain_a chain_d").split()
    q = {n: sem("dn_" + n) for n in names}
    q["cat_done"] = m["cat_done"]
    s_stored = sem("dn_s_stored")

    with nc.Block() as block:
        @block.tensor
        def _(pe):
            nc.tensor.matmul(SLOT[0][:, 0:NCH * HEADS], cum, gcol[:], start=True, stop=True).then_inc(q["summed"], 1)

        @block.vector
        def _(dve):
            dve.wait_ge(q["summed"], 1)
            nc.vector.tensor_copy(gcum[:], SLOT[0][:, 0:NCH * HEADS]).then_inc(q["gam_ready"], 1)
            nc.vector.memset(flat(S), 0.0)

        @block.scalar
        def _(act):
            act.wait_ge(q["gam_ready"], 1)
            nc.scalar.activation(egcum[:], gcum[:], ACT.Exp)

    A_, B_, C_, D_ = range(4)
    PER = {"level": LEVELS}

    def sp_chunk(sp, c):
        sp.wait_ge(q["cat_done"], c + PRIME)
        for n, t in enumerate((qc, kc, vc)):
            sp.dma_start(t[:], qkv_s[8 * n:8 * n + 8, :, bass.ds(c * P, P)].rearrange("h p n -> p h n")).then_inc(q["loaded"], 16)

    def pe_chunk(pe, c):
        pe.wait_ge(q["spread"], c + 1)
        for h in range(HEADS):
            ins = nc.tensor.matmul(psum(A_)[:, h], grows[:, h], cum, start=True, stop=True)
        ins.then_inc(q["gamma"], 1)
        for slot, src, ready, out in ((B_, 0, "sq_q", "ssq"), (C_, 1, "sq_k", "ssk")):
            pe.wait_ge(q[ready], c + 1)
            t = (sq, rr)[src]
            for b in (0, 1):
                ins = nc.tensor.matmul(SLOT[slot][:, 512 * b:512 * b + 512], ones, flat(t)[:, 512 * b:512 * b + 512], start=True, stop=True)
            ins.then_inc(q[out], 1)
        pe.wait_ge(q["normed_k"], c + 1)
        for h in range(HEADS):
            nc.tensor.matmul(psum(D_)[:, h], kn[:, h], kn[:, h], start=True, stop=True)
        pe.wait_ge(q["exps"], c + 1)
        for h in range(HEADS):
            ins = nc.tensor.matmul(psum(A_)[:, h], kn[:, h], qn[:, h], start=True, stop=True)
        ins.then_inc(q["scores"], 1)
        for h in range(HEADS):
            nc.tensor.transpose(psum(B_)[:, h], kn[:, h], ident)
        for h in range(HEADS):
            ins = nc.tensor.transpose(psum(C_)[:, h], vc[:, h], ident)
        ins.then_inc(q["turned"], 1)
        pe.wait_ge(q["kdec_done"], c + 1)
        pe.wait_ge(q["vnat_done"], c + 1)
        for l in range(LEVELS):
            n = c * LEVELS + l
            pe.wait_ge(q["level_l"], n + 1)
            if l == 0:
                pe.wait_ge(q["decayed"], c + 1)
            pe.wait_ge(q["level_t"], n + c + 1)
            for h in range(HEADS):
                ins = nc.tensor.matmul(psum(D_)[:, h], L[l % 2][:, h], Tt[:, h], start=True, stop=True)
            ins.then_inc(q["level_p"], 1)
            pe.wait_ge(q["level_pc"], n + 1)
            for h in range(HEADS):
                nc.tensor.matmul(psum(A_)[:, h], Tn[:, h], half[:, h], start=True, stop=True)
            for h in range(HEADS):
                ins = nc.tensor.matmul(psum(B_)[:, h], half[:, h], Tn[:, h], start=True, stop=True)
            ins.then_inc(q["level_x"], 1)
        for h in range(HEADS):
            ins = nc.tensor.matmul(psum(C_)[:, h], kn[:, h], S[:, h], start=True, stop=True)
        ins.then_inc(q["ks"], 1)
        pe.wait_ge(q["resid_done"], c + 1)
        for h in range(HEADS):
            ins = nc.tensor.matmul(psum(D_)[:, h], Tt[:, h], resid[:, h], start=True, stop=True)
        ins.then_inc(q["vn"], 1)
        pe.wait_ge(q["vn_copied"], c + 1)
        pe.wait_ge(q["qdec_done"], c + 1)
        for h in range(HEADS):
            nc.tensor.matmul(psum(A_)[:, h], S[:, h], qdec[:, h], start=True, stop=False)
            nc.tensor.matmul(psum(A_)[:, h], vnew[:, h], attm[:, h], start=False, stop=True)
        for h in range(HEADS):
            ins = nc.tensor.matmul(psum(B_)[:, h], kdec[:, h], vnew[:, h], start=True, stop=True)
        ins.then_inc(q["outs"], 1)
        pe.wait_ge(q["sqo"], c + 1)
        for b in (0, 1):
            ins = nc.tensor.matmul(SLOT[C_][:, 512 * b:512 * b + 512], ones, flat(sq)[:, 512 * b:512 * b + 512], start=True, stop=True)
        ins.then_inc(q["sso"], 1)

    eps = vecs[:, V_EPS:V_EPS + 1]

    def act_chunk(act, c, chain):
        act.wait_ge(q["loaded"], 48 * c + 48)
        nc.scalar.activation(flat(sq), flat(qc), ACT.Square).then_inc(q["sq_q"], 1)
        nc.scalar.activation(flat(rr), flat(kc), ACT.Square).then_inc(q["sq_k"], 1)
        act.wait_ge(q["diffs"], c + 1)
        nc.scalar.activation(flat(egam), SLOT[A_], ACT.Exp)
        nc.scalar.activation(flat(dA), flat(dA), ACT.Exp, scale=-1.0)
        nc.scalar.activation(flat(dB), flat(dB), ACT.Exp)
        nc.scalar.activation(kscale[:], glast[:], ACT.Exp).then_inc(q["exps"], 1)
        act.wait_ge(q["ssq"], c + 1)
        act.wait_ge(q["ssk"], c + 1)
        nc.scalar.activation(flat(sq), SLOT[B_], ACT.Ln, bias=eps)
        chain.link(nc.scalar.activation(flat(rr), SLOT[C_], ACT.Ln, bias=eps))
        nc.scalar.activation(flat(sq), flat(sq), ACT.Exp, scale=-0.5)
        nc.scalar.activation(flat(rr), flat(rr), ACT.Exp, scale=-0.5).then_inc(q["rk"], 1)
        act.wait_ge(q["turned"], c + 1)
        nc.scalar.copy(flat(vnat), SLOT[C_]).then_inc(q["vnat_done"], 1)
        for l in range(LEVELS):
            act.wait_ge(q["level_p"], c * LEVELS + l + 1)
            nc.scalar.copy(flat(half), SLOT[D_]).then_inc(q["level_pc"], 1)
        act.wait_ge(q["vn"], c + 1)
        nc.scalar.copy(flat(vnew), SLOT[D_]).then_inc(q["vn_copied"], 1)
        act.wait_ge(q["outs"], c + 1)
        nc.scalar.activation(flat(sq), SLOT[A_], ACT.Square).then_inc(q["sqo"], 1)
        nc.scalar.copy(flat(o), SLOT[A_])
        act.wait_ge(q["sso"], c + 1)
        chain.link(nc.scalar.activation(flat(rr), SLOT[C_], ACT.Ln, scale=1.0 / P, bias=eps))
        nc.scalar.activation(flat(rr), flat(rr), ACT.Exp, scale=-0.5).then_inc(q["ro"], 1)
        act.wait_ge(q["cat_done"], c + 1 + PRIME)

    def dve_chunk(dve, c, chain, width):
        tt = nc.vector.tensor_tensor
        cols = lambda t: t[:, bass.ds(c * HEADS, HEADS)]
        dve.wait_ge(q["gamma"], c + 1)
        tt(dA[:], psum(A_), bc_in(cols(gcum)), ALU.subtract)
        tt(glast[:], psum(A_)[:, :, P - 1], cols(gcum), ALU.subtract)
        chain.link(tt(dB[:], psum(A_), bc_in(cols(gcum)), ALU.subtract))
        nc.vector.tensor_scalar(flat(dA), flat(dA), 0.0, None, ALU.max)
        nc.vector.tensor_scalar(flat(dB), flat(dB), 0.0, None, ALU.min).then_inc(q["diffs"], 1)
        dve.wait_ge(q["loaded"], 48 * c + 48)
        dve.wait_ge(q["rk"], c + 1)
        nc.vector.scalar_tensor_tensor(flat(qn), flat(qc), float(P) ** -0.5, flat(sq), ALU.mult, ALU.mult)
        tt(flat(kn), flat(kc), flat(rr), ALU.mult).then_inc(q["normed_k"], 1)
        dve.wait_ge(q["scores"], c + 1)
        chain.link(tt(A[:], psum(D_), bc_in(cols(beta)), ALU.mult))
        dve.wait_ge(q["exps"], c + 1)
        tt(flat(A), flat(A), flat(dA), ALU.mult).then_inc(q["decayed"], 1)
        chain.link(tt(flat(att), SLOT[A_], flat(dB), ALU.mult))
        tt(attm[:], att[:], bc_h(cum), ALU.mult)
        dve.wait_ge(q["turned"], c + 1)
        tt(kdec[:], psum(B_), bc_in(kscale[:]), ALU.mult).then_inc(q["kdec_done"], 1)
        nc.vector.tensor_copy(Tn[:], bc_h(ident))
        nc.vector.tensor_copy(Tt[:], bc_h(ident)).then_inc(q["level_t"], 1)
        for l in range(LEVELS):
            dve.wait_ge(q["level_x"], c * LEVELS + l + 1)
            tt(flat(Tt), flat(Tt), SLOT[A_], ALU.subtract)
            tt(flat(Tn), flat(Tn), SLOT[B_], ALU.subtract).then_inc(q["level_t"], 1)
        dve.wait_ge(q["ks"], c + 1)
        chain.link(tt(resid[:], psum(C_), bc_in(cols(egcum)), ALU.mult))
        chain.link(tt(flat(resid), flat(vnat), flat(resid), ALU.subtract))
        tt(resid[:], resid[:], bc_in(cols(beta)), ALU.mult).then_inc(q["resid_done"], 1)
        dve.wait_ge(q["outs"], c + 1)
        chain.link(tt(Sd[:], S[:], bc_in(egam[:, :, P - 1]), ALU.mult))
        tt(flat(S), flat(Sd), SLOT[B_], ALU.add)
        dve.wait_ge(q["ro"], c + 1)
        chain.link(nc.vector.scalar_tensor_tensor(flat(og), flat(o), vecs[:, V_DN:V_DN + 1], flat(rr), ALU.mult, ALU.mult))
        at = cat[:, 8:16, bass.ds(c * P, width)]
        tt(at, og[:, :, 0:width], at, ALU.mult).then_inc(q["cat_done"], 1)

    def pool_chunk(pool, c):
        pool.wait_ge(q["cat_done"], c + PRIME)
        nc.gpsimd.tensor_tensor(grows[:], bc_h(ones), bc_in(gcol[:, bass.ds(c * HEADS, HEADS)]), ALU.mult).then_inc(q["spread"], 1)
        pool.wait_ge(q["decayed"], c + 1)
        for l in range(LEVELS):
            if l >= 2:
                pool.wait_ge(q["level_p"], c * LEVELS + l - 1)
            nc.gpsimd.tensor_tensor(L[l % 2][:], A[:], bc_h(consts[:, C_LEV + l * P:C_LEV + (l + 1) * P]), ALU.mult).then_inc(q["level_l"], 1)
        nc.gpsimd.tensor_tensor(flat(qdec), flat(qn), flat(egam), ALU.mult).then_inc(q["qdec_done"], 1)

    def chunks(first, count, width):
        def run(eng, body):
            if count > 1:
                with eng.Fori(first, first + count) as c:
                    body(c)
            else:
                body(first)

        with nc.Block() as block:
            @block.sync
            def _(sp):
                run(sp, lambda c: sp_chunk(sp, c))

            @block.tensor
            def _(pe):
                run(pe, lambda c: pe_chunk(pe, c))

            @block.scalar
            def _(act):
                def body(c):
                    chain = Chain(act, q["chain_a"])
                    chain.enter(c, 2)
                    act_chunk(act, c, chain)
                run(act, body)

            @block.vector
            def _(dve):
                def body(c):
                    chain = Chain(dve, q["chain_d"])
                    chain.enter(c, 7)
                    dve_chunk(dve, c, chain, width)
                    assert chain.n == 7, chain.n
                run(dve, body)

            @block.gpsimd
            def _(pool):
                run(pool, lambda c: pool_chunk(pool, c))

    chunks(0, NCH - 1, P)
    with nc.Block() as block:
        @block.sync
        def _(sp):
            sp.dma_start(a["dn_prompt"].rearrange("h p n -> p h n"), S[:]).then_inc(s_stored, 16)
            sp.wait_ge(s_stored, 16)
            sp.dma_start(S[:], a["state"].rearrange("h p n -> p h n")).then_inc(q["s_loaded"], 16)
            sp.wait_ge(q["s_loaded"], 16)
    chunks(NCH - 1, 1, TS)
    with nc.Block() as block:
        @block.sync
        def _(sp):
            sp.dma_start(a["dn_sample"].rearrange("h p n -> p h n"), S[:]).then_inc(s_stored, 16)
            sp.wait_ge(s_stored, 32)


def attention(nc, es, sem, region, a, m):
    pu, pm, q_s, xhi, xlo, ident = (m[k] for k in ("pu", "pm", "q_s", "xhi", "xlo", "ident"))
    place = region(m["WR"], m["W_SIZE"])
    qh = place("qh", [2, MHT, T])
    kh = place("kh", [2, MHT, M])
    vh = place("vh", [2, 2, MHT * P])
    pr = place("pr", [4, M])
    pn = place("pn", [4, M])
    pT = place("pT", [2, TP])
    mx, nmx, sm, rs = (place("at_" + n, [4]) for n in ("mx", "nmx", "sm", "rs"))
    names = "k_loaded0 k_loaded1 scores maxed exps normed turned copied pv out_hi out_lo".split()
    q = {n: sem("at_" + n) for n in names}
    chain_sem = sem("at_chain")
    loaded = [q["k_loaded0"], q["k_loaded1"]]
    jobs = [(h, 0, P, TP // P, a["mkT"], a["mv"]) for h in range(MH)]
    jobs += [(h, TP, TS, 1, a["mkT_sample"], a["mv_sample"]) for h in range(MH)]
    with nc.Block() as block:
        @block.sync
        def _(sp):
            for n, (h, t0, w, tiles, kk, vv) in enumerate(jobs):
                if n >= 2:
                    sp.wait_ge(q["pv"], MHT * (n - 1))
                s = n % 2
                sp.dma_start(qh[:, s], q_s[MHT * h:MHT * h + MHT, :, 0:T].rearrange("k p n -> p k n")).then_inc(loaded[s], 16)
                sp.dma_start(kh[:, s], kk[MHT * h:MHT * h + MHT].rearrange("k p n -> p k n")).then_inc(loaded[s], 16)
                sp.dma_start(vh[:, s], vv[:, :, h * MHT * P:(h + 1) * MHT * P]).then_inc(loaded[s], 16)

        @block.tensor
        def _(pe):
            for n, (h, t0, w, tiles, kk, vv) in enumerate(jobs):
                s = n % 2
                pe.wait_ge(loaded[s], 48 * (n // 2 + 1))
                if n:
                    pe.wait_ge(q["exps"], n)
                for i in range(tiles):
                    for j in range(MHT):
                        ins = nc.tensor.matmul(pm[0:w, i // 2, i % 2, 0:M], qh[:, s, j, t0 + i * P:t0 + i * P + w], kh[:, s, j],
                                               start=(j == 0), stop=(j == MHT - 1))
                ins.then_inc(q["scores"], 1)
                pe.wait_ge(q["normed"], n + 1)
                for i in range(tiles):
                    for b in (0, 1):
                        ins = nc.tensor.transpose(pu[:, 0, b, i * P:i * P + w], pn[0:w, i, b * P:(b + 1) * P], ident[0:w, 0:w])
                ins.then_inc(q["turned"], 1)
                pe.wait_ge(q["copied"], n + 1)
                for j in range(MHT):
                    o = n * MHT + j
                    if o >= 2:
                        pe.wait_ge(q["out_lo"], o - 1)
                    for b in (0, 1):
                        ins = nc.tensor.matmul(pu[:, 1, o % 2, 0:tiles * w], vh[:, s, b, j * P:(j + 1) * P], pT[:, b, 0:tiles * w],
                                               start=(b == 0), stop=(b == 1))
                    ins.then_inc(q["pv"], 1)

        @block.vector
        def _(dve):
            chain = Chain(dve, chain_sem)
            for n, (h, t0, w, tiles, kk, vv) in enumerate(jobs):
                dve.wait_ge(q["scores"], n + 1)
                sc = pm[0:w].rearrange("p a b n -> p (a b) n")[:, 0:tiles, 0:M]
                chain.link(nc.vector.tensor_reduce(mx[0:w, 0:tiles], sc, AX_X, ALU.max))
                nc.vector.tensor_scalar(nmx[0:w, 0:tiles], mx[0:w, 0:tiles], -MEM_SCALE, None, ALU.mult).then_inc(q["maxed"], 1)
                dve.wait_ge(q["exps"], n + 1)
                chain.link(nc.vector.reciprocal(rs[0:w, 0:tiles], sm[0:w, 0:tiles]))
                nc.vector.tensor_tensor(pn[0:w, 0:tiles], pr[0:w, 0:tiles], rs[0:w, 0:tiles].unsqueeze(2).broadcast_to([w, tiles, M]), ALU.mult).then_inc(q["normed"], 1)
                for j in range(MHT):
                    o = n * MHT + j
                    dve.wait_ge(q["out_hi"], o + 1)
                    at = slice(t0, t0 + tiles * w)
                    nc.vector.tensor_tensor(xlo[:, MHT * h + j, at], pu[:, 1, o % 2, 0:tiles * w], xhi[:, MHT * h + j, at].bitcast(F32), ALU.subtract).then_inc(q["out_lo"], 1)

        @block.scalar
        def _(act):
            for n, (h, t0, w, tiles, kk, vv) in enumerate(jobs):
                act.wait_ge(q["maxed"], n + 1)
                for i in range(tiles):
                    ins = nc.scalar.activation(pr[0:w, i], pm[0:w, i // 2, i % 2, 0:M], ACT.Exp, scale=MEM_SCALE,
                                               bias=nmx[0:w, i:i + 1], accum_out=sm[0:w, i:i + 1])
                ins.then_inc(q["exps"], 1)
                act.wait_ge(q["turned"], n + 1)
                nc.scalar.copy(pT[:, :, 0:tiles * w], pu[:, 0, :, 0:tiles * w]).then_inc(q["copied"], 1)
                for j in range(MHT):
                    o = n * MHT + j
                    act.wait_ge(q["pv"], o + 1)
                    nc.scalar.copy(xhi[:, MHT * h + j, t0:t0 + tiles * w], pu[:, 1, o % 2, 0:tiles * w]).then_inc(q["out_hi"], 1)


def routing(nc, es, sem, region, a, m):
    pu, pm, q_s, gate_s, ident, consts = (m[k] for k in ("pu", "pm", "q_s", "gate_s", "ident", "consts"))
    place = region(m["WR"], m["W_SIZE"])
    gateT, rowT, colT = (place(n, [TPAD]) for n in ("gateT", "rowT", "colT"))
    used = 3 * 4 * TPAD
    place = region(m["WR"] + used, m["W_SIZE"] - used)
    qt = place("qt", [KT, P])
    keys = place("keys", [KT, P])
    sc = place("sc", [KT, P])
    cand = place("cand", [8, TOPK * TOPK])
    v1 = place("v1", [KT, TOPK])
    i1 = place("i1", [KT, TOPK], U32)
    f1 = place("f1", [KT, TOPK])
    v2 = place("v2", [8, TOPK])
    i2 = place("i2", [8, TOPK], U32)
    ia, ib = place("ia", [8, TOPK], U32), place("ib", [8, TOPK], U32)
    fa, fb = place("fa", [8, TOPK]), place("fb", [8, TOPK])
    row, col = place("row", [8, TOPK]), place("col", [8, TOPK])
    ex, gate = place("ex", [8, TOPK]), place("gate", [8, TOPK])
    sm, rs, pause = place("rt_sm", [8]), place("rt_rs", [8]), place("pause", [1])
    pick = cand
    names = "keys_loaded q_loaded scores sc_ready dif exped slots_ready turned taken chain".split()
    q = {n: sem("rt_" + n) for n in names}
    LINKS = 21

    with nc.Block() as block:
        @block.sync
        def _(sp):
            sp.dma_start(keys[:], a["keys"]).then_inc(q["keys_loaded"], 16)
            with sp.Fori(0, NCH) as t:
                sp.wait_ge(q["scores"], t)
                sp.dma_start(qt[:], q_s[:, :, bass.ds(t * P, P)].rearrange("k p n -> p k n")).then_inc(q["q_loaded"], 16)

        @block.tensor
        def _(pe):
            pe.wait_ge(q["keys_loaded"], 16)
            with pe.Fori(0, NCH) as t:
                pe.wait_ge(q["q_loaded"], 16 * t + 16)
                pe.wait_ge(q["sc_ready"], t)
                for k in range(KT):
                    ins = nc.tensor.matmul(pm[:, k // 8, (k // 4) % 2, (k % 4) * P:(k % 4 + 1) * P], qt[:, k], keys[:, k], start=True, stop=True)
                ins.then_inc(q["scores"], 1)
                pe.wait_ge(q["slots_ready"], t + 1)
                for n, src in enumerate((gate, row, col)):
                    ins = nc.tensor.transpose(pu[:, 0, 0, n * P:(n + 1) * P], src[:].rearrange("p h k -> p (h k)"), ident)
                ins.then_inc(q["turned"], 1)

        @block.scalar
        def _(act):
            with act.Fori(0, NCH) as t:
                act.wait_ge(q["scores"], t + 1)
                act.wait_ge(q["slots_ready"], t)
                nc.scalar.copy(sc[:].rearrange("p k n -> p (k n)"), pm[:].rearrange("p a b n -> p (a b n)")).then_inc(q["sc_ready"], 1)
                act.wait_ge(q["dif"], t + 1)
                nc.scalar.activation(ex[:], v2[:], ACT.Exp).then_inc(q["exped"], 1)
                act.wait_ge(q["turned"], t + 1)
                for n, dst in enumerate((gateT, rowT, colT)):
                    ins = nc.scalar.copy(dst[:, bass.ds(t * P, P)], pu[:, 0, 0, n * P:(n + 1) * P])
                ins.then_inc(q["taken"], 1)

        @block.vector
        def _(dve):
            chain = Chain(dve, q["chain"])
            link = chain.link
            v = nc.vector

            def settle(ins):
                link(ins)
                v.memset(pause[:], 0.0)
            with dve.Fori(0, NCH) as t:
                chain.enter(t, LINKS)
                dve.wait_ge(q["sc_ready"], t + 1)
                v.memset(pause[:], 0.0)
                for vals, n, best, at in ((sc, KT, v1, i1), (cand, 8, v2, i2)):
                    if n == 8:
                        settle(v.tensor_tensor(cand[:].rearrange("p h (i j) -> p h i j", i=TOPK),
                                             v1[:, 0:KT:2].unsqueeze(3).broadcast_to([P, 8, TOPK, TOPK]),
                                             v1[:, 1:KT:2].unsqueeze(2).broadcast_to([P, 8, TOPK, TOPK]), ALU.add))
                    for r in (0, 1):
                        o = slice(8 * r, 8 * r + 8)
                        for k in range(n):
                            ins = v.max(best[:, k, o], vals[:, k])
                        settle(ins)
                        for k in range(n):
                            ins = v.max_index(at[:, k, o], best[:, k, o], vals[:, k])
                        if r == 0:
                            settle(ins)
                            for k in range(n):
                                ins = v.match_replace(vals[:, k], best[:, k, o], vals[:, k], LOWEST)
                        settle(ins)
                v.tensor_scalar(ia[:], i2[:], 4, None, ALU.logical_shift_right)
                v.tensor_scalar(ib[:], i2[:], 15, None, ALU.bitwise_and)
                link(v.tensor_copy(f1[:], i1[:]))
                v.tensor_copy(fa[:], ia[:])
                link(v.tensor_copy(fb[:], ib[:]))
                steps = consts[:, C_IOTA:C_IOTA + TOPK].unsqueeze(1).broadcast_to([P, 128, TOPK])
                for place_, half, key in ((fa, 0, row), (fb, 1, col)):
                    pk = pick[:].rearrange("p h (k n) -> p (h k) n", k=TOPK)
                    link(v.tensor_tensor(pk, place_[:].rearrange("p h k -> p (h k)").unsqueeze(2).broadcast_to([P, 128, TOPK]), steps, ALU.is_equal))
                    p4 = pick[:].rearrange("p h (k n) -> p h k n", k=TOPK)
                    link(v.tensor_tensor(p4, p4, f1[:, half:KT:2].unsqueeze(2).broadcast_to([P, 8, TOPK, TOPK]), ALU.mult))
                    ins = v.tensor_reduce(key[:].rearrange("p h k -> p (h k)"), pk, AX_X, ALU.add)
                    if half == 0:
                        link(ins)
                link(v.tensor_copy(rs[:], v2[:, :, 0]))
                v.tensor_tensor(v2[:], v2[:], rs[:].unsqueeze(2).broadcast_to([P, 8, TOPK]), ALU.subtract).then_inc(q["dif"], 1)
                dve.wait_ge(q["exped"], t + 1)
                link(v.tensor_reduce(sm[:], ex[:], AX_X, ALU.add))
                link(v.reciprocal(rs[:], sm[:]))
                v.tensor_tensor(gate[:], ex[:], rs[:].unsqueeze(2).broadcast_to([P, 8, TOPK]), ALU.mult).then_inc(q["slots_ready"], 1)
                dve.wait_ge(q["taken"], t + 1)
                assert chain.n == LINKS, chain.n

    TC = 32
    place = region(m["WR"] + used, m["W_SIZE"] - used)
    hot_r = place("hot_r", [2, 4, P])
    hot_c = place("hot_c", [2, 4, P])
    table = [place(f"table{i}", [NGRP, TC, GRP]) for i in (0, 1)]
    names = "rows cols dense out stored0 stored1".split()
    q = {n: sem("gt_" + n) for n in names}
    stored = [q["stored0"], q["stored1"]]
    iota = consts[:, C_IOTA:C_IOTA + P]
    with nc.Block() as block:
        def quads(eng, body):
            with eng.Fori(0, 8) as c:
                for s in (0, 1):
                    with eng.Fori(0, 4) as k:
                        for r in (0, 1):
                            body(c * 16 + k * 2 + (8 * s + r), k * 2 + r, r, c, s)
                    yield c, s
            with eng.Fori(0, 4) as k:
                for r in (0, 1):
                    body(k * 2 + (128 + r), k * 2 + r, r, 8, 0)
            yield 8, 0

        @block.vector
        def _(dve):
            def body(n, k, r, c, s):
                dve.wait_ge(q["dense"], n - r)
                for i in range(4):
                    at = bass.ds(n * 4 + i, 1)
                    ins = nc.vector.tensor_scalar(hot_r[:, r, i], iota, rowT[:, at], gateT[:, at], ALU.is_equal, ALU.mult)
                ins.then_inc(q["rows"], 1)
                nc.vector.tensor_tensor(hot_c[:, r], iota.unsqueeze(1).broadcast_to([P, 4, P]),
                                        colT[:, bass.ds(n * 4, 4)].unsqueeze(2).broadcast_to([P, 4, P]), ALU.is_equal).then_inc(q["cols"], 1)
            for _ in quads(dve, body):
                pass

        @block.tensor
        def _(pe):
            def body(n, k, r, c, s):
                pe.wait_ge(q["rows"], n + 1)
                pe.wait_ge(q["cols"], n + 1)
                pe.wait_ge(q["out"], n - r)
                for i in range(4):
                    ins = nc.tensor.matmul(pm[:, r, 0, i * P:(i + 1) * P], hot_c[:, r, i], hot_r[:, r, i], start=True, stop=True)
                ins.then_inc(q["dense"], 1)
            for _ in quads(pe, body):
                pass

        @block.scalar
        def _(act):
            def body(n, k, r, c, s):
                act.wait_ge(q["dense"], n + 1)
                act.wait_ge(stored[s], 16 * c)
                out = table[s][:, :, bass.ds(k * 4, 4), :]
                nc.scalar.copy(out.rearrange("p g t i -> p t g i"), pm[:, r, 0].rearrange("p (t g i) -> p t g i", t=4, g=NGRP)).then_inc(q["out"], 1)
            for _ in quads(act, body):
                pass

        @block.sync
        def _(sp):
            def store(c, s):
                sp.wait_ge(q["out"], c * 16 + (8 * s + 8))
                sp.dma_start(gate_s[:, :, bass.ds(c * (2 * TC * GRP) + s * TC * GRP, TC * GRP)].rearrange("g p n -> p g n"),
                             table[s][:].rearrange("p g t i -> p g (t i)")).then_inc(stored[s], 16)
            with sp.Fori(0, 8) as c:
                for s in (0, 1):
                    store(c, s)
            store(8, 0)
            sp.wait_ge(stored[0], 16 * 9)
            sp.wait_ge(stored[1], 16 * 8)


def _tiles(a):
    n, m = a.shape
    return np.ascontiguousarray(a.reshape(n // P, P, m).transpose(1, 0, 2))


def _units(w):
    n = w.shape[1] // P
    return w.reshape(KT, P, n, P).transpose(2, 1, 0, 3).reshape(n, P, KT * P)


def kernel(**inputs):
    import concourse.bacc as bacc
    from concourse.bass_utils import run_bass_kernel_spmd

    g = {k: np.asarray(v) for k, v in inputs.items()}
    w_in = g["w_in"][0]
    units = np.zeros((UNITS, P, KT * P), np.float32)
    units[MK0:MV0] = _units(g["w_mk"][0])
    units[MV0:Z0] = g["w_mv"][0].reshape(4, 4, P, 4, 512).transpose(3, 0, 2, 1, 4).reshape(KT, P, KT * P)
    units[Z0:POOL0] = _units(w_in[:, 4112:])
    units[POOL0:AB0] = _units(w_in[:, :4096])
    ab = np.zeros((D, P), np.float32)
    ab[:, :16] = w_in[:, 4096:4112]
    units[AB0:OUT0] = _units(ab)
    units[OUT0:MQ0] = _units(g["w_out"][0])
    units[MQ0:MO0] = _units(g["w_mq"][0])
    units[MO0:PQ0] = _units(g["w_mo"][0])
    units[PQ0:EXP0] = _units(g["w_pq"][0])
    ex = units[EXP0:].reshape(NGRP, 2, GRP, P, KT * P)
    ex[:, 0] = g["u_experts"][0].reshape(NGRP, GRP, P, KT, P).transpose(0, 1, 4, 3, 2).reshape(NGRP, GRP, P, KT * P)
    ex[:, 1] = g["v_experts"][0].reshape(NGRP, GRP, P, 4, 4, P).transpose(0, 3, 2, 4, 1, 5).reshape(NGRP, 4, P, KT * P)
    vecs = np.zeros((P, NV), np.float32)
    for at, name in ((V_MIX, "norm_mix"), (V_XATTN, "norm_xattn"), (V_MEM, "norm_mem"), (V_FFN, "norm_ffn"), (V_FINAL, "norm_final")):
        vecs[:, at:at + KT] = g[name].reshape(KT, P).T
    vecs[:, V_POOL:V_POOL + 8] = g["pool_scale"].reshape(8, P).T
    vecs[:, V_CONV:V_CONV + 96] = g["conv_w"][0].reshape(4, 24, P).transpose(2, 1, 0).reshape(P, 96)
    vecs[:, V_DN] = g["norm_dn"][0]
    vecs[:, V_EPS] = EPS
    vecs[:, V_ALOG:V_ALOG + 8] = g["a_log"][0]
    vecs[:, V_DT:V_DT + 8] = g["dt_bias"][0]
    ins = {
        "units": units,
        "consts": constants(),
        "vecs": vecs,
        "xT": _tiles(np.concatenate([g["x_prompt"][0], g["x_sample"][0]], 0).T),
        "memT": _tiles(g["mem_prompt"][0].T),
        "phist": _tiles(g["cache_pool"][0, 0].T),
        "chist": _tiles(g["cache_conv"][0, 0].T),
        "wpool": np.ascontiguousarray(g["w_pool"][0].reshape(4, 2, P, 2, P).transpose(2, 0, 1, 3, 4).reshape(P, KT, P)),
        "state": np.ascontiguousarray(g["state_dn"][0, 0]),
        "mkT_sample": np.ascontiguousarray(g["cache_mem_k"][0, 0].reshape(M, D).T.reshape(KT, P, M)),
        "mv_sample": _tiles(g["cache_mem_v"][0, 0].reshape(M, D)),
        "keys": np.ascontiguousarray(g["sub_keys"][0].transpose(3, 0, 1, 2).reshape(P, KT, P)),
    }
    outs = {
        "yT": (KT, P, T), "pool_new": (P, 8, 2, 15), "conv_new": (P, 24, 2, 3), "dn_prompt": (8, P, P),
        "dn_sample": (8, P, P), "mkT": (KT, P, M), "mv": (P, 2, D),
    }
    nc = bacc.Bacc("TRN2", target_bir_lowering=False, num_devices=1)
    a = {k: nc.dram_tensor(k, v.shape, F32, kind="ExternalInput").ap() for k, v in ins.items()}
    a.update({k: nc.dram_tensor(k, s, F32, kind="ExternalOutput").ap() for k, s in outs.items()})
    build(nc, a)
    r = run_bass_kernel_spmd(nc, [ins], core_ids=[0]).results[0]
    y = r["yT"].reshape(D, T).T
    hist = lambda v, n: np.ascontiguousarray(v.transpose(2, 3, 1, 0)).reshape(2, 1, 1, n, -1)
    pool, conv = hist(r["pool_new"], 15), hist(r["conv_new"], 3)
    mk = np.ascontiguousarray(r["mkT"].reshape(D, M).T).reshape(1, 1, M, 4, 512)
    mv = np.ascontiguousarray(r["mv"].transpose(1, 0, 2)).reshape(1, 1, M, 4, 512)
    return (np.ascontiguousarray(y[:TP])[None], np.ascontiguousarray(y[TP:])[None],
            pool[0], conv[0], r["dn_prompt"][None, None], mk, mv,
            pool[1], conv[1], r["dn_sample"][None, None])
```

```python
from contextlib import ExitStack

import numpy as np

import concourse.bass as bass
from concourse import mybir

F32 = mybir.dt.float32
F32R = mybir.dt.float32r
U32 = mybir.dt.uint32
ALU = mybir.AluOpType
ACT = mybir.ActivationFunctionType
AX_X = mybir.AxisListType.X

P = 128
D = 2048
KT = D // P
TP, TS = 512, 32
T = TP + TS
HALF = T // 2
NCH = 5
TPAD = NCH * P
M = 256
EPS = 1e-6
HEADS = 8
LEVELS = 7
MH, MHT = 4, 4
MEM_SCALE = float(MHT * P) ** -0.5
TOPK = 16
GRP = 4
NGRP = P // GRP
LOWEST = -3.0e38
PRIME = 1

MK0 = 0
MV0 = MK0 + KT
Z0 = MV0 + KT
AB0 = Z0 + 8
POOL0 = AB0 + 1
QKV0 = POOL0 + 8
OUT0 = QKV0 + 24
MQ0 = OUT0 + KT
MO0 = MQ0 + KT
PQ0 = MO0 + KT
EXP0 = PQ0 + KT
V0 = EXP0 + P
UNITS = V0 + P
TC = 32

V_MIX, V_XATTN, V_MEM, V_FFN, V_FINAL = (16 * i for i in range(5))
V_POOL = 80
V_CONV = V_POOL + 8
V_DN = V_CONV + 96
V_EPS = V_DN + 1
V_ALOG = V_EPS + 1
V_DT = V_ALOG + 8
NV = V_DT + 8

C_ID = 0
C_ONE = C_ID + P
C_CUM = C_ONE + P
C_LEV = C_CUM + P
C_IOTA = C_LEV + LEVELS * P
C_CNT = C_IOTA + P
C_VALID = C_CNT + 64
NC = C_VALID + NCH * HEADS


def constants():
    c = np.zeros((P, NC), np.float32)
    r = np.arange(P)
    c[:, C_ID:C_ID + P] = np.eye(P)
    c[:, C_ONE:C_ONE + P] = 1.0
    c[:, C_CUM:C_CUM + P] = r[:, None] <= r[None, :]
    for l in range(LEVELS):
        s = 1 << l
        same = (r[:, None] // (2 * s)) == (r[None, :] // (2 * s))
        c[:, C_LEV + l * P:C_LEV + (l + 1) * P] = same & ((r[:, None] // s) % 2 == 1) & ((r[None, :] // s) % 2 == 0)
    c[:, C_IOTA:C_IOTA + P] = r[None, :]
    for g in range(4):
        c[:, C_CNT + 16 * g:C_CNT + 16 * g + 16] = 1.0 / np.minimum(np.arange(16) + 1, 2 << g)
    v = np.ones((P, NCH, HEADS), np.float32)
    v[TS:, NCH - 1] = 0.0
    c[:, C_VALID:NC] = v.reshape(P, -1)
    return c


class Chain:

    def __init__(self, eng, sem):
        self.eng, self.sem, self.base, self.n = eng, sem, 0, 0

    def link(self, ins):
        ins.then_inc(self.sem, 1)
        self.n += 1
        self.eng.wait_ge(self.sem, self.base + self.n)

    def enter(self, i, per):
        self.base, self.n = i * per, 0


def build(nc, a):
    es = ExitStack()

    def sem(name):
        return es.enter_context(nc.semaphore(name))

    primed = {n: sem(n) for n in (
        "tiles_done v_stored scaled_lo0 scaled_lo1 y_stored0 y_stored1 k_stored0 k_stored1 conv_done hist_kept "
        "qkv_stored0 qkv_stored1 silu_done q_stored0 q_stored1 sso_read s_updated cat_done scored slots_taken table_filled "
        "table_stored0 table_stored1 h_stored0 h_stored1 squares_summed").split()}

    start = -(-nc.sbuf_base // 64) * 64

    def region(offset, size):
        at = [offset]

        def place(name, free, dtype=F32):
            t = nc.alloc_sbuf_tensor_at(name, [P] + list(free), dtype, offset=at[0])
            at[0] += 4 * int(np.prod(free))
            at[0] = -(-at[0] // 32) * 32
            assert at[0] <= offset + size, (name, at[0] - offset - size)
            return t
        return place

    XR = start
    HR = XR + 4 * KT * T
    RR = HR + 8 * KT * T
    CR = RR + 6 * 4 * KT * P
    WR = -(-(CR + 4 * (NC + NV + 4 * NCH * HEADS) + 256) // 64) * 64
    W_SIZE = nc.sbuf_usable_end - WR
    NR_SIZE = 8 * 4 * T
    NR = (nc.sbuf_usable_end - NR_SIZE) // 64 * 64
    H_SIZE = 8 * KT * T

    place = region(RR, CR - RR)
    raw = place("raw", [2, KT, P])
    whi = place("whi", [2, KT, P], F32R)
    wlo = place("wlo", [2, KT, P], F32R)
    place = region(CR, WR - CR)
    consts = place("consts", [NC])
    vecs = place("vecs", [NV])
    gcol = place("gcol", [NCH * HEADS])
    beta = place("beta", [NCH * HEADS])
    gcum = place("gcum", [NCH * HEADS])
    egcum = place("egcum", [NCH * HEADS])
    place = region(XR, HR - XR)
    x = place("x", [KT, T])
    place = region(XR, HR - XR)
    cat = place("cat", [KT, T])
    place = region(WR, W_SIZE)
    mem = place("mem", [KT, M])
    place = region(HR, H_SIZE)
    xhi = place("xhi", [KT, T], F32R)
    xlo = place("xlo", [KT, T], F32R)
    place = region(HR, H_SIZE)
    memhi = place("memhi", [KT, M], F32R)
    memlo = place("memlo", [KT, M], F32R)

    pu = es.enter_context(nc.psum_tensor("pu", [P, 2, 2, 512], F32))
    pm = es.enter_context(nc.psum_tensor("pm", [P, 2, 2, 512], F32))
    SLOT = [t[:, s].rearrange("p b n -> p (b n)") for t in (pu, pm) for s in (0, 1)]

    ident = consts[:, C_ID:C_ID + P]
    ones = consts[:, C_ONE:C_ONE + P]
    cum = consts[:, C_CUM:C_CUM + P]

    qkv_s = nc.dram_tensor("qkv_s", (24, P, TPAD), F32, kind="Internal").ap()
    q_s = nc.dram_tensor("q_s", (KT, P, TPAD), F32, kind="Internal").ap()
    x_s = nc.dram_tensor("x_s", (P, KT, T), F32, kind="Internal").ap()
    h_s = nc.dram_tensor("h_s", (P, P, T), F32, kind="Internal").ap()
    gate_s = nc.dram_tensor("gate_s", (NGRP, P, T * GRP), F32, kind="Internal").ap()

    raw_loaded = [sem("raw_loaded0"), sem("raw_loaded1")]
    hi_ready = sem("hi_ready")
    lo_ready = sem("lo_ready")
    tiles_done = primed["tiles_done"]
    psum_free = sem("psum_free")

    def finished(eng, n):
        eng.wait_ge(tiles_done, n + PRIME)

    def taken(eng, tile):
        eng.wait_ge(psum_free, tile + 3)

    def unit(base, i, s):
        return base + s + 2 * i, (base + s) % 2, i + (base + s) // 2 + 1

    def load_unit(sp, u, slot):
        sp.wait_ge(lo_ready, u - 1)
        sp.dma_start(raw[:, slot].rearrange("p k n -> p (k n)"), a["units"][bass.ds(u, 1)].rearrange("a p n -> (a p) n")).then_inc(raw_loaded[slot], 16)

    def split_hi(act, slot, fills, done):
        act.wait_ge(raw_loaded[slot], 16 * fills)
        finished(act, done)
        nc.scalar.copy(whi[:, slot], raw[:, slot]).then_inc(hi_ready, 1)

    def split_lo(eng, u, slot, how=None):
        eng.wait_ge(hi_ready, u + 1)
        (how or nc.vector).tensor_tensor(wlo[:, slot], raw[:, slot], whi[:, slot].bitcast(F32), ALU.subtract).then_inc(lo_ready, 1)

    def products(outs, terms, first=True, last=True, before=None, after=None):
        for n, (wh, wl, xs) in enumerate(terms):
            if before:
                before(n)
            for m, w in enumerate((wh, wh, wl)):
                for b, out in enumerate(outs):
                    ins = nc.tensor.matmul(out, w, xs[b][m == 1], start=(first and n == 0 and m == 0),
                                           stop=(last and n == len(terms) - 1 and m == 2))
            if after and n < len(terms) - 1:
                after(n)
        return ins

    def halves(hi, lo, k):
        return [(hi[:, k, b * HALF:(b + 1) * HALF], lo[:, k, b * HALF:(b + 1) * HALF]) for b in (0, 1)]

    def unit_product(pe, u, slot, before=None, after=None):
        pe.wait_ge(lo_ready, u + 1)
        pe.wait_ge(psum_free, u + 1)
        products([pu[:, slot, b, 0:HALF] for b in (0, 1)],
                 [(whi[:, slot, k], wlo[:, slot, k], halves(xhi, xlo, k)) for k in range(KT)],
                 before=before, after=after).then_inc(tiles_done, 1)

    both = lambda slot: pu[:, slot, :, 0:HALF]
    in_two = lambda ap: ap.rearrange("p (b n) -> p b n", b=2)

    place = region(NR, NR_SIZE)
    sumsq = place("sumsq", [T])
    rinv = place("rinv", [T])
    squares = place("squares", [2, T])
    scaled = place("scaled", [4, T])
    sum_cleared = sem("sum_cleared")
    squared = sem("squared")
    squares_summed = primed["squares_summed"]
    summed = sem("summed")
    ln_done = sem("ln_done")
    rinv_ready = sem("rinv_ready")
    scaled_ready = sem("scaled_ready")
    scaled_hi = sem("scaled_hi")
    scaled_lo = [primed["scaled_lo0"], primed["scaled_lo1"]]
    y_stored = [primed["y_stored0"], primed["y_stored1"]]
    counts = {"squares": 0, "sums": 0, "norms": 0}
    row = lambda t, k: t[:, bass.ds(k, 1)].rearrange("p k n -> p (k n)")

    def clear_sum(eng, how=None):
        counts["sums"] += 1
        (how or nc.gpsimd).memset(sumsq[:], 0.0).then_inc(sum_cleared, 1)
        eng.wait_ge(sum_cleared, counts["sums"])

    def act_square(act, src, k, s, n, base):
        act.wait_ge(squares_summed, (k - s) + (base + PRIME))
        nc.scalar.activation(squares[:, s, 0:n], row(src, k), ACT.Square).then_inc(squared, 1)

    def sum_squares(eng, k, s, n, base, how=None):
        eng.wait_ge(squared, k + (base + 1))
        eng.wait_ge(squares_summed, k + (base + PRIME))
        (how or nc.gpsimd).tensor_tensor(sumsq[:, 0:n], sumsq[:, 0:n], squares[:, s, 0:n], ALU.add).then_inc(squares_summed, 1)

    def sum_tiles(pool, n, base):
        clear_sum(pool)
        with pool.Fori(0, KT // 2) as i:
            for s in (0, 1):
                sum_squares(pool, 2 * i + s, s, n, base)

    set_loaded = sem("set_loaded")
    mem_loaded = sem("mem_loaded")
    x_loaded = sem("x_loaded")
    with nc.Block() as block:
        @block.sync
        def _(sp):
            sp.dma_start(mem[:], a["memT"]).then_inc(mem_loaded, 16)
            for u in (0, 1):
                sp.dma_start(raw[:, u].rearrange("p k n -> p (k n)"), a["units"][u]).then_inc(raw_loaded[u], 16)
            sp.dma_start(consts[:], a["consts"]).then_inc(set_loaded, 16)
            sp.dma_start(vecs[:], a["vecs"]).then_inc(set_loaded, 16)
            sp.dma_start(x[:], a["xT"]).then_inc(x_loaded, 16)
            sp.wait_ge(set_loaded, 32)

        @block.gpsimd
        def _(pool):
            for s in primed.values():
                nc.gpsimd.engine_nop().then_inc(s, PRIME)
            nc.gpsimd.engine_nop().then_inc(psum_free, 2)

        @block.scalar
        def _(act):
            act.wait_ge(mem_loaded, 16)
            for k in range(KT):
                act_square(act, mem, k, k % 2, M, 0)
            split_hi(act, 0, 1, 0)

        @block.vector
        def _(dve):
            dve.wait_ge(squares_summed, PRIME)
            clear_sum(dve, nc.vector)
            for k in range(KT):
                sum_squares(dve, k, k % 2, M, 0, nc.vector)
            split_lo(dve, 0, 0)
    counts["squares"] += KT

    class Norm:

        def __init__(self, src, gain, n, hi=None, lo=None, final=None):
            self.src, self.gain, self.n, self.hi, self.lo, self.final = src, gain, n, hi, lo, final
            self.parts = [(0, n)] if n <= 512 else [(0, HALF), (HALF, n)]
            self.run = counts["norms"]
            counts["norms"] += 1
            self.base = self.run * KT

        def pe(self, pe):
            for b, (u, v) in enumerate(self.parts):
                ins = nc.tensor.matmul(pm[:, 0, b, 0:v - u], ones, sumsq[:, u:v], start=True, stop=True)
            ins.then_inc(summed, 1)

        def tile_ready(self, pe, k):
            pe.wait_ge(scaled_lo[k % 2], self.base // 2 + k // 2 + 1 + PRIME)

        def act(self, act):
            act.wait_ge(summed, self.run + 1)
            for b, (u, v) in enumerate(self.parts):
                ins = nc.scalar.activation(rinv[:, u:v], pm[:, 0, b, 0:v - u], ACT.Ln, scale=1.0 / D, bias=vecs[:, V_EPS:V_EPS + 1])
            ins.then_inc(ln_done, 1)
            act.wait_ge(ln_done, self.run + 1)
            nc.scalar.activation(rinv[:, 0:self.n], rinv[:, 0:self.n], ACT.Exp, scale=-0.5).then_inc(rinv_ready, 1)
            if self.final is None:
                with act.Fori(0, KT // 4) as i:
                    for s in range(4):
                        act.wait_ge(scaled_ready, 4 * i + (self.base + s + 1))
                        nc.scalar.copy(row(self.hi, 4 * i + s), scaled[:, s, 0:self.n]).then_inc(scaled_hi, 1)

        def lower(self, eng, how, i, s):
            eng.wait_ge(scaled_hi, 4 * i + (self.base + s + 1))
            how.tensor_tensor(row(self.lo, 4 * i + s), scaled[:, s, 0:self.n], row(self.hi, 4 * i + s).bitcast(F32), ALU.subtract).then_inc(scaled_lo[s % 2], 1)

        def dve(self, dve):
            dve.wait_ge(rinv_ready, self.run + 1)
            with dve.Fori(0, KT // 4) as i:
                for s in range(4):
                    if self.final is None:
                        dve.wait_ge(scaled_lo[s % 2], 2 * i + (self.base // 2 + PRIME))
                    else:
                        dve.wait_ge(y_stored[s % 2], 32 * i + PRIME)
                    nc.vector.scalar_tensor_tensor(scaled[:, s, 0:self.n], row(self.src, 4 * i + s), vecs[:, bass.ds(4 * i + (s + self.gain), 1)],
                                                   rinv[:, 0:self.n], ALU.mult, ALU.mult).then_inc(scaled_ready, 1)
                if self.final is None:
                    for s in (0, 2):
                        self.lower(dve, nc.vector, i, s)

        def sp(self, sp):
            if self.final is None:
                return
            with sp.Fori(0, KT // 4) as i:
                for s in range(4):
                    sp.wait_ge(scaled_ready, 4 * i + (self.base + s + 1))
                    sp.dma_start(self.final[bass.ds(4 * i + s, 1)].rearrange("k p n -> (k p) n"), scaled[:, s, 0:self.n]).then_inc(y_stored[s % 2], 16)
            for s in (0, 1):
                sp.wait_ge(y_stored[s], 8 * KT + PRIME)

        def pool(self, pool):
            if self.final is None:
                with pool.Fori(0, KT // 4) as i:
                    for s in (1, 3):
                        self.lower(pool, nc.gpsimd, i, s)

    def layer(base, n, pe_tile, act_tile=None, dve_tile=None, sp_tile=None, pool_tile=None, norm=None, pe_first=None, pool_first=None, sp_last=None):
        def loop(eng, before, tile, start=0):
            with eng.Fori(start, n // 2) as i:
                for s in (0, 1):
                    u, slot, fills = unit(base, i, s)
                    before(eng, i, s)
                    if tile:
                        tile(eng, u, slot, i, s)

        with nc.Block() as block:
            @block.sync
            def _(sp):
                def before(eng, i, s):
                    u, slot, _ = unit(base, i, s + 2)
                    load_unit(eng, u, slot)
                if norm:
                    norm.sp(sp)
                loop(sp, before, sp_tile)
                if sp_last:
                    sp_last(sp)

            @block.scalar
            def _(act):
                def before(eng, i, s):
                    u, slot, fills = unit(base, i, s + 1)
                    split_hi(eng, slot, fills, u - 1)
                if norm:
                    norm.act(act)
                loop(act, before, act_tile)

            @block.vector
            def _(dve):
                def before(eng, i, s):
                    u, slot, _ = unit(base, i, s + 1)
                    split_lo(eng, u, slot)
                if norm:
                    norm.dve(dve)
                loop(dve, before, dve_tile)

            @block.tensor
            def _(pe):
                nothing = lambda *_: None
                if norm:
                    norm.pe(pe)
                    for s in (0, 1):
                        u, slot, _ = unit(base, 0, s)
                        pe_first(pe, u, slot, (lambda k: norm.tile_ready(pe, k)) if s == 0 else None)
                    loop(pe, nothing, pe_tile, 1)
                else:
                    loop(pe, nothing, pe_tile)

            @block.gpsimd
            def _(pool):
                if pool_first:
                    pool_first(pool)
                if norm:
                    norm.pool(pool)
                if pool_tile:
                    loop(pool, lambda *_: None, pool_tile)

    place = region(WR + 4 * KT * M, W_SIZE - NR_SIZE - 4 * KT * M)
    k_out = place("k_out", [2, M])
    v_out = place("v_out", [2, 2, 512])
    k_stored = [primed["k_stored0"], primed["k_stored1"]]
    v_stored = primed["v_stored"]

    def pe_k(pe, u, slot, before=None):
        pe.wait_ge(lo_ready, u + 1)
        pe.wait_ge(psum_free, u + 1)
        products([pu[:, slot, 0, 0:M]],
                 [(whi[:, slot, k], wlo[:, slot, k], [(memhi[:, k], memlo[:, k])]) for k in range(KT)], before=before).then_inc(tiles_done, 1)

    def act_k(act, u, slot, i, s):
        finished(act, u + 1)
        act.wait_ge(k_stored[s], 16 * i + PRIME)
        nc.scalar.copy(k_out[:, s], pu[:, slot, 0, 0:M]).then_inc(psum_free, 1)

    def sp_k(sp, u, slot, i, s):
        taken(sp, u)
        sp.dma_start(a["mkT"][bass.ds(2 * i + s, 1)].rearrange("k p n -> (k p) n"), k_out[:, s]).then_inc(k_stored[s], 16)

    layer(MK0, KT, lambda pe, u, slot, i, s: pe_k(pe, u, slot), act_k, None, sp_k, norm=Norm(mem, V_MEM, M, memhi, memlo), pe_first=pe_k)

    squares_before = counts["squares"]
    counts["squares"] += KT
    with nc.Block() as block:
        @block.sync
        def _(sp):
            for s in (0, 1):
                sp.wait_ge(k_stored[s], 16 * KT // 2 + PRIME)
            with sp.Fori(0, 2) as i:
                for r in (0, 1):
                    for j in range(4):
                        load_unit(sp, i * 8 + (MV0 + 4 * r + j + 2), (MV0 + j) % 2)
                    taken(sp, i * 8 + (MV0 + 4 * r + 3))
                    sp.dma_start(a["mv"][:, :, bass.ds(i * 1024 + 512 * r, 512)], v_out[:, r]).then_inc(v_stored, 16)
            sp.wait_ge(v_stored, 16 * 4 + PRIME)

        @block.tensor
        def _(pe):
            with pe.Fori(0, 2) as i:
                for r in (0, 1):
                    pe.wait_ge(psum_free, i * 8 + (MV0 + 4 * r - 2))
                    for j in range(4):
                        slot = (MV0 + j) % 2
                        pe.wait_ge(lo_ready, i * 8 + (MV0 + 4 * r + j + 1))
                        for b in (0, 1):
                            at = slice(b * P, (b + 1) * P)
                            wide = lambda w: w[:, slot].rearrange("p k n -> p (k n)").rearrange("p (k n) -> p k n", k=4)
                            ins = products([pu[:, r, b]],
                                           [(memhi[:, 4 * j + k, at], memlo[:, 4 * j + k, at], [(wide(whi)[:, k], wide(wlo)[:, k])]) for k in range(4)],
                                           first=(j == 0), last=(j == 3))
                        ins.then_inc(tiles_done, 1)

        @block.scalar
        def _(act):
            act.wait_ge(x_loaded, 16)
            with act.Fori(0, 2) as i:
                for r in (0, 1):
                    for j in range(4):
                        c = 4 * r + j
                        act_square(act, x, i * 8 + c, j % 2, T, squares_before)
                        split_hi(act, (MV0 + j + 1) % 2, i * 4 + ((MV0 + c + 1) // 2 + 1), i * 8 + (MV0 + c))
                    finished(act, i * 8 + (MV0 + 4 * r + 4))
                    if r == 0:
                        act.wait_ge(v_stored, 32 * i + PRIME)
                    nc.scalar.copy(v_out[:, r], pu[:, r]).then_inc(psum_free, 4)

        @block.gpsimd
        def _(pool):
            sum_tiles(pool, T, squares_before)

        @block.vector
        def _(dve):
            with dve.Fori(0, 2) as i:
                for c in range(8):
                    split_lo(dve, i * 8 + (MV0 + c + 1), (MV0 + c + 1) % 2)

    norm_mix = Norm(x, V_MIX, T, xhi, xlo)

    place = region(WR, W_SIZE)
    CL = 3 + TP + 3 + TS
    ext = place("ext", [2, CL])
    acc = [place(f"acc{i}", [CL - 3]) for i in range(4)]
    convd = place("convd", [2, TPAD])
    chist = place("chist", [24, 3])
    conv_new = place("conv_new", [24, 2, 3])
    PH = 15
    PL = PH + TP + PH + TS
    phist = place("phist", [8, PH])
    pool_new = place("pool_new", [8, 2, PH])
    pext = place("pext", [2, PL])
    wins = [place(f"win{i}", [PL]) for i in range(2)]
    mixes = [place(f"mix{i}", [2, T]) for i in (0, 1)]
    wpool = place("wpool", [KT, P])
    abT = place("abT", [TPAD])
    NG = NCH * HEADS
    ab = place("ab", [NCH, 16])
    gt = [place(f"gt{i}", [NG]) for i in range(6)]

    def act_z(act, u, slot, i, s):
        finished(act, u + 1)
        nc.scalar.activation(cat[:, bass.ds(2 * i + s + 8, 1)].rearrange("p k (b n) -> p (k b) n", b=2), both(slot), ACT.Silu).then_inc(psum_free, 1)

    pe_linear = lambda pe, u, slot, i, s: unit_product(pe, u, slot)
    def clear_history(pool):
        nc.gpsimd.memset(pext[:], 0.0)
        nc.gpsimd.memset(ext[:], 0.0)
        nc.gpsimd.memset(convd[:], 0.0)

    layer(Z0, 8, pe_linear, act_z, norm=norm_mix, pe_first=unit_product, pool_first=clear_history)

    pool_loaded = sem("pool_loaded")
    pext_used = sem("pext_used")
    mix_ready = sem("mix_ready")
    mixed = sem("mixed")
    mixed_out = sem("mixed_out")
    pool_chain = sem("pool_chain")
    pool_stored = sem("pool_stored")
    ab_cleared = sem("ab_cleared")
    ab_turned = sem("ab_turned")
    g_act = sem("g_act")
    g_chain = sem("g_chain")
    decay_ready = sem("decay_ready")
    decay_summed = sem("decay_summed")
    gcum_ready = sem("gcum_ready")

    def dve_decays(dve):
        chain = Chain(dve, g_chain)
        v3 = lambda t: t[:].rearrange("p (c h) -> p c h", c=NCH)
        dve.wait_ge(ab_turned, 1)
        chain.link(nc.vector.tensor_copy(ab[:], pm[:, 0, 0, 0:16 * NCH].rearrange("p (c n) -> p c n", c=NCH)))
        chain.link(nc.vector.tensor_tensor(v3(gt[0]), ab[:, :, 0:8], vecs[:, V_DT:V_DT + 8].unsqueeze(1).broadcast_to([P, NCH, 8]), ALU.add))
        chain.link(nc.vector.tensor_scalar(gt[4][:], gt[0][:], -1.0, None, ALU.mult))
        chain.link(nc.vector.tensor_tensor(gt[1][:], gt[0][:], gt[4][:], ALU.min))
        dve.wait_ge(g_act, 3)
        chain.link(nc.vector.scalar_tensor_tensor(gt[4][:], gt[0][:], 0.0, gt[3][:], ALU.max, ALU.add))
        chain.link(nc.vector.scalar_tensor_tensor(v3(gt[0]), v3(gt[4]), -1.0, gt[5][:, 0:8].unsqueeze(1).broadcast_to([P, NCH, 8]), ALU.mult, ALU.mult))
        valid = consts[:, C_VALID:C_VALID + NG]
        nc.vector.tensor_tensor(gcol[:], gt[0][:], valid, ALU.mult).then_inc(decay_ready, 1)
        chain.link(nc.vector.tensor_tensor(gt[1][:], beta[:], valid, ALU.mult))
        chain.link(nc.vector.tensor_copy(beta[:], gt[1][:]))

    def act_decays(act):
        act.wait_ge(g_chain, 4)
        nc.scalar.activation(gt[2][:], gt[1][:], ACT.Exp).then_inc(g_act, 1)
        act.wait_ge(g_act, 1)
        nc.scalar.activation(gt[3][:], gt[2][:], ACT.Ln, bias=1.0).then_inc(g_act, 1)
        nc.scalar.activation(gt[5][:, 0:HEADS], vecs[:, V_ALOG:V_ALOG + HEADS], ACT.Exp)
        nc.scalar.activation(beta[:].rearrange("p (c h) -> p c h", c=NCH), ab[:, :, 8:16], ACT.Sigmoid).then_inc(g_act, 1)

    with nc.Block() as block:
        S0 = PH + TP + PH

        @block.sync
        def _(sp):
            sp.dma_start(phist[:], a["phist"]).then_inc(pool_loaded, 16)
            sp.dma_start(chist[:], a["chist"]).then_inc(pool_loaded, 16)
            sp.dma_start(wpool[:], a["wpool"]).then_inc(pool_loaded, 16)
            load_unit(sp, AB0 + 2, AB0 % 2)
            with sp.Fori(0, 4) as i:
                for s in (0, 1):
                    u, slot, _ = unit(POOL0, i, s + 2)
                    load_unit(sp, u, slot)
            sp.wait_ge(pext_used, 8)
            sp.dma_start(a["pool_new"], pool_new[:]).then_inc(pool_stored, 16)
            sp.wait_ge(pool_stored, 16)

        @block.gpsimd
        def _(pool):
            nc.gpsimd.memset(abT[:], 0.0).then_inc(ab_cleared, 1)

        @block.tensor
        def _(pe):
            unit_product(pe, AB0, AB0 % 2)
            for g in range(5):
                if g < 4:
                    for s in (0, 1):
                        u, slot, _ = unit(POOL0, g, s)
                        unit_product(pe, u, slot)
                        if (g, s) == (0, 0):
                            taken(pe, AB0)
                            for c in range(NCH):
                                ins = nc.tensor.transpose(pm[:, 0, 0, 16 * c:16 * c + 16], abT[0:16, c * P:(c + 1) * P], ident[0:16, 0:16])
                            ins.then_inc(ab_turned, 1)
                        elif (g, s) == (0, 1):
                            pe.wait_ge(decay_ready, 1)
                            nc.tensor.matmul(pm[:, 1, 0, 0:NG], cum, gcol[:], start=True, stop=True).then_inc(decay_summed, 1)
                g -= 1
                if g < 0:
                    continue
                pe.wait_ge(mix_ready, 2 * g + 2)
                pe.wait_ge(pool_loaded, 48)
                for d in (0, 1):
                    if g:
                        pe.wait_ge(mixed_out, 2 * (g - 1) + d + 1)
                    else:
                        pe.wait_ge(gcum_ready, 1)
                    for b in (0, 1):
                        for c in (0, 1):
                            ins = nc.tensor.matmul(pm[:, d, b, 0:HALF], wpool[:, 4 * g + 2 * c + d], mixes[g % 2][:, c, b * HALF:(b + 1) * HALF],
                                                   start=(c == 0), stop=(c == 1))
                    ins.then_inc(mixed, 1)

        @block.scalar
        def _(act):
            split_hi(act, POOL0 % 2, POOL0 // 2 + 1, AB0)
            act.wait_ge(ab_cleared, 1)
            finished(act, AB0 + 1)
            for b in (0, 1):
                ins = nc.scalar.copy(abT[0:16, b * HALF:(b + 1) * HALF], pu[0:16, AB0 % 2, b, 0:HALF])
            ins.then_inc(psum_free, 1)
            for g in range(5):
                for s in (0, 1) if g < 4 else ():
                    j = 2 * g + s
                    u, slot, fills = unit(POOL0, g, s + 1)
                    split_hi(act, slot, fills, u - 1)
                    u, slot, _ = unit(POOL0, g, s)
                    finished(act, u + 1)
                    if g:
                        act.wait_ge(pext_used, j - 1)
                    act.wait_ge(pool_loaded, 48)
                    nc.scalar.copy(pext[:, s, PH:PH + HALF], pu[:, slot, 0, 0:HALF])
                    nc.scalar.copy(pext[:, s, PH + HALF:PH + TP], pu[:, slot, 1, 0:TP - HALF])
                    nc.scalar.copy(pext[:, s, S0 - PH:S0], phist[:, j])
                    nc.scalar.copy(pext[:, s, S0:PL], pu[:, slot, 1, TP - HALF:HALF]).then_inc(psum_free, 1)
                    if (g, s) == (0, 0):
                        act_decays(act)
                    elif (g, s) == (1, 0):
                        act.wait_ge(gcum_ready, 1)
                        nc.scalar.activation(egcum[:], gcum[:], ACT.Exp)
                g -= 1
                for d in (0, 1) if g >= 0 else ():
                    act.wait_ge(mixed, 2 * g + d + 1)
                    scale = vecs[:, V_POOL + 2 * g + d:V_POOL + 2 * g + d + 1]
                    nc.scalar.activation(in_two(cat[:, 2 * g + d]), pm[:, d, :, 0:HALF], ACT.Copy, scale=scale).then_inc(mixed_out, 1)

        @block.vector
        def _(dve):
            chain = Chain(dve, pool_chain)
            split_lo(dve, POOL0, POOL0 % 2)
            for g in range(4):
                for s in (0, 1):
                    j = 2 * g + s
                    u, slot, _ = unit(POOL0, g, s + 1)
                    split_lo(dve, u, slot)
                    taken(dve, POOL0 + j)
                    e = pext[:, s]
                    cur = e
                    for l in range(g + 1):
                        sh = 1 << l
                        nxt = wins[l % 2]
                        chain.link(nc.vector.tensor_tensor(nxt[:, 2 * sh - 1:PL], cur[:, 2 * sh - 1:PL], cur[:, sh - 1:PL - sh], ALU.add))
                        cur = nxt
                    if g >= 2:
                        dve.wait_ge(mixed, 2 * g - 2)
                    w = 2 << g
                    chain.link(nc.vector.tensor_tensor(wins[(g + 1) % 2][:, 0:16], cur[:, PH:PH + 16], consts[:, C_CNT + 16 * g:C_CNT + 16 * g + 16], ALU.mult))
                    nc.vector.tensor_tensor(mixes[g % 2][:, s, 0:16], wins[(g + 1) % 2][:, 0:16], e[:, PH:PH + 16], ALU.subtract)
                    nc.vector.scalar_tensor_tensor(mixes[g % 2][:, s, 16:TP], cur[:, PH + 16:PH + TP], 1.0 / w, e[:, PH + 16:PH + TP], ALU.mult, ALU.subtract)
                    nc.vector.scalar_tensor_tensor(mixes[g % 2][:, s, TP:T], cur[:, S0:PL], 1.0 / w, e[:, S0:PL], ALU.mult, ALU.subtract).then_inc(mix_ready, 1)
                    nc.vector.tensor_copy(pool_new[:, j, 0], e[:, TP:TP + PH])
                    nc.vector.tensor_copy(pool_new[:, j, 1], e[:, PL - PH:PL]).then_inc(pext_used, 1)
                    dve.wait_ge(pext_used, j + 1)
                    if j == 0:
                        dve_decays(dve)
                    elif j == 1:
                        dve.wait_ge(decay_summed, 1)
                        nc.vector.tensor_copy(gcum[:], pm[:, 1, 0, 0:NG]).then_inc(gcum_ready, 1)

    conv_done = primed["conv_done"]
    silu_done = primed["silu_done"]
    qkv_stored = [primed["qkv_stored0"], primed["qkv_stored1"]]
    conv_chain = sem("conv_chain")
    hist_kept = primed["hist_kept"]
    conv_stored = sem("conv_stored")

    def act_qkv(act, u, slot, i, s):
        j = 2 * i + s
        finished(act, u + 1)
        act.wait_ge(conv_done, 2 * i + PRIME)
        act.wait_ge(hist_kept, 2 * i + PRIME)
        nc.scalar.copy(ext[:, s, 3:3 + HALF], pu[:, slot, 0, 0:HALF])
        nc.scalar.copy(ext[:, s, 3 + HALF:3 + TP], pu[:, slot, 1, 0:TP - HALF])
        nc.scalar.copy(ext[:, s, 3 + TP:6 + TP], chist[:, bass.ds(j, 1)].rearrange("p j n -> p (j n)"))
        nc.scalar.copy(ext[:, s, 6 + TP:CL], pu[:, slot, 1, TP - HALF:HALF]).then_inc(psum_free, 1)
        act.wait_ge(conv_done, j + (1 + PRIME))
        act.wait_ge(qkv_stored[s], 16 * i + PRIME)
        nc.scalar.activation(convd[:, s, 0:TP], acc[3][:, 0:TP], ACT.Silu)
        nc.scalar.activation(convd[:, s, TP:T], acc[3][:, TP + 3:TP + 3 + TS], ACT.Silu).then_inc(silu_done, 1)

    def pool_qkv(pool, u, slot, i, s):
        j = 2 * i + s
        taken(pool, u)
        at = bass.ds(j, 1)
        nc.gpsimd.tensor_copy(conv_new[:, at, 0].rearrange("p j n -> p (j n)"), ext[:, s, TP:TP + 3])
        nc.gpsimd.tensor_copy(conv_new[:, at, 1].rearrange("p j n -> p (j n)"), ext[:, s, CL - 3:CL]).then_inc(hist_kept, 1)

    def sp_qkv(sp, u, slot, i, s):
        sp.wait_ge(silu_done, 2 * i + (s + 1 + PRIME))
        sp.dma_start(qkv_s[bass.ds(2 * i + s, 1)].rearrange("k p n -> (k p) n"), convd[:, s]).then_inc(qkv_stored[s], 16)

    chains = {}

    def dve_qkv(dve, u, slot, i, s):
        j = 2 * i + s
        if s == 0:
            chains["conv"] = Chain(dve, conv_chain)
            chains["conv"].enter(i, 6)
        link = chains["conv"].link
        taken(dve, u)
        n = CL - 3
        tap = lambda q: vecs[:, bass.ds(j * 4 + (V_CONV + q), 1)]
        dve.wait_ge(silu_done, j + PRIME)
        link(nc.vector.tensor_scalar(acc[0][:], ext[:, s, 0:n], tap(0), None, ALU.mult))
        link(nc.vector.scalar_tensor_tensor(acc[1][:], ext[:, s, 1:1 + n], tap(1), acc[0][:], ALU.mult, ALU.add))
        link(nc.vector.scalar_tensor_tensor(acc[2][:], ext[:, s, 2:2 + n], tap(2), acc[1][:], ALU.mult, ALU.add))
        nc.vector.scalar_tensor_tensor(acc[3][:], ext[:, s, 3:3 + n], tap(3), acc[2][:], ALU.mult, ALU.add).then_inc(conv_done, 1)

    def store_history(sp):
        sp.wait_ge(hist_kept, 24 + PRIME)
        sp.dma_start(a["conv_new"], conv_new[:]).then_inc(conv_stored, 16)
        for s in (0, 1):
            sp.wait_ge(qkv_stored[s], 16 * 12 + PRIME)
        sp.wait_ge(conv_stored, 16)

    layer(QKV0, 24, pe_linear, act_qkv, dve_qkv, sp_qkv, pool_qkv, sp_last=store_history)

    s_stored = sem("s_stored")
    S_sample = deltanet(nc, es, sem, region, a, dict(
        s_stored=s_stored,
        HR=HR, H_SIZE=H_SIZE, WR=WR, W_SIZE=W_SIZE, consts=consts, vecs=vecs, gcol=gcol, beta=beta, gcum=gcum, egcum=egcum, cat=cat,
        SLOT=SLOT, qkv_s=qkv_s, ident=ident, ones=ones, cum=cum, primed=primed))

    x_back = sem("x_back")

    class Split:
        cat_hi = sem("cat_hi")
        cat_lo = [sem("cat_lo0"), sem("cat_lo1")]

        def sp(self, sp):
            sp.dma_start(a["dn_sample"].rearrange("h p n -> p h n"), S_sample[:]).then_inc(s_stored, 16)
            for j in range(4):
                for s in (0, 1):
                    sp.wait_ge(self.cat_lo[s], KT // 8 * (j + 1))
                at = slice(KT // 4 * j, KT // 4 * (j + 1))
                sp.dma_start(x[:, at], a["xT"][:, at]).then_inc(x_back, 16)
            sp.wait_ge(s_stored, 32)

        def pe(self, pe):
            pass

        def tile_ready(self, pe, k):
            pe.wait_ge(self.cat_lo[k % 2], k // 2 + 1)

        def act(self, act):
            with act.Fori(0, KT) as k:
                nc.scalar.copy(row(xhi, k), row(cat, k)).then_inc(self.cat_hi, 1)

        def lower(self, eng, how, s):
            with eng.Fori(0, KT // 2) as i:
                k = 2 * i + s
                eng.wait_ge(self.cat_hi, 2 * i + (s + 1))
                how.tensor_tensor(row(xlo, k), row(cat, k), row(xhi, k).bitcast(F32), ALU.subtract).then_inc(self.cat_lo[s], 1)

        def dve(self, dve):
            self.lower(dve, nc.vector, 0)

        def pool(self, pool):
            self.lower(pool, nc.gpsimd, 1)

    def residual_layer(base, split=None):
        before = counts["squares"]
        counts["squares"] += KT

        def dve_residual(dve, u, slot, i, s):
            finished(dve, u + 1)
            if split:
                dve.wait_ge(x_back, 16 * 4)
            at = x[:, bass.ds(2 * i + s, 1)].rearrange("p k (b n) -> p (k b) n", b=2)
            nc.vector.tensor_tensor(at, both(slot), at, ALU.add).then_inc(psum_free, 1)

        def act_residual(act, u, slot, i, s):
            taken(act, u)
            act_square(act, x, 2 * i + s, s, T, before)

        def pool_residual(pool, u, slot, i, s):
            sum_squares(pool, 2 * i + s, s, T, before)

        layer(base, KT, pe_linear, act_residual, dve_residual, None, pool_residual, norm=split, pe_first=unit_product, pool_first=clear_sum)

    residual_layer(OUT0, Split())

    q_stored = [primed["q_stored0"], primed["q_stored1"]]
    place = region(WR, W_SIZE)
    q_out = place("q_out", [2, TPAD])
    pad_cleared = sem("pad_cleared")

    def to_scratch(base, norm, run):
        def clear_pad(pool):
            nc.gpsimd.memset(q_out[:, :, T:TPAD], 0.0).then_inc(pad_cleared, 1)

        def act_q(act, u, slot, i, s):
            finished(act, u + 1)
            act.wait_ge(q_stored[s], 16 * i + (run * 8 * KT + PRIME))
            nc.scalar.copy(in_two(q_out[:, s, 0:T]), both(slot)).then_inc(psum_free, 1)

        def sp_q(sp, u, slot, i, s):
            taken(sp, u)
            sp.wait_ge(pad_cleared, run + 1)
            sp.dma_start(q_s[bass.ds(2 * i + s, 1)].rearrange("k p n -> (k p) n"), q_out[:, s]).then_inc(q_stored[s], 16)

        layer(base, KT, pe_linear, act_q, None, sp_q, norm=norm, pe_first=unit_product, pool_first=clear_pad)
        with nc.Block() as block:
            @block.sync
            def _(sp):
                for s in (0, 1):
                    sp.wait_ge(q_stored[s], (run + 1) * 8 * KT + PRIME)

    to_scratch(MQ0, Norm(x, V_XATTN, T, xhi, xlo), 0)
    attention(nc, es, sem, region, a, dict(WR=WR, W_SIZE=W_SIZE, pu=pu, pm=pm, q_s=q_s, xhi=xhi, xlo=xlo, ident=ident))
    residual_layer(MO0)

    to_scratch(PQ0, Norm(x, V_FFN, T, xhi, xlo), 1)

    STRETCH = 6
    ROUTED = NCH * STRETCH
    TCH = T // TC
    CHUNK_UNITS = 4
    TABLED = ROUTED + CHUNK_UNITS * TCH
    place = region(WR, W_SIZE)
    h_out = place("h_out", [2, T])
    rowT, colT = place("rowT", [TPAD]), place("colT", [TPAD])
    place_gates = region(CR + 4 * C_LEV, 4 * LEVELS * P)
    gate_hi, gate_lo = place_gates("gate_hi", [TPAD], F32R), place("gate_lo", [TPAD], F32R)
    used = 4 * (3 * TPAD + 2 * T)
    place = region(WR + used, W_SIZE - used)
    qt = place("qt", [KT, P])
    keys = place("keys", [KT, P])
    place_sc = region(WR + used + 8 * KT * P, W_SIZE - used - 8 * KT * P)
    sc = place("sc", [KT, P])
    cand = place_sc("cand", [8, TOPK * TOPK])
    pick = cand
    v1 = place("v1", [KT, TOPK])
    i1 = place("i1", [KT, TOPK], U32)
    f1 = place("f1", [KT, TOPK])
    v2 = place("v2", [8, TOPK])
    i2 = place("i2", [8, TOPK], U32)
    ia, ib = place("ia", [8, TOPK], U32), place("ib", [8, TOPK], U32)
    fa, fb = place("fa", [8, TOPK]), place("fb", [8, TOPK])
    row_key, col_key = place("row_key", [8, TOPK]), place("col_key", [8, TOPK])
    ex, gate = place("ex", [8, TOPK]), place("gate", [8, TOPK])
    sm, rs, pause = place("rt_sm", [8]), place("rt_rs", [8]), place("pause", [1])
    place = region(WR + used, W_SIZE - used)
    hot_r = place("hot_r", [2, 4, 2, P], F32R)
    hot_c = place("hot_c", [2, 4, P], F32R)
    lower_sums = place("lower_sums", [2, 4, NGRP, GRP])
    place = region(XR, HR - XR)
    table = [place(f"table{i}", [NGRP, TC, GRP]) for i in (0, 1)]
    iota = consts[:, C_IOTA:C_IOTA + P]

    place = region(WR + 8 * T, W_SIZE - 8 * T)
    h_in = [place(f"h_in{i}", [GRP, T]) for i in (0, 1)]
    gate_in = [place(f"gate_in{i}", [T, GRP]) for i in (0, 1)]
    coef = place("coef", [GRP, T])

    keys_loaded = sem("keys_loaded")
    queries_loaded = sem("queries_loaded")
    scored = primed["scored"]
    less_max = sem("less_max")
    exped = sem("exped")
    slots_ready = sem("slots_ready")
    slots_turned = sem("slots_turned")
    slots_taken = primed["slots_taken"]
    route_chain = sem("route_chain")
    rows_hot = sem("rows_hot")
    cols_hot = sem("cols_hot")
    lower_out = sem("lower_out")
    x_parked = sem("x_parked")
    x_restored = sem("x_restored")
    dense = sem("dense")
    table_filled = primed["table_filled"]
    table_stored = [primed["table_stored0"], primed["table_stored1"]]
    h_stored = [primed["h_stored0"], primed["h_stored1"]]

    def hidden_unit(first, per, i, m):
        at = EXP0 + first + m
        return i * per + at, at % 2, i * (per // 2) + at // 2, i * (per // 2) + (first + m) // 2

    def hidden_sp(sp, *at):
        u, slot, _, _ = hidden_unit(*at)
        s = at[-1] % 2
        load_unit(sp, u + 2, slot)
        taken(sp, u)
        sp.dma_start(h_s[bass.ds(u - EXP0, 1)].rearrange("k p n -> (k p) n"), h_out[:, s]).then_inc(h_stored[s], 16)

    def hidden_act(act, *at):
        u, slot, pairs, uses = hidden_unit(*at)
        s = at[-1] % 2
        split_hi(act, 1 - slot, pairs + 1 + slot, u)
        finished(act, u + 1)
        act.wait_ge(h_stored[s], 16 * uses + PRIME)
        nc.scalar.activation(in_two(h_out[:, s]), both(slot), ACT.Gelu).then_inc(psum_free, 1)

    def hidden_pool(pool, *at):
        u, slot, _, _ = hidden_unit(*at)
        split_lo(pool, u + 1, 1 - slot, nc.gpsimd)

    def hidden_pe(pe, *at, before=None):
        u, slot, _, _ = hidden_unit(*at)
        unit_product(pe, u, slot, before=before)

    def pe_scores(pe, t):
        pe.wait_ge(keys_loaded, 16)
        pe.wait_ge(queries_loaded, 16 * t + 16)
        pe.wait_ge(slots_taken, t + PRIME)
        for k in range(KT):
            ins = nc.tensor.matmul(pm[:, k // 8, (k // 4) % 2, (k % 4) * P:(k % 4 + 1) * P], qt[:, k], keys[:, k], start=True, stop=True)
        ins.then_inc(scored, 1)

    def pe_turn(pe, t):
        pe.wait_ge(slots_ready, t + 1)
        for n, src in enumerate((gate, row_key, col_key)):
            ins = nc.tensor.transpose(pm[:, 0, 0, n * P:(n + 1) * P], src[:].rearrange("p h k -> p (h k)"), ident)
        ins.then_inc(slots_turned, 1)

    def dve_route(dve, t, chain):
        link = chain.link
        v = nc.vector

        def settle(ins):
            link(ins)
            v.memset(pause[:], 0.0)
        dve.wait_ge(scored, t + (1 + PRIME))
        settle(v.tensor_copy(sc[:].rearrange("p k n -> p (k n)"), pm[:].rearrange("p a b n -> p (a b n)")))
        for vals, n, best, at in ((sc, KT, v1, i1), (cand, 8, v2, i2)):
            if n == 8:
                settle(v.tensor_tensor(cand[:].rearrange("p h (i j) -> p h i j", i=TOPK),
                                       v1[:, 0:KT:2].unsqueeze(3).broadcast_to([P, 8, TOPK, TOPK]),
                                       v1[:, 1:KT:2].unsqueeze(2).broadcast_to([P, 8, TOPK, TOPK]), ALU.add))
            for r in (0, 1):
                o = slice(8 * r, 8 * r + 8)
                for k in range(n):
                    ins = v.max(best[:, k, o], vals[:, k])
                settle(ins)
                for k in range(n):
                    ins = v.max_index(at[:, k, o], best[:, k, o], vals[:, k])
                if r == 0:
                    settle(ins)
                    for k in range(n):
                        ins = v.match_replace(vals[:, k], best[:, k, o], vals[:, k], LOWEST)
                settle(ins)
        v.tensor_scalar(ia[:], i2[:], 4, None, ALU.logical_shift_right)
        v.tensor_scalar(ib[:], i2[:], 15, None, ALU.bitwise_and)
        link(v.tensor_copy(f1[:], i1[:]))
        v.tensor_copy(fa[:], ia[:])
        link(v.tensor_copy(fb[:], ib[:]))
        steps = iota[:, 0:TOPK].unsqueeze(1).broadcast_to([P, 128, TOPK])
        for place_, half, key in ((fa, 0, row_key), (fb, 1, col_key)):
            pk = pick[:].rearrange("p h (k n) -> p (h k) n", k=TOPK)
            link(v.tensor_tensor(pk, place_[:].rearrange("p h k -> p (h k)").unsqueeze(2).broadcast_to([P, 128, TOPK]), steps, ALU.is_equal))
            p4 = pick[:].rearrange("p h (k n) -> p h k n", k=TOPK)
            link(v.tensor_tensor(p4, p4, f1[:, half:KT:2].unsqueeze(2).broadcast_to([P, 8, TOPK, TOPK]), ALU.mult))
            ins = v.tensor_reduce(key[:].rearrange("p h k -> p (h k)"), pk, AX_X, ALU.add)
            if half == 0:
                link(ins)
        link(v.tensor_copy(rs[:], v2[:, :, 0]))
        v.tensor_tensor(v2[:], v2[:], rs[:].unsqueeze(2).broadcast_to([P, 8, TOPK]), ALU.subtract).then_inc(less_max, 1)
        dve.wait_ge(exped, t + 1)
        link(v.tensor_reduce(sm[:], ex[:], AX_X, ALU.add))
        link(v.reciprocal(rs[:], sm[:]))
        v.tensor_tensor(gate[:], ex[:], rs[:].unsqueeze(2).broadcast_to([P, 8, TOPK]), ALU.mult).then_inc(slots_ready, 1)
        dve.wait_ge(slots_turned, t + 1)
        to = bass.ds(t * P, P)
        v.tensor_copy(rowT[:, to], pm[:, 0, 0, P:2 * P])
        v.tensor_copy(colT[:, to], pm[:, 0, 0, 2 * P:3 * P])
        link(v.tensor_copy(gate_hi[:, to], pm[:, 0, 0, 0:P]))
        v.tensor_tensor(gate_lo[:, to], pm[:, 0, 0, 0:P], gate_hi[:, to].bitcast(F32), ALU.subtract).then_inc(slots_taken, 1)
    ROUTE_LINKS = 23

    QUADS = TC // 4

    def pe_quad(pe, c, k):
        n = c * QUADS + k
        pe.wait_ge(rows_hot, n + 1)
        pe.wait_ge(cols_hot, n + 1)
        pe.wait_ge(table_filled, c * QUADS + (max(k - 1, 0) + PRIME))
        for i in range(4):
            ins = nc.tensor.matmul(pm[:, k % 2, i // 2, (i % 2) * 2 * P:(i % 2 + 1) * 2 * P], hot_c[:, k % 2, i],
                                   hot_r[:, k % 2, i].rearrange("p two n -> p (two n)"), start=True, stop=True)
        ins.then_inc(dense, 1)

    def dve_chunk_of_table(dve, c, s, uses):
        def fill(k):
            dve.wait_ge(dense, c * QUADS + (k + 1))
            if k == 0:
                dve.wait_ge(table_stored[s], 16 * uses + PRIME)
            sums = pm[:, k % 2].rearrange("p b n -> p (b n)").rearrange("p (t two g i) -> p t two g i", t=4, two=2, g=NGRP)
            nc.vector.tensor_copy(lower_sums[:, k % 2], sums[:, :, 1]).then_inc(lower_out, 1)
            dve.wait_ge(lower_out, c * QUADS + (k + 1))
            nc.vector.tensor_tensor(table[s][:, :, 4 * k:4 * k + 4, :].rearrange("p g t i -> p t g i"),
                                    sums[:, :, 0], lower_sums[:, k % 2], ALU.add).then_inc(table_filled, 1)

        for k in range(QUADS):
            for i in range(4):
                at = bass.ds(c * TC + (4 * k + i), 1)
                for side, gates in enumerate((gate_hi, gate_lo)):
                    ins = nc.vector.tensor_scalar(hot_r[:, k % 2, i, side], iota, rowT[:, at], gates[:, at].bitcast(F32), ALU.is_equal, ALU.mult)
            ins.then_inc(rows_hot, 1)
            nc.vector.tensor_tensor(hot_c[:, k % 2], iota.unsqueeze(1).broadcast_to([P, 4, P]),
                                    colT[:, bass.ds(c * TC + 4 * k, 4)].unsqueeze(2).broadcast_to([P, 4, P]), ALU.is_equal).then_inc(cols_hot, 1)
            if k:
                fill(k - 1)
        fill(QUADS - 1)

    group_loaded = [sem("group_loaded0"), sem("group_loaded1")]
    coef_ready = sem("coef_ready")
    chi_ready = sem("chi_ready")
    clo_ready = sem("clo_ready")

    def load_group(sp, g, s):
        sp.dma_start(h_in[s][:], h_s[bass.ds(g * GRP, GRP)].rearrange("k p n -> p k n")).then_inc(group_loaded[s], 16)
        sp.dma_start(gate_in[s][:].rearrange("p t i -> p (t i)"), gate_s[bass.ds(g, 1)].rearrange("g p n -> (g p) n")).then_inc(group_loaded[s], 16)

    def pool_gate(pool, g, s, fills):
        pool.wait_ge(group_loaded[s], 32 * fills)
        for q in range(GRP):
            nc.gpsimd.tensor_tensor(coef[:, q], h_in[s][:, q], gate_in[s][:, :, q], ALU.mult).then_inc(coef_ready, 1)

    with nc.Block() as block:
        @block.sync
        def _(sp):
            def load_queries(t):
                sp.dma_start(qt[:], q_s[:, :, bass.ds(t * P, P)].rearrange("k p n -> p k n")).then_inc(queries_loaded, 16)

            def table_chunk(c, first, per, i, s, m):
                for j in range(CHUNK_UNITS):
                    hidden_sp(sp, first, per, i, m + j)
                sp.wait_ge(table_filled, c * QUADS + (QUADS + PRIME))
                sp.dma_start(gate_s[:, :, bass.ds(c * (TC * GRP), TC * GRP)].rearrange("g p n -> p g n"),
                             table[s][:].rearrange("p g t i -> p g (t i)")).then_inc(table_stored[s], 16)

            sp.dma_start(keys[:], a["keys"]).then_inc(keys_loaded, 16)
            load_queries(0)
            sp.dma_start(x_s, x[:]).then_inc(x_parked, 16)
            with sp.Fori(0, NCH - 1) as t:
                for m in range(STRETCH):
                    hidden_sp(sp, 0, STRETCH, t, m)
                    if m == 1:
                        sp.wait_ge(scored, t + (1 + PRIME))
                        load_queries(t + 1)
            for m in range(STRETCH):
                hidden_sp(sp, 0, STRETCH, NCH - 1, m)
            with sp.Fori(0, TCH // 2) as c:
                for s in (0, 1):
                    table_chunk(c * 2 + s, ROUTED, 2 * CHUNK_UNITS, c, s, CHUNK_UNITS * s)
            table_chunk(TCH - 1, ROUTED, CHUNK_UNITS, TCH - 1, 0, 0)
            for m in (0, 1):
                hidden_sp(sp, TABLED, 2, 0, m)
            sp.wait_ge(table_stored[0], 16 * (TCH // 2 + 1) + PRIME)
            sp.wait_ge(table_stored[1], 16 * (TCH // 2) + PRIME)
            for i in range(6):
                if i < 4:
                    at = slice(KT // 4 * i, KT // 4 * (i + 1))
                    sp.dma_start(x[:, at], x_s[:, at]).then_inc(x_restored, 16)
                else:
                    load_group(sp, i - 4, i - 4)
                for m in (0, 1):
                    hidden_sp(sp, TABLED, 2, i + 1, m)
            with sp.Fori(7, (P - TABLED) // 2) as i:
                for m in (0, 1):
                    hidden_sp(sp, TABLED, 2, i, m)
            sp.wait_ge(x_restored, 16 * 4)
            for s in (0, 1):
                sp.wait_ge(h_stored[s], 8 * P + PRIME)

        @block.tensor
        def _(pe):
            with pe.Fori(0, NCH) as t:
                for m in range(STRETCH):
                    hidden_pe(pe, 0, STRETCH, t, m, before=(lambda n: pe_scores(pe, t) if n == KT // 2 else None) if m == 0 else None)
                pe_turn(pe, t)
            with pe.Fori(0, TCH) as c:
                for m in range(CHUNK_UNITS):
                    hidden_pe(pe, ROUTED, CHUNK_UNITS, c, m, before=lambda n: pe_quad(pe, c, 2 * m + n // 8) if n % 8 == 4 else None)
            with pe.Fori(0, (P - TABLED) // 2) as i:
                for m in (0, 1):
                    hidden_pe(pe, TABLED, 2, i, m)

        @block.scalar
        def _(act):
            with act.Fori(0, NCH) as t:
                for m in range(STRETCH):
                    hidden_act(act, 0, STRETCH, t, m)
                    if m == STRETCH - 2:
                        act.wait_ge(less_max, t + 1)
                        nc.scalar.activation(ex[:], v2[:], ACT.Exp).then_inc(exped, 1)
            with act.Fori(0, (P - ROUTED) // 2) as i:
                for m in (0, 1):
                    hidden_act(act, ROUTED, 2, i, m)

        @block.gpsimd
        def _(pool):
            with pool.Fori(0, P // 2) as i:
                for m in (0, 1):
                    hidden_pool(pool, 0, 2, i, m)
            pool_gate(pool, 0, 0, 1)

        @block.vector
        def _(dve):
            with dve.Fori(0, NCH) as t:
                chain = Chain(dve, route_chain)
                chain.enter(t, ROUTE_LINKS)
                dve_route(dve, t, chain)
                assert chain.n == ROUTE_LINKS, chain.n
            dve.wait_ge(slots_taken, NCH + PRIME)
            dve.wait_ge(x_parked, 16)
            with dve.Fori(0, TCH // 2) as c:
                for s in (0, 1):
                    dve_chunk_of_table(dve, c * 2 + s, s, c)
            dve_chunk_of_table(dve, TCH - 1, 0, TCH // 2)

    VU = KT // 4
    squares_before = counts["squares"]
    counts["squares"] += KT
    place = region(HR, H_SIZE)
    chi = [place(f"chi{i}", [GRP, T], F32R) for i in (0, 1)]
    clo = [place(f"clo{i}", [GRP, T], F32R) for i in (0, 1)]
    def pool_coefs(pool, g, s, fills):
        pool.wait_ge(clo_ready, g * GRP)
        pool_gate(pool, g, s, fills)
        finished(pool, g * KT + (V0 - KT))
        for q in range(GRP):
            lower_coef(pool, nc.gpsimd, g, s, q)

    def lower_coef(eng, how, g, s, q):
        eng.wait_ge(chi_ready, g * GRP + (q + 1))
        how.tensor_tensor(clo[s][:, q], coef[:, q], chi[s][:, q].bitcast(F32), ALU.subtract).then_inc(clo_ready, 1)

    def act_coef(act, g, s, q):
        act.wait_ge(coef_ready, g * GRP + (q + 1))
        nc.scalar.copy(chi[s][:, q], coef[:, q]).then_inc(chi_ready, 1)

    def out_slot(d):
        return (pu, pm)[d // 2][:, (1 - d) % 2]

    def pair_sp(sp, i, last):
        for r in (0, 1):
            for w in range(VU):
                m = VU * r + w
                if not (last and m >= 2 * VU - 2):
                    load_unit(sp, i * (2 * VU) + (V0 + m + 2), (V0 + m) % 2)
                if w == 0 and not last:
                    sp.wait_ge(coef_ready, i * (2 * GRP) + GRP * (r + 1))
                    load_group(sp, i * 2 + (r + 2), r)

    def pair_pe(pe, i):
        for r in (0, 1):
            for w in range(VU):
                n = VU * r + w
                slot = (V0 + n) % 2
                pe.wait_ge(lo_ready, i * (2 * VU) + (V0 + n + 1))
                if w == 0:
                    pe.wait_ge(clo_ready, i * (2 * GRP) + GRP * (r + 1))
                for d in range(4):
                    if d % 2 == 0:
                        pe.wait_ge(psum_free, i * (2 * KT) + (V0 + 4 * n + d))
                    products([out_slot(d)[:, b, 0:HALF] for b in (0, 1)],
                             [(whi[:, slot, GRP * d + k], wlo[:, slot, GRP * d + k], halves(chi[r], clo[r], k)) for k in range(GRP)]).then_inc(tiles_done, 1)

    def pair_act(act, i, last):
        for r in (0, 1):
            for w in range(VU):
                n = VU * r + w
                if not (last and n == 2 * VU - 1):
                    split_hi(act, (V0 + n + 1) % 2, i * VU + ((V0 + n + 1) // 2 + 1), i * (2 * KT) + (V0 + 4 * n))
                if w < 2 and not (last and r):
                    for q in (2 * w, 2 * w + 1):
                        act_coef(act, i * 2 + (r + 1), 1 - r, q)
                if last and r:
                    if w == 0:
                        act.wait_ge(sum_cleared, counts["sums"] + 1)
                    for o in range(4 * w, 4 * w + 4):
                        taken(act, i * (2 * KT) + (V0 + KT + o))
                        act_square(act, x, o, o % 2, T, squares_before)

    def pair_dve(dve, i, last):
        for n in range(2 * VU):
            if not (last and n == 2 * VU - 1):
                split_lo(dve, i * (2 * VU) + (V0 + n + 1), (V0 + n + 1) % 2)
            for d in range(4):
                o = 4 * (n % VU) + d
                finished(dve, i * (2 * KT) + (V0 + 4 * n + d + 1))
                nc.vector.tensor_tensor(in_two(x[:, o]), out_slot(d)[:, :, 0:HALF], in_two(x[:, o]), ALU.add).then_inc(psum_free, 1)

    def pair_pool(pool, i, last):
        pool_coefs(pool, i * 2 + 1, 1, i + 1)
        if not last:
            pool_coefs(pool, i * 2 + 2, 0, i + 2)
        else:
            pool.wait_ge(clo_ready, NGRP * GRP)
            sum_tiles(pool, T, squares_before)

    with nc.Block() as block:
        def pairs(eng, pair):
            with eng.Fori(0, NGRP // 2 - 1) as i:
                pair(eng, i, False)
            pair(eng, NGRP // 2 - 1, True)

        @block.sync
        def _(sp):
            pairs(sp, pair_sp)

        @block.tensor
        def _(pe):
            with pe.Fori(0, NGRP // 2) as i:
                pair_pe(pe, i)

        @block.scalar
        def _(act):
            for q in range(GRP):
                act_coef(act, 0, 0, q)
            pairs(act, pair_act)

        @block.vector
        def _(dve):
            for q in range(GRP):
                lower_coef(dve, nc.vector, 0, 0, q)
            pairs(dve, pair_dve)

        @block.gpsimd
        def _(pool):
            pairs(pool, pair_pool)

    norm_final = Norm(x, V_FINAL, T, final=a["yT"])
    with nc.Block() as block:
        @block.tensor
        def _(pe):
            norm_final.pe(pe)

        @block.scalar
        def _(act):
            norm_final.act(act)

        @block.vector
        def _(dve):
            norm_final.dve(dve)

        @block.sync
        def _(sp):
            norm_final.sp(sp)

    es.close()


def deltanet(nc, es, sem, region, a, m):
    consts, vecs, SLOT, cat, ident, ones, cum = (m[k] for k in ("consts", "vecs", "SLOT", "cat", "ident", "ones", "cum"))
    beta, gcol, gcum, egcum, qkv_s, primed = (m[k] for k in ("beta", "gcol", "gcum", "egcum", "qkv_s", "primed"))
    HP = [HEADS, P]
    HH = HEADS // 2
    pw = region(m["WR"], m["W_SIZE"])
    ph = region(m["HR"], m["H_SIZE"])
    qc, kc, vc = (pw(n, HP) for n in ("qc", "kc", "vc"))
    qn, kn, qdec, grows, egam = (pw(n, HP) for n in ("qn", "kn", "qdec", "grows", "egam"))
    vnat, kdec, resid, S_sample = (pw(n, HP) for n in ("vnat", "kdec", "resid", "S_sample"))
    glast, kscale = pw("glast", [HEADS]), pw("kscale", [HEADS])
    dA, dB, A, att, attm = (ph(n, HP) for n in ("dA", "dB", "A", "att", "attm"))
    Tn, Tt, half, vnew, S_prompt, Sd, o, og = (ph(n, HP) for n in ("Tn", "Tt", "halfp", "vnew", "S_prompt", "Sd", "o", "og"))
    L = [ph(f"L{i}", HP) for i in (0, 1)]
    sq = ph("sq", HP)
    rr = ph("rr", HP)
    heads = [slice(0, HH), slice(HH, HEADS)]
    flat = lambda t, b: t[:, heads[b]].rearrange("p h n -> p (h n)")
    bank = lambda s, b: SLOT[s][:, 512 * b:512 * b + 512]
    psum = lambda s: SLOT[s].rearrange("p (h n) -> p h n", n=P)
    bc_in = lambda ap: ap.unsqueeze(2).broadcast_to([P, HH, P])
    bc_h = lambda ap: ap.unsqueeze(1).broadcast_to([P, HH, P])

    names = ("loaded gamma gam_taken diffs exps sq_q sq_k ssq ssk ln_q ln_k rk normed scores decayed turned "
             "att_done kdec_done vnat_done level_l level_p level_pc level_x level_t ks resid_done vn vn_copied qdec_done outs sqo sso "
             "ro s_loaded spread chain_d").split()
    q = {n: sem("dn_" + n) for n in names}
    s_stored = m["s_stored"]
    sso_read, s_updated, cat_done = primed["sso_read"], primed["s_updated"], primed["cat_done"]

    A_, B_, C_, D_ = range(4)

    def ready(eng, name, c, b):
        eng.wait_ge(q[name], c * 2 + (b + 1))

    def level(eng, name, c, l, b):
        eng.wait_ge(q[name], c * (2 * LEVELS) + (2 * l + b + 1))

    def part(ap, l, side):
        return ap.rearrange("p (m two s) -> p m two s", two=2, s=1 << l)[:, :, side]

    def joined(slot, h, l):
        if isinstance(h, slice):
            return SLOT[slot][:, P * h.start:P * h.start + HH * P // 2].rearrange("p (m s) -> p m s", s=1 << l)
        at = P * HH * (h // HH) + P // 2 * (h % HH)
        return SLOT[slot][:, at:at + P // 2].rearrange("p (m s) -> p m s", s=1 << l)

    def sp_load(sp, c):
        for n, t in enumerate((qc, kc, vc)):
            sp.dma_start(t[:], qkv_s[8 * n:8 * n + 8, :, bass.ds(c * P, P)].rearrange("h p n -> p h n")).then_inc(q["loaded"], 16)

    def heads_of(b):
        return range(HH * b, HH * b + HH)

    def pe_sum_squares(pe, c, t, squares_of, out):
        for b in (0, 1):
            ready(pe, squares_of, c, b)
            nc.tensor.matmul(bank(C_, b), ones, flat(t, b), start=True, stop=True).then_inc(q[out], 1)

    def pe_gamma(pe, c):
        pe.wait_ge(q["spread"], c + 1)
        for b in (0, 1):
            ready(pe, "ln_k", c, b)
            for h in heads_of(b):
                ins = nc.tensor.matmul(psum(C_)[:, h], grows[:, h], cum, start=True, stop=True)
            ins.then_inc(q["gamma"], 1)

    def pe_ahead(pe, c, l, first=False):
        if l == 3:
            if not first:
                ready(pe, "resid_done", c - 1, 1)
            pe_sum_squares(pe, c, sq, "sq_q", "ssq")
        elif l == 4:
            for b in (0, 1):
                ready(pe, "ln_q", c, b)
            pe_sum_squares(pe, c, rr, "sq_k", "ssk")
        elif l == 5:
            pe_gamma(pe, c)

    def pe_chunk(pe, c, levels, ahead, S):
        for b in (0, 1):
            ready(pe, "normed", c, b)
            for h in heads_of(b):
                nc.tensor.matmul(psum(D_)[:, h], kn[:, h], kn[:, h], start=True, stop=True)
            for h in heads_of(b):
                ins = nc.tensor.matmul(psum(A_)[:, h], kn[:, h], qn[:, h], start=True, stop=True)
            ins.then_inc(q["scores"], 1)
        pe.wait_ge(s_updated, c * 2 + PRIME)
        pe.wait_ge(sso_read, c + PRIME)
        for b in (0, 1):
            for h in heads_of(b):
                nc.tensor.transpose(psum(B_)[:, h], kn[:, h], ident)
            ready(pe, "exps", c, b)
            for h in heads_of(b):
                ins = nc.tensor.transpose(psum(C_)[:, h], vc[:, h], ident)
            ins.then_inc(q["turned"], 1)
        for b in (0, 1):
            ready(pe, "vnat_done", c, b)
            for h in heads_of(b):
                ins = nc.tensor.matmul(psum(C_)[:, h], kn[:, h], S[:, h], start=True, stop=True)
            ins.then_inc(q["ks"], 1)
        for b in (0, 1):
            level(pe, "level_l", c, 0, b)
            ready(pe, "att_done", c, b)
            for h in heads_of(b):
                ins = nc.tensor.transpose(psum(A_)[:, h], L[0][:, h], ident)
            ins.then_inc(q["level_x"], 1)
        for l in range(1, levels):
            for b in (0, 1):
                level(pe, "level_l", c, l, b)
                level(pe, "level_t", c, l - 1, b)
                for h in heads_of(b):
                    ins = nc.tensor.matmul(psum(D_)[:, h], L[l % 2][:, h], Tt[:, h], start=True, stop=True)
                ins.then_inc(q["level_p"], 1)
            if ahead:
                pe_ahead(pe, c + 1, l)
            for b in (0, 1):
                pe.wait_ge(q["level_pc"], c * (2 * LEVELS - 2) + (2 * l + b - 1))
                for h in heads_of(b):
                    ins = nc.tensor.matmul(joined(A_, h, l), Tn[:, h], part(half[:, h], l, 1), start=True, stop=True)
                if l == 1:
                    ready(pe, "kdec_done", c, b)
                if l < levels - 1:
                    for h in heads_of(b):
                        ins = nc.tensor.matmul(joined(B_, h, l), half[:, h], part(Tn[:, h], l, 0), start=True, stop=True)
                ins.then_inc(q["level_x"], 1)
        for b in (0, 1):
            ready(pe, "resid_done", c, b)
            level(pe, "level_t", c, levels - 1, b)
            for h in heads_of(b):
                ins = nc.tensor.matmul(psum(D_)[:, h], Tt[:, h], resid[:, h], start=True, stop=True)
            ins.then_inc(q["vn"], 1)
        for b in (0, 1):
            ready(pe, "vn_copied", c, b)
            ready(pe, "qdec_done", c, b)
            for h in heads_of(b):
                nc.tensor.matmul(psum(A_)[:, h], S[:, h], qdec[:, h], start=True, stop=False)
                nc.tensor.matmul(psum(A_)[:, h], vnew[:, h], attm[:, h], start=False, stop=True)
            for h in heads_of(b):
                ins = nc.tensor.matmul(psum(B_)[:, h], kdec[:, h], vnew[:, h], start=True, stop=True)
            ins.then_inc(q["outs"], 1)
        for b in (0, 1):
            ready(pe, "sqo", c, b)
            nc.tensor.matmul(bank(C_, b), ones, flat(sq, b), start=True, stop=True).then_inc(q["sso"], 1)

    eps = vecs[:, V_EPS:V_EPS + 1]

    def act_square(c, src, dst, name):
        for b in (0, 1):
            nc.scalar.activation(flat(dst, b), flat(src, b), ACT.Square).then_inc(q[name], 1)

    def act_ln(act, c, t, sums, name):
        for b in (0, 1):
            ready(act, sums, c, b)
            nc.scalar.activation(flat(t, b), bank(C_, b), ACT.Ln, bias=eps).then_inc(q[name], 1)

    def act_rsqrt(act, c, b):
        ready(act, "ln_q", c, b)
        ready(act, "ln_k", c, b)
        nc.scalar.activation(flat(sq, b), flat(sq, b), ACT.Exp, scale=-0.5)
        nc.scalar.activation(flat(rr, b), flat(rr, b), ACT.Exp, scale=-0.5).then_inc(q["rk"], 1)

    def act_decays(act, c, b):
        ready(act, "diffs", c, b)
        nc.scalar.activation(flat(egam, b), bank(C_, b), ACT.Exp)
        nc.scalar.activation(flat(dA, b), flat(dA, b), ACT.Exp, scale=-1.0)
        nc.scalar.activation(flat(dB, b), flat(dB, b), ACT.Exp)
        nc.scalar.activation(kscale[:, heads[b]], glast[:, heads[b]], ACT.Exp).then_inc(q["exps"], 1)

    def act_ahead(act, c, l, b):
        if (l, b) == (2, 0):
            act.wait_ge(q["loaded"], c * 48 + 48)
            act_square(c, qc, sq, "sq_q")
        elif (l, b) == (2, 1):
            act_square(c, kc, rr, "sq_k")
        elif (l, b) == (3, 1):
            act_ln(act, c, sq, "ssq", "ln_q")
        elif (l, b) == (4, 1):
            act_ln(act, c, rr, "ssk", "ln_k")
        elif l == 5:
            act_rsqrt(act, c, b)

    def act_chunk(act, c, levels, ahead):
        for b in (0, 1):
            ready(act, "turned", c, b)
            nc.scalar.copy(flat(vnat, b), bank(C_, b)).then_inc(q["vnat_done"], 1)
        for l in range(1, levels):
            for b in (0, 1):
                act.wait_ge(q["level_p"], c * (2 * LEVELS - 2) + (2 * l + b - 1))
                nc.scalar.copy(flat(half, b), bank(D_, b)).then_inc(q["level_pc"], 1)
                if (l, b) == (2, 0):
                    act.wait_ge(cat_done, c * 2 + PRIME)
                if ahead:
                    act_ahead(act, c + 1, l, b)
        for b in (0, 1):
            ready(act, "vn", c, b)
            nc.scalar.copy(flat(vnew, b), bank(D_, b)).then_inc(q["vn_copied"], 1)
        if ahead:
            for b in (0, 1):
                ready(act, "normed", c + 1, b)
                ready(act, "qdec_done", c, b)
                act_decays(act, c + 1, b)
        for b in (0, 1):
            ready(act, "outs", c, b)
            nc.scalar.copy(flat(o, b), bank(A_, b))
            nc.scalar.activation(flat(sq, b), bank(A_, b), ACT.Square).then_inc(q["sqo"], 1)
        for b in (0, 1):
            ready(act, "sso", c, b)
            ins = nc.scalar.activation(flat(rr, b), bank(C_, b), ACT.Ln, scale=1.0 / P, bias=eps)
        ins.then_inc(sso_read, 1)
        act.wait_ge(sso_read, c + (1 + PRIME))
        for b in (0, 1):
            nc.scalar.activation(flat(rr, b), flat(rr, b), ACT.Exp, scale=-0.5).then_inc(q["ro"], 1)

    tt = nc.vector.tensor_tensor
    cols = lambda t, c, b: t[:, bass.ds(c * HEADS + HH * b, HH)]

    def dve_diffs(dve, c, b):
        hs = heads[b]
        ready(dve, "gamma", c, b)
        tt(dA[:, hs], psum(C_)[:, hs], bc_in(cols(gcum, c, b)), ALU.subtract)
        tt(glast[:, hs], psum(C_)[:, hs, P - 1], cols(gcum, c, b), ALU.subtract)
        tt(dB[:, hs], psum(C_)[:, hs], bc_in(cols(gcum, c, b)), ALU.subtract).then_inc(q["gam_taken"], 1)
        ready(dve, "gam_taken", c, b)
        nc.vector.tensor_scalar(flat(dA, b), flat(dA, b), 0.0, None, ALU.max)
        nc.vector.tensor_scalar(flat(dB, b), flat(dB, b), 0.0, None, ALU.min).then_inc(q["diffs"], 1)

    def dve_normalise(dve, c):
        for b in (0, 1):
            ready(dve, "rk", c, b)
            nc.vector.scalar_tensor_tensor(flat(qn, b), flat(qc, b), float(P) ** -0.5, flat(sq, b), ALU.mult, ALU.mult)
            tt(flat(kn, b), flat(kc, b), flat(rr, b), ALU.mult).then_inc(q["normed"], 1)

    def dve_chunk(dve, c, chain, levels, width, ahead, S):
        for b in (0, 1):
            hs = heads[b]
            ready(dve, "scores", c, b)
            chain.link(tt(A[:, hs], psum(D_)[:, hs], bc_in(cols(beta, c, b)), ALU.mult))
            ready(dve, "exps", c, b)
            tt(flat(A, b), flat(A, b), flat(dA, b), ALU.mult).then_inc(q["decayed"], 1)
        for b in (0, 1):
            tt(flat(att, b), bank(A_, b), flat(dB, b), ALU.mult).then_inc(q["att_done"], 1)
        for b in (0, 1):
            hs = heads[b]
            ready(dve, "turned", c, b)
            tt(kdec[:, hs], psum(B_)[:, hs], bc_in(kscale[:, hs]), ALU.mult).then_inc(q["kdec_done"], 1)
        for l in range(levels):
            for b in (0, 1):
                hs = heads[b]
                level(dve, "level_x", c, l, b)
                if l == 0:
                    tt(Tn[:, hs], bc_h(ident), L[0][:, hs], ALU.subtract)
                    tt(Tt[:, hs], bc_h(ident), psum(A_)[:, hs], ALU.subtract).then_inc(q["level_t"], 1)
                    continue
                pairs = [(Tt, A_, 1), (Tn, B_, 0)] if l < levels - 1 else [(Tt, A_, 1)]
                for t, slot, side in pairs:
                    at = part(flat(t, b), l, side)
                    ins = tt(at, at, joined(slot, hs, l), ALU.subtract)
                ins.then_inc(q["level_t"], 1)
            if l == 0:
                for b in (0, 1):
                    ready(dve, "att_done", c, b)
                    tt(attm[:, heads[b]], att[:, heads[b]], bc_h(cum), ALU.mult)
            if l in (1, 2):
                b = l - 1
                hs = heads[b]
                ready(dve, "ks", c, b)
                chain.link(tt(resid[:, hs], psum(C_)[:, hs], bc_in(cols(egcum, c, b)), ALU.mult))
                chain.link(tt(flat(resid, b), flat(vnat, b), flat(resid, b), ALU.subtract))
                tt(resid[:, hs], resid[:, hs], bc_in(cols(beta, c, b)), ALU.mult).then_inc(q["resid_done"], 1)
                chain.link(tt(Sd[:, hs], S[:, hs], bc_in(egam[:, hs, P - 1]), ALU.mult))
            if ahead and l == 5:
                dve_diffs(dve, c + 1, 0)
        if ahead:
            for b in (0, 1):
                ready(dve, "qdec_done", c, b)
            dve_normalise(dve, c + 1)
            dve_diffs(dve, c + 1, 1)
        for b in (0, 1):
            ready(dve, "outs", c, b)
            tt(flat(S, b), flat(Sd, b), bank(B_, b), ALU.add).then_inc(s_updated, 1)
        for b in (0, 1):
            ready(dve, "ro", c, b)
            chain.link(nc.vector.scalar_tensor_tensor(flat(og, b), flat(o, b), vecs[:, V_DN:V_DN + 1], flat(rr, b), ALU.mult, ALU.mult))
            at = cat[:, HEADS + HH * b:HEADS + HH * b + HH, bass.ds(c * P, width)]
            tt(at, og[:, heads[b], 0:width], at, ALU.mult).then_inc(cat_done, 1)

    def pool_spread(pool, c):
        nc.gpsimd.tensor_tensor(grows[:], ones.unsqueeze(1).broadcast_to([P, HEADS, P]),
                                gcol[:, bass.ds(c * HEADS, HEADS)].unsqueeze(2).broadcast_to([P, HEADS, P]), ALU.mult).then_inc(q["spread"], 1)

    def pool_chunk(pool, c, levels, ahead):
        for l in range(levels):
            for b in (0, 1):
                hs = heads[b]
                if l == 0:
                    ready(pool, "decayed", c, b)
                elif l == 2:
                    level(pool, "level_x", c, 0, b)
                    level(pool, "level_t", c, 0, b)
                elif l > 2:
                    pool.wait_ge(q["level_p"], c * (2 * LEVELS - 2) + (2 * l + b - 5))
                nc.gpsimd.tensor_tensor(L[l % 2][:, hs], A[:, hs], bc_h(consts[:, C_LEV + l * P:C_LEV + (l + 1) * P]), ALU.mult).then_inc(q["level_l"], 1)
            if l == 1:
                for b in (0, 1):
                    nc.gpsimd.tensor_tensor(flat(qdec, b), flat(qn, b), flat(egam, b), ALU.mult).then_inc(q["qdec_done"], 1)
                if ahead:
                    ready(pool, "gamma", c, 1)
                    pool_spread(pool, c + 1)

    sample = NCH - 1
    sample_levels = TS.bit_length() - 1
    with nc.Block() as block:
        @block.sync
        def _(sp):
            sp_load(sp, 0)
            sp.dma_start(S_sample[:], a["state"].rearrange("h p n -> p h n")).then_inc(q["s_loaded"], 16)
            with sp.Fori(0, sample) as c:
                ready(sp, "turned", c, 1)
                sp_load(sp, c + 1)
            sp.wait_ge(s_updated, 2 * sample + PRIME)
            sp.dma_start(a["dn_prompt"].rearrange("h p n -> p h n"), S_prompt[:]).then_inc(s_stored, 16)
            sp.wait_ge(s_stored, 16)

        @block.tensor
        def _(pe):
            for l in (3, 4, 5):
                pe_ahead(pe, 0, l, first=True)
            with pe.Fori(0, sample) as c:
                pe_chunk(pe, c, LEVELS, True, S_prompt)
            pe.wait_ge(q["s_loaded"], 16)
            pe_chunk(pe, sample, sample_levels, False, S_sample)

        @block.scalar
        def _(act):
            for l in (2, 3, 4, 5):
                for b in (0, 1):
                    act_ahead(act, 0, l, b)
            for b in (0, 1):
                act_decays(act, 0, b)
            with act.Fori(0, sample) as c:
                act_chunk(act, c, LEVELS, True)
            act_chunk(act, sample, sample_levels, False)

        @block.vector
        def _(dve):
            def chunk(c, *rest):
                chain = Chain(dve, q["chain_d"])
                chain.enter(c, 10)
                dve_chunk(dve, c, chain, *rest)
                assert chain.n == 10, chain.n

            nc.vector.memset(S_prompt[:], 0.0)
            dve.wait_ge(q["loaded"], 48)
            dve_normalise(dve, 0)
            for b in (0, 1):
                dve_diffs(dve, 0, b)
            with dve.Fori(0, sample) as c:
                chunk(c, LEVELS, P, True, S_prompt)
            dve.wait_ge(q["s_loaded"], 16)
            chunk(sample, sample_levels, TS, False, S_sample)

        @block.gpsimd
        def _(pool):
            pool_spread(pool, 0)
            with pool.Fori(0, sample) as c:
                pool_chunk(pool, c, LEVELS, True)
            pool_chunk(pool, sample, sample_levels, False)
    return S_sample


def attention(nc, es, sem, region, a, m):
    pu, pm, q_s, xhi, xlo, ident = (m[k] for k in ("pu", "pm", "q_s", "xhi", "xlo", "ident"))
    place = region(m["WR"], m["W_SIZE"])
    qh = place("qh", [2, MHT, T])
    kh = place("kh", [2, MHT, M])
    vh = place("vh", [2, 2, MHT * P])
    pr = place("pr", [4, M])
    pn = place("pn", [4, M])
    pT = place("pT", [2, TP])
    mx, nmx, sm, rs = (place("at_" + n, [4]) for n in ("mx", "nmx", "sm", "rs"))
    names = "qk_loaded0 qk_loaded1 v_loaded0 v_loaded1 scores maxed exps normed turned copied pv out_hi out_lo".split()
    q = {n: sem("at_" + n) for n in names}
    chain_sem = sem("at_chain")
    qk_loaded = [q["qk_loaded0"], q["qk_loaded1"]]
    v_loaded = [q["v_loaded0"], q["v_loaded1"]]
    jobs = [(h, 0, P, TP // P, a["mkT"], a["mv"]) for h in range(MH)]
    jobs += [(h, TP, TS, 1, a["mkT_sample"], a["mv_sample"]) for h in range(MH)]

    def score_tiles(n, w, tiles):
        return [pm[0:w, n % 2, i // 2, (i % 2) * M:(i % 2 + 1) * M] for i in range(tiles)]

    with nc.Block() as block:
        @block.sync
        def _(sp):
            def load_qk(n):
                h, t0, w, tiles, kk, vv = jobs[n]
                s = n % 2
                if n >= 2:
                    sp.wait_ge(q["scores"], n - 1)
                sp.dma_start(qh[:, s], q_s[MHT * h:MHT * h + MHT, :, 0:T].rearrange("k p n -> p k n")).then_inc(qk_loaded[s], 16)
                sp.dma_start(kh[:, s], kk[MHT * h:MHT * h + MHT].rearrange("k p n -> p k n")).then_inc(qk_loaded[s], 16)

            load_qk(0)
            for n, (h, t0, w, tiles, kk, vv) in enumerate(jobs):
                if n + 1 < len(jobs):
                    load_qk(n + 1)
                if n >= 2:
                    sp.wait_ge(q["pv"], MHT * (n - 1))
                sp.dma_start(vh[:, n % 2], vv[:, :, h * MHT * P:(h + 1) * MHT * P]).then_inc(v_loaded[n % 2], 16)

        @block.tensor
        def _(pe):
            def scores(n):
                h, t0, w, tiles, kk, vv = jobs[n]
                s = n % 2
                pe.wait_ge(qk_loaded[s], 32 * (n // 2 + 1))
                if n >= 2:
                    pe.wait_ge(q["exps"], n - 1)
                for i, out in enumerate(score_tiles(n, w, tiles)):
                    for j in range(MHT):
                        ins = nc.tensor.matmul(out, qh[:, s, j, t0 + i * P:t0 + i * P + w], kh[:, s, j], start=(j == 0), stop=(j == MHT - 1))
                ins.then_inc(q["scores"], 1)

            scores(0)
            for n, (h, t0, w, tiles, kk, vv) in enumerate(jobs):
                s = n % 2
                if n + 1 < len(jobs):
                    scores(n + 1)
                pe.wait_ge(q["normed"], n + 1)
                for i in range(tiles):
                    for b in (0, 1):
                        ins = nc.tensor.transpose(pu[:, 0, b, i * P:i * P + w], pn[0:w, i, b * P:(b + 1) * P], ident[0:w, 0:w])
                ins.then_inc(q["turned"], 1)
                pe.wait_ge(q["copied"], n + 1)
                pe.wait_ge(v_loaded[s], 16 * (n // 2 + 1))
                for j in range(MHT):
                    o = n * MHT + j
                    if o >= 2:
                        pe.wait_ge(q["out_lo"], o - 1)
                    for b in (0, 1):
                        ins = nc.tensor.matmul(pu[:, 1, o % 2, 0:tiles * w], vh[:, s, b, j * P:(j + 1) * P], pT[:, b, 0:tiles * w],
                                               start=(b == 0), stop=(b == 1))
                    ins.then_inc(q["pv"], 1)

        @block.vector
        def _(dve):
            chain = Chain(dve, chain_sem)

            def maxima(n):
                h, t0, w, tiles, kk, vv = jobs[n]
                dve.wait_ge(q["scores"], n + 1)
                sc = pm[0:w, n % 2].rearrange("p b n -> p (b n)").rearrange("p (t m) -> p t m", m=M)[:, 0:tiles]
                chain.link(nc.vector.tensor_reduce(mx[0:w, 0:tiles], sc, AX_X, ALU.max))
                nc.vector.tensor_scalar(nmx[0:w, 0:tiles], mx[0:w, 0:tiles], -MEM_SCALE, None, ALU.mult).then_inc(q["maxed"], 1)

            def normalise(n):
                h, t0, w, tiles, kk, vv = jobs[n]
                dve.wait_ge(q["exps"], n + 1)
                chain.link(nc.vector.reciprocal(rs[0:w, 0:tiles], sm[0:w, 0:tiles]))
                nc.vector.tensor_tensor(pn[0:w, 0:tiles], pr[0:w, 0:tiles], rs[0:w, 0:tiles].unsqueeze(2).broadcast_to([w, tiles, M]), ALU.mult).then_inc(q["normed"], 1)

            maxima(0)
            normalise(0)
            for n, (h, t0, w, tiles, kk, vv) in enumerate(jobs):
                if n + 1 < len(jobs):
                    maxima(n + 1)
                for j in range(MHT):
                    if j == MHT // 2 and n + 1 < len(jobs):
                        normalise(n + 1)
                    o = n * MHT + j
                    dve.wait_ge(q["out_hi"], o + 1)
                    at = slice(t0, t0 + tiles * w)
                    nc.vector.tensor_tensor(xlo[:, MHT * h + j, at], pu[:, 1, o % 2, 0:tiles * w], xhi[:, MHT * h + j, at].bitcast(F32), ALU.subtract).then_inc(q["out_lo"], 1)

        @block.scalar
        def _(act):
            def exponentials(n):
                h, t0, w, tiles, kk, vv = jobs[n]
                act.wait_ge(q["maxed"], n + 1)
                for i, scores in enumerate(score_tiles(n, w, tiles)):
                    ins = nc.scalar.activation(pr[0:w, i], scores, ACT.Exp, scale=MEM_SCALE, bias=nmx[0:w, i:i + 1], accum_out=sm[0:w, i:i + 1])
                ins.then_inc(q["exps"], 1)

            exponentials(0)
            for n, (h, t0, w, tiles, kk, vv) in enumerate(jobs):
                act.wait_ge(q["turned"], n + 1)
                nc.scalar.copy(pT[:, :, 0:tiles * w], pu[:, 0, :, 0:tiles * w]).then_inc(q["copied"], 1)
                if n + 1 < len(jobs):
                    exponentials(n + 1)
                for j in range(MHT):
                    o = n * MHT + j
                    act.wait_ge(q["pv"], o + 1)
                    nc.scalar.copy(xhi[:, MHT * h + j, t0:t0 + tiles * w], pu[:, 1, o % 2, 0:tiles * w]).then_inc(q["out_hi"], 1)


def _tiles(a):
    n, m = a.shape
    return np.ascontiguousarray(a.reshape(n // P, P, m).transpose(1, 0, 2))


def _units(w):
    n = w.shape[1] // P
    return w.reshape(KT, P, n, P).transpose(2, 1, 0, 3).reshape(n, P, KT * P)


def kernel(**inputs):
    import concourse.bacc as bacc
    from concourse.bass_utils import run_bass_kernel_spmd

    g = {k: np.asarray(v) for k, v in inputs.items()}
    w_in = g["w_in"][0]
    units = np.zeros((UNITS, P, KT * P), np.float32)
    units[MK0:MV0] = _units(g["w_mk"][0])
    units[MV0:Z0] = g["w_mv"][0].reshape(4, 4, P, 4, 512).transpose(3, 0, 2, 1, 4).reshape(KT, P, KT * P)
    units[Z0:AB0] = _units(w_in[:, 4112:])
    units[POOL0:OUT0] = _units(w_in[:, :4096])
    ab = np.zeros((D, P), np.float32)
    ab[:, :16] = w_in[:, 4096:4112]
    units[AB0:POOL0] = _units(ab)
    units[OUT0:MQ0] = _units(g["w_out"][0])
    units[MQ0:MO0] = _units(g["w_mq"][0])
    units[MO0:PQ0] = _units(g["w_mo"][0])
    units[PQ0:EXP0] = _units(g["w_pq"][0])
    units[EXP0:V0] = g["u_experts"][0].reshape(P, P, KT, P).transpose(0, 3, 2, 1).reshape(P, P, KT * P)
    units[V0:] = g["v_experts"][0].reshape(NGRP, GRP, P, 4, 4, P).transpose(0, 3, 2, 4, 1, 5).reshape(P, P, KT * P)
    vecs = np.zeros((P, NV), np.float32)
    for at, name in ((V_MIX, "norm_mix"), (V_XATTN, "norm_xattn"), (V_MEM, "norm_mem"), (V_FFN, "norm_ffn"), (V_FINAL, "norm_final")):
        vecs[:, at:at + KT] = g[name].reshape(KT, P).T
    vecs[:, V_POOL:V_POOL + 8] = g["pool_scale"].reshape(8, P).T
    vecs[:, V_CONV:V_CONV + 96] = g["conv_w"][0].reshape(4, 24, P).transpose(2, 1, 0).reshape(P, 96)
    vecs[:, V_DN] = g["norm_dn"][0]
    vecs[:, V_EPS] = EPS
    vecs[:, V_ALOG:V_ALOG + 8] = g["a_log"][0]
    vecs[:, V_DT:V_DT + 8] = g["dt_bias"][0]
    ins = {
        "units": units,
        "consts": constants(),
        "vecs": vecs,
        "xT": _tiles(np.concatenate([g["x_prompt"][0], g["x_sample"][0]], 0).T),
        "memT": _tiles(g["mem_prompt"][0].T),
        "phist": _tiles(g["cache_pool"][0, 0].T),
        "chist": _tiles(g["cache_conv"][0, 0].T),
        "wpool": np.ascontiguousarray(g["w_pool"][0].reshape(4, 2, P, 2, P).transpose(2, 0, 1, 3, 4).reshape(P, KT, P)),
        "state": np.ascontiguousarray(g["state_dn"][0, 0]),
        "mkT_sample": np.ascontiguousarray(g["cache_mem_k"][0, 0].reshape(M, D).T.reshape(KT, P, M)),
        "mv_sample": _tiles(g["cache_mem_v"][0, 0].reshape(M, D)),
        "keys": np.ascontiguousarray(g["sub_keys"][0].transpose(3, 0, 1, 2).reshape(P, KT, P)),
    }
    outs = {
        "yT": (KT, P, T), "pool_new": (P, 8, 2, 15), "conv_new": (P, 24, 2, 3), "dn_prompt": (8, P, P),
        "dn_sample": (8, P, P), "mkT": (KT, P, M), "mv": (P, 2, D),
    }
    nc = bacc.Bacc("TRN2", target_bir_lowering=False, num_devices=1)
    a = {k: nc.dram_tensor(k, v.shape, F32, kind="ExternalInput").ap() for k, v in ins.items()}
    a.update({k: nc.dram_tensor(k, s, F32, kind="ExternalOutput").ap() for k, s in outs.items()})
    build(nc, a)
    r = run_bass_kernel_spmd(nc, [ins], core_ids=[0]).results[0]
    y = r["yT"].reshape(D, T).T
    hist = lambda v, n: np.ascontiguousarray(v.transpose(2, 3, 1, 0)).reshape(2, 1, 1, n, -1)
    pool, conv = hist(r["pool_new"], 15), hist(r["conv_new"], 3)
    mk = np.ascontiguousarray(r["mkT"].reshape(D, M).T).reshape(1, 1, M, 4, 512)
    mv = np.ascontiguousarray(r["mv"].transpose(1, 0, 2)).reshape(1, 1, M, 4, 512)
    return (np.ascontiguousarray(y[:TP])[None], np.ascontiguousarray(y[TP:])[None],
            pool[0], conv[0], r["dn_prompt"][None, None], mk, mv,
            pool[1], conv[1], r["dn_sample"][None, None])
```
